# Optimizing a Trainium2 kernel written in Bass

```python
import math
import jax
import jax.numpy as jnp
from jax import lax
import numpy as np

D_MODEL = 1024
BATCH = 1
SEQ = 1024
DEPTH = 2

N_MIXERS = 4
N_MEM = 256
EPS = 1e-6
ROPE_THETA = 10000.0
POS_OFFSET_MAX = 4096
CHUNK = 64
D_MIX = 768
XA_HEADS = 4
XA_HEAD_DIM = 64
D_XA = XA_HEADS * XA_HEAD_DIM
GLA_HEADS = 4
GLA_DK = D_MIX // 2 // GLA_HEADS
GLA_DV = D_MIX // GLA_HEADS
GLA_RANK = 16
GLA_GATE_NORM = 16.0
DIL_GROUPS = ((128, 1), (512, 4), (2048, 16))
DIL_HEADS = 4
DIL_HEAD_DIM = 128
DIL_BLOCK = 128
D_DIL = DIL_HEADS * DIL_HEAD_DIM
SSM_HEAD_DIM = 64
SSM_HEADS = D_MIX // SSM_HEAD_DIM
SSM_GROUPS = 2
SSM_STATE = 128
SSM_CONV = 4
HGRN_EXPAND = 128
HGRN_HEADS = D_MIX // HGRN_EXPAND
HGRN_DK = HGRN_EXPAND
HGRN_DV = D_MIX // HGRN_HEADS
D_FF = 2816
FFN_CONV = 3

kernel_name = "hybrid_interleaved_gla_dilated_ssd_hgrn2_block"

F32 = jnp.float32

def rms_norm(x, g):
    xf = x.astype(F32)
    y = xf * lax.rsqrt(jnp.mean(xf * xf, axis=-1, keepdims=True) + EPS)
    return (y * g.astype(F32)).astype(x.dtype)

def split_cols(y, sizes):
    return jnp.split(y, [int(c) for c in np.cumsum(sizes)[:-1]], axis=-1)

def causal_dwconv(x, w, b):
    K, S = w.shape[0], x.shape[1]
    xp = jnp.pad(x, ((0, 0), (K - 1, 0), (0, 0)))
    y = b
    for j in range(K):
        y = y + xp[:, j:j + S] * w[j]
    return y

def rope_tables(positions, dim):
    half = dim // 2
    inv_freq = ROPE_THETA ** (-jnp.arange(half, dtype=F32) / half)
    ang = positions.astype(F32)[..., None] * inv_freq
    return jnp.cos(ang)[:, :, None], jnp.sin(ang)[:, :, None]

def apply_rope(x, cos, sin):
    half = x.shape[-1] // 2
    x1, x2 = x[..., :half].astype(F32), x[..., half:].astype(F32)
    return jnp.concatenate([x1 * cos - x2 * sin, x2 * cos + x1 * sin], axis=-1).astype(x.dtype)

def chunked_gla(q, k, v, log_a):
    Bsz, S, H, K = q.shape
    V = v.shape[-1]
    C = CHUNK
    n = S // C
    q, k, v, log_a = (t.astype(F32).reshape(Bsz, n, C, H, -1) for t in (q, k, v, log_a))
    b = jnp.cumsum(log_a, axis=2)
    b_last = b[:, :, -1:]
    b_ref = b[:, :, C // 2 - 1:C // 2]
    att = jnp.einsum('bnihk,bnjhk->bnhij', q * jnp.exp(b - b_ref), k * jnp.exp(b_ref - b))
    att = jnp.where(jnp.tril(jnp.ones((C, C), bool)), att, 0.0)
    o_intra = jnp.einsum('bnhij,bnjhv->bnihv', att, v)
    q_inter = q * jnp.exp(b)
    k_state = k * jnp.exp(b_last - b)
    decay = jnp.exp(b_last[:, :, 0])

    def step(state, xs):
        qc, kc, vc, dc = xs
        o = jnp.einsum('bchk,bhkv->bchv', qc, state)
        state = dc[..., None] * state + jnp.einsum('bchk,bchv->bhkv', kc, vc)
        return state, o

    tm = lambda t: jnp.moveaxis(t, 1, 0)
    _, o_inter = lax.scan(step, jnp.zeros((Bsz, H, K, V), F32),
                          (tm(q_inter), tm(k_state), tm(v), tm(decay)))
    return (o_intra + jnp.moveaxis(o_inter, 0, 1)).reshape(Bsz, S, H, V)

def ssd_chunked(x, dt, A, Bm, Cm):
    Bsz, S, G, Hg, P = x.shape
    N = Bm.shape[-1]
    C = CHUNK
    n = S // C
    a = (dt * A).reshape(Bsz, n, C, G, Hg)
    xdt = (x * dt[..., None]).reshape(Bsz, n, C, G, Hg, P)
    Bc = Bm.astype(F32).reshape(Bsz, n, C, G, N)
    Cc = Cm.astype(F32).reshape(Bsz, n, C, G, N)
    acs = jnp.cumsum(a, axis=2)
    seg = acs[:, :, :, None] - acs[:, :, None]
    causal = jnp.tril(jnp.ones((C, C), bool))[:, :, None, None]
    Lmat = jnp.exp(jnp.where(causal, seg, -jnp.inf))
    cb = jnp.einsum('bnlgk,bnsgk->bnlsg', Cc, Bc)
    y_diag = jnp.einsum('bnlsgh,bnsghp->bnlghp', cb[..., None] * Lmat, xdt)
    x_end = xdt * jnp.exp(acs[:, :, -1:] - acs)[..., None]
    in_decay = jnp.exp(acs)
    chunk_decay = jnp.exp(acs[:, :, -1])

    def step(hst, xs):
        c_c, b_c, xe_c, ind_c, cd_c = xs
        y_off = jnp.einsum('blgk,bghpk->blghp', c_c, hst) * ind_c[..., None]
        hst = cd_c[..., None, None] * hst + jnp.einsum('bsgk,bsghp->bghpk', b_c, xe_c)
        return hst, y_off

    tm = lambda t: jnp.moveaxis(t, 1, 0)
    _, y_off = lax.scan(step, jnp.zeros((Bsz, G, Hg, P, N), F32),
                        (tm(Cc), tm(Bc), tm(x_end), tm(in_decay), tm(chunk_decay)))
    return (y_diag + jnp.moveaxis(y_off, 0, 1)).reshape(Bsz, S, G, Hg, P)

def dilated_window_attention(q, k, v, window, dilation):
    Bsz, S, H, hd = q.shape
    r = dilation
    W = window // dilation
    Q = DIL_BLOCK
    L = S // r
    nb = -(-L // Q)
    Lp = nb * Q

    def to_blocks(t):
        t = t.reshape(Bsz, L, r, H, hd).transpose(0, 2, 1, 3, 4)
        t = jnp.pad(t, ((0, 0), (0, 0), (0, Lp - L), (0, 0), (0, 0)))
        return t.reshape(Bsz, r, nb, Q, H, hd)

    def with_prev(t):
        prev = jnp.pad(t, ((0, 0), (0, 0), (1, 0), (0, 0), (0, 0), (0, 0)))[:, :, :-1]
        return jnp.concatenate([prev, t], axis=3)

    qb = to_blocks(q)
    kk = with_prev(to_blocks(k))
    vv = with_prev(to_blocks(v))
    i = jnp.arange(Q)[:, None]
    j = jnp.arange(2 * Q)[None, :]
    dist = Q + i - j
    band = (dist >= 0) & (dist <= W)
    valid = (jnp.arange(nb)[:, None, None] > 0) | (j >= Q)[None]
    mask = band[None] & valid
    s = jnp.einsum('brnqhd,brnkhd->brnhqk', qb, kk).astype(F32) * (hd ** -0.5)
    s = jnp.where(mask[None, None, :, None], s, -jnp.inf)
    m = jnp.max(s, axis=-1, keepdims=True)
    p = jnp.exp(s - m)
    l = jnp.sum(p, axis=-1, keepdims=True)
    o = jnp.einsum('brnhqk,brnkhd->brnqhd', p / l, vv.astype(F32))
    lse = (m + jnp.log(l))[..., 0].transpose(0, 1, 2, 4, 3)
    o = o.reshape(Bsz, r, Lp, H, hd)[:, :, :L].transpose(0, 2, 1, 3, 4).reshape(Bsz, S, H, hd)
    lse = lse.reshape(Bsz, r, Lp, H)[:, :, :L].transpose(0, 2, 1, 3).reshape(Bsz, S, H)
    return o, lse

def gla_mixer(h, w_in, w_gate2, b_gate, o_norm):
    Bsz, S, _ = h.shape
    q, k, v, glr, og, xq = split_cols(
        h @ w_in, [GLA_HEADS * GLA_DK, GLA_HEADS * GLA_DK, D_MIX, GLA_RANK, D_MIX, D_XA])
    log_a = jax.nn.log_sigmoid((glr @ w_gate2 + b_gate).astype(F32)) / GLA_GATE_NORM
    hs = lambda t: t.reshape(Bsz, S, GLA_HEADS, -1)
    o = chunked_gla(hs(q) * (GLA_DK ** -0.5), hs(k), hs(v), hs(log_a))
    o = rms_norm(o, o_norm).reshape(Bsz, S, D_MIX) * jax.nn.silu(og.astype(F32))
    return o.astype(h.dtype), xq

def dilated_mixer(h, w_in, q_norm, k_norm, positions):
    Bsz, S, _ = h.shape
    nh = len(DIL_GROUPS) * DIL_HEADS
    q, k, v, xq = split_cols(h @ w_in, [nh * DIL_HEAD_DIM] * 3 + [D_XA])
    hs = lambda t: t.reshape(Bsz, S, nh, DIL_HEAD_DIM)
    cos, sin = rope_tables(positions, DIL_HEAD_DIM)
    q = apply_rope(rms_norm(hs(q), q_norm), cos, sin)
    k = apply_rope(rms_norm(hs(k), k_norm), cos, sin)
    v = hs(v)
    outs, lses = [], []
    for g, (window, dilation) in enumerate(DIL_GROUPS):
        sl = slice(g * DIL_HEADS, (g + 1) * DIL_HEADS)
        o, lse = dilated_window_attention(q[:, :, sl], k[:, :, sl], v[:, :, sl], window, dilation)
        outs.append(o)
        lses.append(lse)
    wts = jax.nn.softmax(jnp.stack(lses), axis=0)
    o = jnp.sum(wts[..., None] * jnp.stack(outs), axis=0)
    return o.reshape(Bsz, S, D_DIL).astype(h.dtype), xq

def mamba2_mixer(h, w_in, conv_w, conv_b, dt_bias, a_log, d_skip, norm_g):
    Bsz, S, _ = h.shape
    GN = SSM_GROUPS * SSM_STATE
    hg = SSM_HEADS // SSM_GROUPS
    z, xbc, dt, xq = split_cols(h @ w_in, [D_MIX, D_MIX + 2 * GN, SSM_HEADS, D_XA])
    xbc = jax.nn.silu(causal_dwconv(xbc, conv_w, conv_b))
    xs, bm, cm = split_cols(xbc, [D_MIX, GN, GN])
    dt = jax.nn.softplus(dt.astype(F32) + dt_bias.astype(F32)).reshape(Bsz, S, SSM_GROUPS, hg)
    A = -jnp.exp(a_log.astype(F32)).reshape(SSM_GROUPS, hg)
    xs = xs.astype(F32).reshape(Bsz, S, SSM_GROUPS, hg, SSM_HEAD_DIM)
    y = ssd_chunked(xs, dt, A, bm.reshape(Bsz, S, SSM_GROUPS, SSM_STATE),
                    cm.reshape(Bsz, S, SSM_GROUPS, SSM_STATE))
    y = y + d_skip.astype(F32).reshape(SSM_GROUPS, hg)[..., None] * xs
    y = y.reshape(Bsz, S, D_MIX) * jax.nn.silu(z.astype(F32))
    y = rms_norm(y.reshape(Bsz, S, SSM_GROUPS, -1), norm_g.reshape(SSM_GROUPS, -1))
    return y.reshape(Bsz, S, D_MIX).astype(h.dtype), xq

def hgrn2_mixer(h, w_in, lower_bounds, o_norm, layer):
    Bsz, S, _ = h.shape
    q, f, i, og, xq = split_cols(
        h @ w_in, [HGRN_HEADS * HGRN_DK, HGRN_HEADS * HGRN_DK, D_MIX, D_MIX, D_XA])
    lbs = jnp.cumsum(jax.nn.softmax(lower_bounds.astype(F32), axis=0), axis=0)
    lb = lbs[layer] - lbs[0]
    fg = lb + (1.0 - lb) * jax.nn.sigmoid(f.astype(F32))
    hk = lambda t: t.reshape(Bsz, S, HGRN_HEADS, HGRN_DK)
    o = chunked_gla(hk(jax.nn.silu(q.astype(F32))), hk(1.0 - fg),
                    i.reshape(Bsz, S, HGRN_HEADS, HGRN_DV), hk(jnp.log(fg)))
    o = rms_norm(o, o_norm).reshape(Bsz, S, D_MIX) * jax.nn.sigmoid(og.astype(F32))
    return o.astype(h.dtype), xq

def memory_cross_attention(xq, mem_n, w_kv, q_norm, k_norm):
    Bsz, S, _ = xq.shape
    M = mem_n.shape[1]
    k, v = jnp.split(mem_n @ w_kv, 2, axis=-1)
    q = rms_norm(xq.reshape(Bsz, S, XA_HEADS, XA_HEAD_DIM), q_norm).astype(F32)
    k = rms_norm(k.reshape(Bsz, M, XA_HEADS, XA_HEAD_DIM), k_norm).astype(F32)
    v = v.reshape(Bsz, M, XA_HEADS, XA_HEAD_DIM).astype(F32)
    p = jax.nn.softmax(jnp.einsum('bshd,bmhd->bhsm', q, k) * (XA_HEAD_DIM ** -0.5), axis=-1)
    o = jnp.einsum('bhsm,bmhd->bshd', p, v)
    return o.reshape(Bsz, S, D_XA).astype(xq.dtype)

def conv_ffn(h, w_up, conv_w, conv_b, w_down):
    u = causal_dwconv(h @ w_up, conv_w, conv_b)
    gate, val = jnp.split(u, 2, axis=-1)
    return (jax.nn.silu(gate) * val) @ w_down

def setup_inputs(seed: int = 0) -> dict:
    key = jax.random.key(seed)
    ks = iter(jax.random.split(key, 40))

    def nrm(shape, scale=1.0):
        return jax.random.normal(next(ks), shape, F32) * scale

    def gain(shape):
        return 1.0 + nrm(shape, 0.02)

    D, F = D_MODEL, D_FF
    GN = SSM_GROUPS * SSM_STATE
    a_cols = 2 * GLA_HEADS * GLA_DK + 2 * D_MIX + GLA_RANK + D_XA
    b_cols = 3 * len(DIL_GROUPS) * D_DIL + D_XA
    c_cols = 2 * D_MIX + 2 * GN + SSM_HEADS + D_XA
    d_cols = 2 * HGRN_HEADS * HGRN_DK + 2 * D_MIX + D_XA
    a_out_in, b_out_in = D_MIX + D_XA, D_DIL + D_XA
    c_out_in, d_out_in = D_MIX + D_XA, D_MIX + D_XA
    inp = {}
    inp['x'] = nrm((BATCH, SEQ, D))
    inp['mem'] = nrm((BATCH, N_MEM, D))
    inp['positions'] = (jnp.arange(SEQ, dtype=jnp.int32)[None, :]
                        + jax.random.randint(next(ks), (BATCH, 1), 0, POS_OFFSET_MAX, dtype=jnp.int32))
    inp['mem_norm'] = gain((D,))
    inp['mix_norm'] = gain((DEPTH, D))
    inp['xa_w_kv'] = nrm((DEPTH, D, 2 * D_XA), D ** -0.5)
    inp['xa_q_norm'] = gain((DEPTH, XA_HEAD_DIM))
    inp['xa_k_norm'] = gain((DEPTH, XA_HEAD_DIM))
    inp['ffn_norm'] = gain((DEPTH, D))
    inp['ffn_w_up'] = nrm((DEPTH, D, 2 * F), D ** -0.5)
    inp['ffn_conv_w'] = nrm((DEPTH, FFN_CONV, 2 * F), FFN_CONV ** -0.5)
    inp['ffn_conv_b'] = nrm((DEPTH, 2 * F), 0.02)
    inp['ffn_w_down'] = nrm((DEPTH, F, D), 0.5 * F ** -0.5)
    inp['a_w_in'] = nrm((D, a_cols), D ** -0.5)
    inp['a_w_gate2'] = nrm((GLA_RANK, GLA_HEADS * GLA_DK), GLA_RANK ** -0.5)
    inp['a_b_gate'] = nrm((GLA_HEADS * GLA_DK,), 0.1)
    inp['a_o_norm'] = gain((GLA_DV,))
    inp['a_w_out'] = nrm((a_out_in, D), 0.5 * a_out_in ** -0.5)
    inp['b_w_in'] = nrm((D, b_cols), D ** -0.5)
    inp['b_q_norm'] = gain((DIL_HEAD_DIM,))
    inp['b_k_norm'] = gain((DIL_HEAD_DIM,))
    inp['b_w_out'] = nrm((b_out_in, D), 0.5 * b_out_in ** -0.5)
    inp['c_w_in'] = nrm((D, c_cols), D ** -0.5)
    inp['c_conv_w'] = nrm((SSM_CONV, D_MIX + 2 * GN), 0.5)
    inp['c_conv_b'] = nrm((D_MIX + 2 * GN,), 0.02)
    dt0 = jnp.exp(jax.random.uniform(next(ks), (SSM_HEADS,), F32, math.log(1e-3), math.log(1e-1)))
    inp['c_dt_bias'] = dt0 + jnp.log(-jnp.expm1(-dt0))
    inp['c_a_log'] = jnp.log(jax.random.uniform(next(ks), (SSM_HEADS,), F32, 1.0, 16.0))
    inp['c_d'] = gain((SSM_HEADS,))
    inp['c_norm'] = gain((D_MIX,))
    inp['c_w_out'] = nrm((c_out_in, D), 0.5 * c_out_in ** -0.5)
    inp['d_w_in'] = nrm((D, d_cols), D ** -0.5)
    inp['d_lower_bounds'] = nrm((DEPTH, HGRN_HEADS * HGRN_DK), 0.02)
    inp['d_o_norm'] = gain((HGRN_DV,))
    inp['d_w_out'] = nrm((d_out_in, D), 0.5 * d_out_in ** -0.5)
    return inp

def reference(x, mem, positions, mem_norm, mix_norm, xa_w_kv, xa_q_norm, xa_k_norm,
              ffn_norm, ffn_w_up, ffn_conv_w, ffn_conv_b, ffn_w_down,
              a_w_in, a_w_gate2, a_b_gate, a_o_norm, a_w_out,
              b_w_in, b_q_norm, b_k_norm, b_w_out,
              c_w_in, c_conv_w, c_conv_b, c_dt_bias, c_a_log, c_d, c_norm, c_w_out,
              d_w_in, d_lower_bounds, d_o_norm, d_w_out):
    mem_n = rms_norm(mem, mem_norm)
    for i in range(DEPTH):
        h = rms_norm(x, mix_norm[i])
        kind = i % N_MIXERS
        if kind == 0:
            tok, xq = gla_mixer(h, a_w_in, a_w_gate2, a_b_gate, a_o_norm)
            w_out = a_w_out
        elif kind == 1:
            tok, xq = dilated_mixer(h, b_w_in, b_q_norm, b_k_norm, positions)
            w_out = b_w_out
        elif kind == 2:
            tok, xq = mamba2_mixer(h, c_w_in, c_conv_w, c_conv_b, c_dt_bias, c_a_log, c_d, c_norm)
            w_out = c_w_out
        else:
            tok, xq = hgrn2_mixer(h, d_w_in, d_lower_bounds, d_o_norm, i)
            w_out = d_w_out
        xa = memory_cross_attention(xq, mem_n, xa_w_kv[i], xa_q_norm[i], xa_k_norm[i])
        x = x + jnp.concatenate([tok, xa], axis=-1) @ w_out
        x = x + conv_ffn(rms_norm(x, ffn_norm[i]), ffn_w_up[i], ffn_conv_w[i], ffn_conv_b[i],
                         ffn_w_down[i])
    return x


_drawn_inputs = setup_inputs


def setup_inputs(seed=0):
    import zlib

    import numpy as np

    out = dict(_drawn_inputs(seed))
    spreads = {}
    factors = {'mem_norm': 8.0,
     'mix_norm': 4.983,
     'xa_q_norm': 8.0,
     'xa_k_norm': 8.0,
     'ffn_norm': 4.926,
     'ffn_conv_b': 4.974,
     'a_b_gate': 4.414,
     'a_o_norm': 8.0,
     'b_q_norm': 22.996,
     'b_k_norm': 22.776}
    for name, (base, spread) in spreads.items():
        noise = np.random.default_rng([zlib.crc32(name.encode()), seed]).standard_normal(out[name].shape)
        drawn = base * np.exp(spread * noise) if base else spread * noise
        out[name] = jnp.asarray(drawn.astype(out[name].dtype))
    for name, factor in factors.items():
        out[name] = (out[name] * factor).astype(out[name].dtype)
    return out
```

```python
import concourse.bass as bass
from concourse import mybir
from concourse.alu_op_type import AluOpType as ALU
import math
from contextlib import ExitStack

F32 = mybir.dt.float32
F32R = mybir.dt.float32r
ACT = mybir.ActivationFunctionType
AX = mybir.AxisListType

P = 128
D = 1024
SEQ = 1024
DC = D // P
TT = SEQ // P
HALF = 512
FF = 2816
FC = FF // P
GROUPS = FC // 2
BANKS = 8


def phase_semaphore(nc, ctx, name):
    s = ctx.enter_context(nc.semaphore(name))
    ctx.callback(nc.gpsimd.sem_clear, s)
    return s


def split_matmul(nc, out, lhs_hi, lhs_lo, rhs_hi, rhs_lo, start, stop):
    nc.tensor.matmul(out, lhs_hi, rhs_hi, start=start, stop=False)
    nc.tensor.matmul(out, lhs_hi, rhs_lo, start=False, stop=False)
    return nc.tensor.matmul(out, lhs_lo, rhs_hi, start=False, stop=stop)


def ffn_phase(nc, ph, psum, ident, X, hT_hi, hT_lo, w_up, conv_w, conv_b, w_down, x_out):
    with ExitStack() as ctx:
        ctx.callback(nc.all_engine_barrier)
        def sb(name, shape, dt=F32):
            return ctx.enter_context(nc.sbuf_tensor(f"{ph}_{name}", shape, dt))

        def sem(name):
            return phase_semaphore(nc, ctx, f"{ph}_{name}")

        up_raw = [sb(f"up_raw{j}", [P, DC, P]) for j in range(2)]
        up_hi = [sb(f"up_hi{j}", [P, DC, P], F32R) for j in range(2)]
        up_lo = [sb(f"up_lo{j}", [P, DC, P], F32R) for j in range(2)]
        down_raw = sb("down_raw", [P, 2, D])
        down_hi = sb("down_hi", [P, 2, D], F32R)
        down_lo = sb("down_lo", [P, 2, D], F32R)
        act_hi = [sb(f"act_hi{j}", [P, 2, SEQ], F32R) for j in range(2)]
        act_lo = [sb(f"act_lo{j}", [P, 2, SEQ], F32R) for j in range(2)]
        conv_out = [sb("conv_gate", [P, SEQ]), sb("conv_value", [P, SEQ])]
        taps_rows = sb("taps_rows", [2 * FC, 4, P])
        taps = sb("taps", [P, 4, 2 * FC])

        up_loaded = [sem("up_loaded_gate"), sem("up_loaded_value")]
        down_loaded = sem("down_loaded")
        taps_loaded = sem("taps_loaded")
        taps_turned = sem("taps_turned")
        taps_ready = sem("taps_ready")
        up_high = sem("up_high")
        up_split = sem("up_split")
        down_high = sem("down_high")
        down_split = sem("down_split")
        up_done = sem("up_done")
        conv_started = sem("conv_started")
        conv_tap = sem("conv_tap")
        conv_done = sem("conv_done")
        gate_done = sem("gate_done")
        prod_done = sem("prod_done")
        act_high = sem("act_high")
        act_split = sem("act_split")
        down_done = sem("down_done")
        x_added = sem("x_added")
        stored = sem("stored")

        up_view = w_up.rearrange("(d p) c -> p d c", p=P)
        down_view = w_down.rearrange("(f p) n -> p f n", p=P)
        ups = [psum[:, 2 * j:2 * j + 2, :].rearrange("p b n -> p (b n)") for j in range(2)]

        def over_groups(eng, group):
            group(0, 0)
            group(1, 1)
            with eng.Fori(0, (GROUPS - 3) // 2) as it:
                group(it * 2 + 2, 0)
                group(it * 2 + 3, 1)
            group(GROUPS - 1, 0, last=True)

        def is_first(g):
            return isinstance(g, int) and g == 0

        block = ctx.enter_context(nc.Block())

        @block.sync
        def _(sp):
            def group(g, par, last=False):
                for c in range(2):
                    for j in range(2):
                        n = g * 4 + 2 * c + j
                        if not is_first(g) or c:
                            sp.wait_ge(up_split, n - 1)
                        sp.dma_start(up_raw[j][:, :, :],
                                     up_view[:, :, bass.ds(g * 2 * P + (j * FC + c) * P, P)]).then_inc(up_loaded[j], 16)
                if not is_first(g):
                    sp.wait_ge(down_split, g)
                sp.dma_start(down_raw[:, :, :], down_view[:, bass.ds(g * 2, 2), :]).then_inc(down_loaded, 16)

            over_groups(sp, group)
            for t in range(TT):
                sp.wait_ge(x_added, 2 * TT * (GROUPS - 1) + 2 * t + 2)
                sp.dma_start(x_out[t * P:(t + 1) * P, :], X[:, t, :]).then_inc(stored, 16)
            sp.wait_ge(stored, 16 * TT)

        @block.scalar
        def _(act):
            def high_up(n_slot, n):
                act.wait_ge(up_loaded[n_slot], n * 8 + (16 - 8 * n_slot))
                nc.scalar.activation(up_hi[n_slot][:, :, :], up_raw[n_slot][:, :, :], ACT.Copy).then_inc(up_high, 1)

            def high_down(g):
                act.wait_ge(down_loaded, g * 16 + 16)
                if not is_first(g):
                    act.wait_ge(down_done, g * (2 * TT))
                nc.scalar.activation(down_hi[:, :, :], down_raw[:, :, :], ACT.Copy).then_inc(down_high, 1)

            for k in range(3):
                act.dma_start(taps_rows[:, k, :], conv_w[k, :].rearrange("(c p) -> c p", p=P)).then_inc(taps_loaded, 16)
            act.dma_start(taps_rows[:, 3, :], conv_b.rearrange("(c p) -> c p", p=P)).then_inc(taps_loaded, 16)
            high_up(0, 0)
            high_up(1, 1)
            act.wait_ge(taps_ready, 1)

            def group(g, par, last=False):
                if not is_first(g):
                    high_down(g - 1)
                for c in range(2):
                    for j in range(2):
                        n = g * 4 + 2 * c + j
                        act.wait_ge(up_done, n + 1)
                        if not (last and c):
                            high_up(j, n + 2)
                        if not is_first(g) or c:
                            act.wait_ge(act_split, g * 2 + c)
                        f = g * 2 + (c + j * FC)
                        nc.scalar.activation(conv_out[j][:, :], ups[j], ACT.Identity,
                                             bias=taps[:, 3, bass.ds(f, 1)], scale=taps[:, 2, bass.ds(f, 1)]
                                             ).then_inc(conv_started, 1)
                        if j == 1:
                            act.wait_ge(conv_done, n)
                            nc.scalar.activation(conv_out[0][:, :], conv_out[0][:, :], ACT.Silu).then_inc(gate_done, 1)
                            act.wait_ge(prod_done, g * 2 + (c + 1))
                            if not is_first(g) and not (isinstance(g, int) and g == 1):
                                act.wait_ge(down_done, g * (2 * TT) - 2 * TT)
                            nc.scalar.activation(act_hi[par][:, c, :], conv_out[0][:, :], ACT.Copy).then_inc(act_high, 1)

            over_groups(act, group)
            high_down(GROUPS - 1)

        @block.vector
        def _(dve):
            def low_up(n_slot, n):
                dve.wait_ge(up_high, n + 1)
                nc.vector.tensor_tensor(up_lo[n_slot][:, :, :], up_raw[n_slot][:, :, :],
                                        up_hi[n_slot][:, :, :].bitcast(F32), ALU.subtract).then_inc(up_split, 1)

            def low_down(g):
                dve.wait_ge(down_high, g + 1)
                nc.vector.tensor_tensor(down_lo[:, :, :], down_raw[:, :, :], down_hi[:, :, :].bitcast(F32),
                                        ALU.subtract).then_inc(down_split, 1)

            def add_group(g, banks):
                for i in banks:
                    dve.wait_ge(down_done, g * (2 * TT) + i + 1)
                    xs = X[:, i // 2, (i % 2) * HALF:(i % 2 + 1) * HALF]
                    nc.vector.tensor_tensor(xs, xs, psum[:, 4 + i % 4, :], ALU.add).then_inc(x_added, 1)

            low_up(0, 0)
            low_up(1, 1)
            dve.wait_ge(taps_turned, 1)
            nc.vector.tensor_copy(taps[:, :, :], psum[:, 4, 0:8 * FC].rearrange("p (k f) -> p k f", k=4)).then_inc(taps_ready, 1)
            dve.wait_ge(taps_ready, 1)

            def group(g, par, last=False):
                if not is_first(g):
                    low_down(g - 1)
                for c in range(2):
                    for j in range(2):
                        n = g * 4 + 2 * c + j
                        if not (last and c):
                            low_up(j, n + 2)
                        f = g * 2 + (c + j * FC)
                        y = conv_out[j]
                        dve.wait_ge(conv_started, n + 1)
                        nc.vector.scalar_tensor_tensor(y[:, 1:SEQ], ups[j][:, 0:SEQ - 1], taps[:, 1, bass.ds(f, 1)],
                                                       y[:, 1:SEQ], ALU.mult, ALU.add).then_inc(conv_tap, 1)
                        dve.wait_ge(conv_tap, n + 1)
                        nc.vector.scalar_tensor_tensor(y[:, 2:SEQ], ups[j][:, 0:SEQ - 2], taps[:, 0, bass.ds(f, 1)],
                                                       y[:, 2:SEQ], ALU.mult, ALU.add).then_inc(conv_done, 1)
                    if c and not is_first(g):
                        add_group(g - 1, range(0, 4))
                    dve.wait_ge(conv_done, g * 4 + 2 * c + 2)
                    dve.wait_ge(gate_done, g * 2 + (c + 1))
                    nc.vector.tensor_tensor(conv_out[0][:, :], conv_out[0][:, :], conv_out[1][:, :],
                                            ALU.mult).then_inc(prod_done, 1)
                    if c and not is_first(g):
                        add_group(g - 1, range(4, 8))
                    dve.wait_ge(prod_done, g * 2 + (c + 1))
                    dve.wait_ge(act_high, g * 2 + (c + 1))
                    nc.vector.tensor_tensor(act_lo[par][:, c, :], conv_out[0][:, :],
                                            act_hi[par][:, c, :].bitcast(F32), ALU.subtract).then_inc(act_split, 1)
                if not is_first(g):
                    add_group(g - 1, range(8, 2 * TT))

            over_groups(dve, group)
            low_down(GROUPS - 1)
            add_group(GROUPS - 1, range(2 * TT))

        @block.tensor
        def _(pe):
            def turn_taps():
                pe.wait_ge(taps_loaded, 64)
                for k in range(4):
                    turn = nc.tensor.transpose(psum[:, 4, k * 2 * FC:(k + 1) * 2 * FC], taps_rows[:, k, :],
                                               ident[0:2 * FC, 0:2 * FC])
                turn.then_inc(taps_turned, 1)

            def down_group(g, par):
                pe.wait_ge(act_split, g * 2 + 2)
                pe.wait_ge(down_split, g + 1)
                for i in range(2 * TT):
                    t, half = i // 2, i % 2
                    if not is_first(g) or i >= 4:
                        pe.wait_ge(x_added, g * (2 * TT) + (i - 3))
                    for c in range(2):
                        tok = slice(t * P, (t + 1) * P)
                        cols = slice(half * HALF, (half + 1) * HALF)
                        last = split_matmul(nc, psum[:, 4 + i % 4, :], act_hi[par][:, c, tok], act_lo[par][:, c, tok],
                                            down_hi[:, c, cols], down_lo[:, c, cols], c == 0, c == 1)
                    last.then_inc(down_done, 1)

            def group(g, par, last=False):
                for c in range(2):
                    for j in range(2):
                        n = g * 4 + 2 * c + j
                        pe.wait_ge(up_split, n + 1)
                        if not is_first(g) or c:
                            pe.wait_ge(conv_done, n - 1)
                        for d in range(DC):
                            for w, h, first, final in ((up_hi, hT_hi, d == 0, False), (up_hi, hT_lo, False, False),
                                                       (up_lo, hT_hi, False, d == DC - 1)):
                                for half in range(2):
                                    mm = nc.tensor.matmul(psum[:, 2 * j + half, :], w[j][:, d, :],
                                                          h[:, d, half * HALF:(half + 1) * HALF],
                                                          start=first, stop=final)
                        mm.then_inc(up_done, 1)
                        if is_first(g) and c == 0 and j == 0:
                            turn_taps()
                if isinstance(g, int) and g == 1:
                    pe.wait_ge(taps_ready, 1)
                if not is_first(g):
                    down_group(g - 1, 1 - par)

            over_groups(pe, group)
            down_group(GROUPS - 1, (GROUPS - 1) % 2)


EPS = 1e-6
N_MEM = 256
XA_HEADS, XA_DIM = 4, 64
D_XA = XA_HEADS * XA_DIM
D_MIX = 768
GLA_HEADS, GLA_DK, GLA_DV, GLA_RANK = 4, 96, 192, 16
CHUNK = 64
DIL_DIM, DIL_HEADS = 128, 4
D_DIL = DIL_DIM * DIL_HEADS
DILATIONS = (1, 4, 16)
NEG = -1e30


class Norm:

    def __init__(self, nc, ctx, ph, psum, bank0, ident, gain_t, neg_half, out_hi, out_lo):
        self.nc, self.psum, self.bank0, self.ident = nc, psum, bank0, ident
        self.gain_t, self.neg_half, self.hi, self.lo = gain_t, neg_half, out_hi, out_lo

        def sb(name, shape):
            return ctx.enter_context(nc.sbuf_tensor(f"{ph}_{name}", shape, F32))

        def sem(name):
            return phase_semaphore(nc, ctx, f"{ph}_{name}")

        self.scaled_rows = [sb(f"scaled_rows{i}", [P, D]) for i in range(2)]
        self.gained_cols = [sb(f"gained_cols{i}", [P, DC, P]) for i in range(1)]
        self.sums = sb("norm_sums", [P, TT])
        self.rstd = sb("norm_rstd", [P, TT])
        self.squared = sem("squared")
        self.mean = sem("mean")
        self.rstd_ready = sem("rstd_ready")
        self.scaled = sem("scaled")
        self.turned = sem("turned")
        self.gained = sem("gained")
        self.high = sem("norm_high")
        self.low = sem("norm_low")

    def act_scale(self, act, t, rows):
        nc, buf = self.nc, self.scaled_rows[t % 2]
        if t >= 2:
            act.wait_ge(self.turned, t - 1)
        nc.scalar.activation(buf[:, :], rows, ACT.Square, accum_out=self.sums[:, t:t + 1]).then_inc(self.squared, 1)
        act.wait_ge(self.rstd_ready, t + 1)
        nc.scalar.activation(buf[:, :], rows, ACT.Copy, scale=self.rstd[:, t:t + 1]).then_inc(self.scaled, 1)

    def pool(self, pool, t):
        nc, s, r = self.nc, self.sums[:, t:t + 1], self.rstd[:, t:t + 1]
        pool.wait_ge(self.squared, t + 1)
        nc.gpsimd.tensor_scalar(s, s, 1.0 / D, EPS, ALU.mult, ALU.add).then_inc(self.mean, 1)
        pool.wait_ge(self.mean, t + 1)
        nc.gpsimd.tensor_tensor(r, s, self.neg_half[:, 0:1], ALU.pow).then_inc(self.rstd_ready, 1)

    def pe(self, pe, t):
        pe.wait_ge(self.scaled, t + 1)
        if t >= 2:
            pe.wait_ge(self.gained, t - 1)
        for d in range(DC):
            turn = self.nc.tensor.transpose(self.psum[:, self.bank0 + 2 * (t % 2) + d // 4, (d % 4) * P:(d % 4 + 1) * P],
                                            self.scaled_rows[t % 2][:, d * P:(d + 1) * P], self.ident[:, :])
        turn.then_inc(self.turned, 1)

    def dve_gain(self, dve, t):
        dve.wait_ge(self.turned, t + 1)
        if t >= 1:
            dve.wait_ge(self.low, t)
        b = self.bank0 + 2 * (t % 2)
        self.nc.vector.tensor_tensor(self.gained_cols[0][:, :, :],
                                     self.psum[:, b:b + 2, :].rearrange("p b (d n) -> p (b d) n", d=4),
                                     self.gain_t[:, :].unsqueeze(2).broadcast_to([P, DC, P]), ALU.mult).then_inc(self.gained, 1)

    def act_high(self, act, t):
        act.wait_ge(self.gained, t + 1)
        self.nc.scalar.activation(self.hi[:, :, t * P:(t + 1) * P], self.gained_cols[0][:, :, :], ACT.Copy).then_inc(self.high, 1)

    def dve_low(self, dve, t):
        dve.wait_ge(self.high, t + 1)
        self.nc.vector.tensor_tensor(self.lo[:, :, t * P:(t + 1) * P], self.gained_cols[0][:, :, :],
                                     self.hi[:, :, t * P:(t + 1) * P].bitcast(F32), ALU.subtract).then_inc(self.low, 1)


def norm_phase(nc, ph, psum, ident, neg_half, rows_dram, tiles, gain, out_hi, out_lo):
    with ExitStack() as ctx:
        ctx.callback(nc.all_engine_barrier)
        rows = [ctx.enter_context(nc.sbuf_tensor(f"{ph}_rows{i}", [P, D], F32)) for i in range(2)]
        gain_t = ctx.enter_context(nc.sbuf_tensor(f"{ph}_gain", [P, DC], F32))
        loaded = [phase_semaphore(nc, ctx, f"{ph}_loaded{i}") for i in range(2)]
        gain_loaded = phase_semaphore(nc, ctx, f"{ph}_gain_loaded")
        norm = Norm(nc, ctx, ph, psum, 0, ident, gain_t, neg_half, out_hi, out_lo)
        block = ctx.enter_context(nc.Block())

        @block.sync
        def _(sp):
            for t in range(tiles):
                if t >= 2:
                    sp.wait_ge(norm.scaled, t - 1)
                sp.dma_start(rows[t % 2][:, :], rows_dram[t * P:(t + 1) * P, :]).then_inc(loaded[t % 2], 16)

        @block.scalar
        def _(act):
            act.dma_start(gain_t[:, :], gain.rearrange("(d p) -> p d", p=P), allow_slow_non_contiguous=True).then_inc(gain_loaded, 16)
            for t in range(tiles):
                act.wait_ge(loaded[t % 2], 16 * (t // 2 + 1))
                norm.act_scale(act, t, rows[t % 2][:, :])
                if t >= 1:
                    norm.act_high(act, t - 1)
            norm.act_high(act, tiles - 1)

        @block.gpsimd
        def _(pool):
            for t in range(tiles):
                norm.pool(pool, t)

        @block.tensor
        def _(pe):
            for t in range(tiles):
                norm.pe(pe, t)

        @block.vector
        def _(dve):
            dve.wait_ge(gain_loaded, 16)
            for t in range(tiles):
                norm.dve_gain(dve, t)
                norm.dve_low(dve, t)


def out_phase(nc, ph, psum, ident, neg_half, XY, chunks, w_out, x_dram, gain, out_hi, out_lo):
    with ExitStack() as ctx:
        ctx.callback(nc.all_engine_barrier)
        def sb(name, shape, dt=F32):
            return ctx.enter_context(nc.sbuf_tensor(f"{ph}_{name}", shape, dt))

        def sem(name):
            return phase_semaphore(nc, ctx, f"{ph}_{name}")

        w_raw = [sb(f"w_raw{i}", [P, D]) for i in range(2)]
        w_hi = sb("w_hi", [P, chunks, D], F32R)
        w_lo = sb("w_lo", [P, chunks, D], F32R)
        y_hi = sb("y_hi", [P, chunks, P], F32R)
        y_lo = sb("y_lo", [P, chunks, P], F32R)
        x_old = sb("x_old", [P, D])
        gain_t = sb("gain", [P, DC])
        w_loaded = [sem(f"w_loaded{i}") for i in range(2)]
        gain_loaded = sem("gain_loaded")
        x_loaded = sem("x_loaded")
        w_high, w_split = sem("w_high"), sem("w_split")
        y_turned = sem("y_turned")
        y_high, y_split = sem("y_high"), sem("y_split")
        summed = sem("summed")
        x_ready = sem("x_ready")
        norm = Norm(nc, ctx, ph, psum, 4, ident, gain_t, neg_half, out_hi, out_lo)
        block = ctx.enter_context(nc.Block())

        @block.sync
        def _(sp):
            for k in range(chunks):
                if k >= 2:
                    sp.wait_ge(w_split, k - 1)
                sp.dma_start(w_raw[k % 2][:, :], w_out[k * P:(k + 1) * P, :]).then_inc(w_loaded[k % 2], 16)
            for t in range(TT):
                if t >= 1:
                    sp.wait_ge(x_ready, 2 * t)
                sp.dma_start(x_old[:, :], x_dram[t * P:(t + 1) * P, :]).then_inc(x_loaded, 16)

        def y_cols(t):
            b = 2 * (t % 2)
            return psum[:, b:b + 2, :].rearrange("p b (d n) -> p (b d) n", d=4)[:, 0:chunks, :]

        @block.scalar
        def _(act):
            act.dma_start(gain_t[:, :], gain.rearrange("(d p) -> p d", p=P), allow_slow_non_contiguous=True).then_inc(gain_loaded, 16)

            def y_part(t):
                act.wait_ge(y_turned, t + 1)
                if t >= 1:
                    act.wait_ge(summed, 2 * t)
                nc.scalar.activation(y_hi[:, :, :], y_cols(t), ACT.Copy).then_inc(y_high, 1)

            for k in range(chunks):
                act.wait_ge(w_loaded[k % 2], 16 * (k // 2 + 1))
                nc.scalar.activation(w_hi[:, k, :], w_raw[k % 2][:, :], ACT.Copy).then_inc(w_high, 1)
                if k == 0:
                    y_part(0)
            for t in range(TT):
                if t + 1 < TT:
                    y_part(t + 1)
                act.wait_ge(x_ready, 2 * t + 2)
                norm.act_scale(act, t, XY[:, t, :])
                if t >= 1:
                    norm.act_high(act, t - 1)
            norm.act_high(act, TT - 1)

        @block.gpsimd
        def _(pool):
            for t in range(TT):
                norm.pool(pool, t)

        @block.vector
        def _(dve):
            dve.wait_ge(gain_loaded, 16)

            def y_part(t):
                dve.wait_ge(y_high, t + 1)
                nc.vector.tensor_tensor(y_lo[:, :, :], y_cols(t), y_hi[:, :, :].bitcast(F32), ALU.subtract).then_inc(y_split, 1)

            for k in range(chunks):
                dve.wait_ge(w_high, k + 1)
                nc.vector.tensor_tensor(w_lo[:, k, :], w_raw[k % 2][:, :], w_hi[:, k, :].bitcast(F32), ALU.subtract).then_inc(w_split, 1)
                if k == 0:
                    y_part(0)
            for t in range(TT):
                dve.wait_ge(x_loaded, 16 * (t + 1))
                for half in range(2):
                    cols = slice(half * HALF, (half + 1) * HALF)
                    dve.wait_ge(summed, 2 * t + half + 1)
                    nc.vector.tensor_tensor(XY[:, t, cols], psum[:, 2 * (t % 2) + half, :], x_old[:, cols], ALU.add).then_inc(x_ready, 1)
                if t + 1 < TT:
                    y_part(t + 1)
                if t >= 1:
                    norm.dve_gain(dve, t - 1)
                    norm.dve_low(dve, t - 1)
            norm.dve_gain(dve, TT - 1)
            norm.dve_low(dve, TT - 1)

        @block.tensor
        def _(pe):
            def y_turn(t):
                if t >= 2:
                    pe.wait_ge(x_ready, 2 * t - 2)
                for k in range(chunks):
                    turn = nc.tensor.transpose(psum[:, 2 * (t % 2) + k // 4, (k % 4) * P:(k % 4 + 1) * P],
                                               XY[:, t, k * P:(k + 1) * P], ident[:, :])
                turn.then_inc(y_turned, 1)

            y_turn(0)
            for t in range(TT):
                if t + 1 < TT:
                    y_turn(t + 1)
                pe.wait_ge(y_split, t + 1)
                for half in range(2):
                    cols = slice(half * HALF, (half + 1) * HALF)
                    for k in range(chunks):
                        if t == 0 and half == 0:
                            pe.wait_ge(w_split, k + 1)
                        last = split_matmul(nc, psum[:, 2 * (t % 2) + half, :], y_hi[:, k, :], y_lo[:, k, :],
                                            w_hi[:, k, cols], w_lo[:, k, cols], k == 0, k == chunks - 1)
                    last.then_inc(summed, 1)
                if t >= 1:
                    norm.pe(pe, t - 1)
            norm.pe(pe, TT - 1)


def project_phase(nc, ph, psum, ident, neg_half, tiles, stat_hi, stat_lo, blocks, extra_loads=()):
    half_d = DC // 2
    groups, t = [], 0
    while t < tiles:
        groups.append(list(range(t, min(t + 3, tiles))))
        t += 3
    n_groups = len(groups)
    dve_kinds = ("heads",)
    freed, count = [], {"act": 0, "dve": 0}
    heads_before = []
    n_heads = 0
    for b in blocks:
        for t in range(tiles):
            who = "dve" if b["kind"] in dve_kinds else "act"
            count[who] += 1
            freed.append((who, count[who]))
            heads_before.append(n_heads)
            n_heads += b["kind"] == "heads"
    gates_before, n = [], 0
    for b in blocks:
        gates_before.append(n)
        n += tiles * (b["kind"] == "gate")

    with ExitStack() as ctx:
        ctx.callback(nc.all_engine_barrier)
        def sb(name, shape, dt=F32):
            return ctx.enter_context(nc.sbuf_tensor(f"{ph}_{name}", shape, dt))

        def sem(name):
            return phase_semaphore(nc, ctx, f"{ph}_{name}")

        width = max(b["w"].shape[1] for b in blocks)
        w_raw = [sb(f"w_raw{i}", [P, half_d, width]) for i in range(2)]
        w_hi = [sb(f"w_hi{i}", [P, half_d, width], F32R) for i in range(2)]
        w_lo = [sb(f"w_lo{i}", [P, half_d, width], F32R) for i in range(2)]
        w_loaded = [sem(f"w_loaded{i}") for i in range(2)]
        extra_loaded = sem("extra_loaded")
        w_high, w_split = sem("w_high"), sem("w_split")
        first_read = sem("first_read")
        done = sem("done")
        gate_free = sem("gate_gained")
        if n_heads:
            hw = max(b["w"].shape[1] for b in blocks if b["kind"] == "heads")
            squares = sb("squares", [P, 2, hw])
            sums = sb("head_sums", [P, 2, 4])
            rstd = sb("head_rstd", [P, 2, 4])
            rows = sb("head_rows", [P, hw])
            roped = [sb(f"head_roped{i}", [P, hw]) for i in range(3)]
            cross = sb("rope_cross", [P, hw])
        squared, mean, rstd_ready = sem("squared"), sem("mean"), sem("rstd_ready")
        rows_ready, link = sem("rows_ready"), sem("rope_link")
        turned, turn_out = sem("turned"), sem("turn_out")
        free = {"act": sem("freed_by_act"), "dve": rows_ready}

        def bank_of(T):
            b, t = divmod(T, tiles)
            g = t // 3
            return 3 * ((b * n_groups + g) % 2) + t % 3

        block = ctx.enter_context(nc.Block())

        @block.sync
        def _(sp):
            for out, src in extra_loads:
                sp.dma_start(out, src).then_inc(extra_loaded, 16)
            for s in range(2 * len(blocks)):
                b, kh = divmod(s, 2)
                w = blocks[b]["w"]
                if s >= 2:
                    sp.wait_ge(w_split, s - 1)
                sp.dma_start(w_raw[kh][:, :, 0:w.shape[1]],
                             w.rearrange("(d p) n -> p d n", p=P)[:, kh * half_d:(kh + 1) * half_d, :]).then_inc(w_loaded[kh], 16)

        def slots_free(eng, s):
            b, kh = divmod(s, 2)
            if b >= 1:
                if kh == 0:
                    eng.wait_ge(first_read, b)
                else:
                    eng.wait_ge(done, tiles * b)

        def over_tiles(split, tile, turn):
            split(0)
            split(1)
            before = []
            for b in range(len(blocks)):
                for g, group in enumerate(groups):
                    if g == n_groups - 1 and b + 1 < len(blocks):
                        split(2 * b + 2)
                    for t in group:
                        tile(b, t)
                    if g == n_groups - 1 and b + 1 < len(blocks):
                        split(2 * b + 3)
                    for bt in before:
                        turn(*bt)
                    before = [(b, t) for t in group]
            for bt in before:
                turn(*bt)

        @block.scalar
        def _(act):
            if extra_loads:
                act.wait_ge(extra_loaded, 16 * len(extra_loads))

            def split(s):
                b, kh = divmod(s, 2)
                n = blocks[b]["w"].shape[1]
                act.wait_ge(w_loaded[kh], 16 * (b + 1))
                slots_free(act, s)
                nc.scalar.activation(w_hi[kh][:, :, 0:n], w_raw[kh][:, :, 0:n], ACT.Copy).then_inc(w_high, 1)

            def tile(b, t):
                blk, T = blocks[b], b * tiles + t
                n = blk["w"].shape[1]
                acc = psum[:, bank_of(T), 0:n]
                act.wait_ge(done, T + 1)
                if blk["kind"] == "heads":
                    H, dim = heads_before[T], blk["dim"]
                    if H >= 2:
                        act.wait_ge(rows_ready, H - 1)
                    for h in range(n // dim):
                        nc.scalar.activation(squares[:, H % 2, h * dim:(h + 1) * dim], acc[:, h * dim:(h + 1) * dim], ACT.Square,
                                             accum_out=sums[:, H % 2, h:h + 1]).then_inc(squared, 1)
                else:
                    nc.scalar.activation(blk["dest"](t), acc, ACT.Silu if blk["kind"] == "gate" else ACT.Copy).then_inc(free["act"], 1)

            def turn(b, t):
                blk, T = blocks[b], b * tiles + t
                if blk["kind"] != "heads":
                    return
                H, n = heads_before[T], blk["w"].shape[1]
                act.wait_ge(turned, H + 1)
                for i, (dst, src) in enumerate(blk["dest"](t, psum[:, 6 + H % 2, 0:n])):
                    ins = nc.scalar.activation(dst, src, ACT.Copy)
                ins.then_inc(turn_out, 1)

            over_tiles(split, tile, turn)

        @block.gpsimd
        def _(pool):
            n_sq = 0
            for b, blk in enumerate(blocks):
                if blk["kind"] != "heads":
                    continue
                for t in range(tiles):
                    H, nh, dim = heads_before[b * tiles + t], blk["w"].shape[1] // blk["dim"], blk["dim"]
                    n_sq += nh
                    s, r = sums[:, H % 2, 0:nh], rstd[:, H % 2, 0:nh]
                    pool.wait_ge(squared, n_sq)
                    if H >= 2:
                        pool.wait_ge(rows_ready, H - 1)
                    nc.gpsimd.tensor_scalar(s, s, 1.0 / dim, EPS, ALU.mult, ALU.add).then_inc(mean, 1)
                    pool.wait_ge(mean, H + 1)
                    nc.gpsimd.tensor_tensor(r, s, neg_half[:, 0:nh], ALU.pow).then_inc(rstd_ready, 1)

        @block.vector
        def _(dve):
            if extra_loads:
                dve.wait_ge(extra_loaded, 16 * len(extra_loads))
            links = [0]

            def split(s):
                b, kh = divmod(s, 2)
                n = blocks[b]["w"].shape[1]
                dve.wait_ge(w_high, s + 1)
                nc.vector.tensor_tensor(w_lo[kh][:, :, 0:n], w_raw[kh][:, :, 0:n], w_hi[kh][:, :, 0:n].bitcast(F32),
                                        ALU.subtract).then_inc(w_split, 1)

            def tile(b, t):
                blk, T = blocks[b], b * tiles + t
                n = blk["w"].shape[1]
                acc = psum[:, bank_of(T), 0:n]
                if blk["kind"] == "gate":
                    dve.wait_ge(free["act"], freed[T][1])
                    out = blk["dest"](t).rearrange("p (h v) -> p h v", v=GLA_DV)
                    nc.vector.tensor_tensor(out, out, blk["gain"].unsqueeze(1).broadcast_to([P, n // GLA_DV, GLA_DV]),
                                            ALU.mult).then_inc(gate_free, 1)
                if blk["kind"] != "heads":
                    return
                H, dim = heads_before[T], blk["dim"]
                nh, buf = n // dim, rows if blk.get("rope") else roped[H % 3]
                dve.wait_ge(rstd_ready, H + 1)
                if H >= 3:
                    dve.wait_ge(turned, H - 2)
                for h in range(nh):
                    cols = slice(h * dim, (h + 1) * dim)
                    ins = nc.vector.scalar_tensor_tensor(buf[:, cols], acc[:, cols], rstd[:, H % 2, h:h + 1],
                                                         blk["gain"], ALU.mult, ALU.mult)
                if not blk.get("rope"):
                    ins.then_inc(rows_ready, 1)
                    return
                links[0] += 1
                ins.then_inc(link, 1)
                dve.wait_ge(link, links[0])
                half = dim // 2
                cos, sin = (x[:, t, :].unsqueeze(1).broadcast_to([P, nh, half]) for x in blk["rope"])
                x = buf[:, 0:n].rearrange("p (h two k) -> p h two k", two=2, k=half)
                o = roped[H % 3][:, 0:n].rearrange("p (h two k) -> p h two k", two=2, k=half)
                c = cross[:, 0:n].rearrange("p (h two k) -> p h two k", two=2, k=half)
                for two in range(2):
                    nc.vector.tensor_tensor(o[:, :, two, :], x[:, :, two, :], cos, ALU.mult)
                    ins = nc.vector.tensor_tensor(c[:, :, two, :], x[:, :, 1 - two, :], sin, ALU.mult)
                links[0] += 1
                ins.then_inc(link, 1)
                dve.wait_ge(link, links[0])
                nc.vector.tensor_tensor(o[:, :, 0, :], o[:, :, 0, :], c[:, :, 0, :], ALU.subtract)
                nc.vector.tensor_tensor(o[:, :, 1, :], o[:, :, 1, :], c[:, :, 1, :], ALU.add).then_inc(rows_ready, 1)

            over_tiles(split, tile, lambda b, t: None)

        @block.tensor
        def _(pe):
            before = []

            def turns():
                for b, t in before:
                    blk, T = blocks[b], b * tiles + t
                    if blk["kind"] != "heads":
                        continue
                    H, n = heads_before[T], blk["w"].shape[1]
                    pe.wait_ge(rows_ready, H + 1)
                    if H >= 2:
                        pe.wait_ge(turn_out, H - 1)
                    for i in range(n // P):
                        ins = nc.tensor.transpose(psum[:, 6 + H % 2, i * P:(i + 1) * P],
                                                  roped[H % 3][:, i * P:(i + 1) * P], ident[:, :])
                    ins.then_inc(turned, 1)

            for b, blk in enumerate(blocks):
                n = blk["w"].shape[1]
                for g, group in enumerate(groups):
                    G = b * n_groups + g
                    if G >= 2:
                        b2, g2 = divmod(G - 2, n_groups)
                        for who in ("act", "dve"):
                            upto = [v for w, v in freed[:b2 * tiles + groups[g2][-1] + 1] if w == who]
                            if upto:
                                pe.wait_ge(free[who], upto[-1])
                    for kh in range(2):
                        pe.wait_ge(w_split, 2 * b + kh + 1)
                        for t in group:
                            for d in range(half_d):
                                dd = kh * half_d + d
                                last = split_matmul(nc, psum[:, bank_of(b * tiles + t), 0:n],
                                                    blk["pick"](stat_hi, dd, t), blk["pick"](stat_lo, dd, t),
                                                    w_hi[kh][:, d, 0:n], w_lo[kh][:, d, 0:n], dd == 0, dd == DC - 1)
                            if kh == 1:
                                last.then_inc(done, 1)
                        if kh == 0 and g == n_groups - 1:
                            last.then_inc(first_read, 1)
                    turns()
                    before[:] = [(b, t) for t in group]
            turns()


def attention_phase(nc, ph, psum, ident, scale, units, stage_tile=None, lse=None):
    U = len(units)
    with ExitStack() as ctx:
        ctx.callback(nc.all_engine_barrier)
        def sb(name, shape, dt=F32):
            return ctx.enter_context(nc.sbuf_tensor(f"{ph}_{name}", shape, dt))

        def sem(name):
            return phase_semaphore(nc, ctx, f"{ph}_{name}")

        S, T, O = 3, 2, 2
        masked = [sb(f"masked{i}", [P, 2 * P]) for i in range(3)]
        probs = [sb(f"probs{i}", [P, 2 * P]) for i in range(3)]
        probs_t = [sb(f"probs_t{i}", [P, 2 * P]) for i in range(3)]
        top = sb("top", [P, U])
        neg_top = sb("neg_top", [P, U])
        total = sb("total", [P, U])
        inv = sb("inv", [P, U])
        scored = sem("scored")
        topped = sem("topped")
        negated = sem("negated")
        expd = sem("expd")
        turned = sem("turned")
        turn_out = sem("turn_out")
        mixed = sem("mixed")
        inverted = sem("inverted")
        out_done = sem("out_done")
        stored = sem("stored")
        logged, lse_done = sem("logged"), sem("lse_done")
        block = ctx.enter_context(nc.Block())
        T_LAG, O_LAG = 2, 3

        @block.tensor
        def _(pe):
            for i in range(U + O_LAG):
                if i < U:
                    q, k, n, mask, vals, out = units[i]
                    if i >= S:
                        pe.wait_ge(topped, i - S + 1)
                    nc.tensor.matmul(psum[:, i % S, 0:n], q, k, start=True, stop=True).then_inc(scored, 1)
                u = i - T_LAG
                if 0 <= u < U:
                    n = units[u][2]
                    pe.wait_ge(expd, u + 1)
                    if u >= T:
                        pe.wait_ge(turn_out, u - T + 1)
                    for c in range(n // P):
                        ins = nc.tensor.transpose(psum[:, S + u % T, c * P:(c + 1) * P], probs[u % 3][:, c * P:(c + 1) * P], ident[:, :])
                    ins.then_inc(turned, 1)
                u = i - O_LAG
                if 0 <= u < U:
                    n, vals = units[u][2], units[u][4]
                    pe.wait_ge(turn_out, u + 1)
                    if u >= O:
                        pe.wait_ge(out_done, u - O + 1)
                    for c, v in enumerate(vals):
                        ins = nc.tensor.matmul(psum[:, S + T + u % O, 0:v.shape[-1]], probs_t[u % 3][:, c * P:(c + 1) * P], v,
                                               start=c == 0, stop=c == len(vals) - 1)
                    ins.then_inc(mixed, 1)

        @block.vector
        def _(dve):
            for i in range(U + O_LAG):
                if i < U:
                    n, mask = units[i][2], units[i][3]
                    dve.wait_ge(scored, i + 1)
                    if i >= 3:
                        dve.wait_ge(expd, i - 2)
                    nc.vector.tensor_tensor_reduce(masked[i % 3][:, 0:n], psum[:, i % S, 0:n], mask, 1.0, -3e38,
                                                   ALU.add, ALU.max, top[:, i:i + 1]).then_inc(topped, 1)
                    dve.wait_ge(topped, i + 1)
                    nc.vector.tensor_scalar(neg_top[:, i:i + 1], top[:, i:i + 1], -scale, None, ALU.mult).then_inc(negated, 1)
                u = i - T_LAG
                if 0 <= u < U:
                    n = units[u][2]
                    dve.wait_ge(turned, u + 1)
                    if u >= 3:
                        dve.wait_ge(mixed, u - 2)
                    nc.vector.tensor_copy(probs_t[u % 3][:, 0:n], psum[:, S + u % T, 0:n]).then_inc(turn_out, 1)
                    nc.vector.reciprocal(inv[:, u:u + 1], total[:, u:u + 1]).then_inc(inverted, 1)
            if lse is not None:
                dve.wait_ge(logged, 1)
                nc.vector.scalar_tensor_tensor(lse[:, 0:U], top[:, :], scale, total[:, :], ALU.mult, ALU.add).then_inc(lse_done, 1)
                dve.wait_ge(lse_done, 1)

        @block.scalar
        def _(act):
            for i in range(U + O_LAG):
                if i < U:
                    n = units[i][2]
                    act.wait_ge(negated, i + 1)
                    if i >= 3:
                        act.wait_ge(turned, i - 2)
                    nc.scalar.activation(probs[i % 3][:, 0:n], masked[i % 3][:, 0:n], ACT.Exp, bias=neg_top[:, i:i + 1],
                                         scale=scale, accum_out=total[:, i:i + 1]).then_inc(expd, 1)
                u = i - O_LAG
                if 0 <= u < U:
                    w, out = units[u][4][0].shape[-1], units[u][5]
                    act.wait_ge(mixed, u + 1)
                    act.wait_ge(inverted, u + 1)
                    if stage_tile is not None and u >= 8 and u % 4 == 0:
                        act.wait_ge(stored, 16 * stage_tile.parts * (u // 4 - 1))
                    nc.scalar.activation(out, psum[:, S + T + u % O, 0:w], ACT.Copy, scale=inv[:, u:u + 1]).then_inc(out_done, 1)
            if lse is not None:
                act.wait_ge(inverted, U)
                nc.scalar.activation(total[:, :], total[:, :], ACT.Ln).then_inc(logged, 1)

        if stage_tile is not None:
            @block.sync
            def _(sp):
                for t in range(U // 4):
                    sp.wait_ge(out_done, 4 * t + 4)
                    if t >= 1:
                        sp.wait_ge(stored, 16 * stage_tile.parts * t)
                    stage_tile(sp, t, stored)
                sp.wait_ge(lse_done, 1)
                n = stage_tile.parts * (U // 4)
                n += stage_tile.store_lse(sp, stored)
                sp.wait_ge(stored, 16 * n)


def gla_phase(nc, ph, psum, ident, neg_half, hT_hi, hT_lo, w_in, w_gate2, b_gate, V, Y):
    DK, DV, PAIRS, CH = GLA_DK, GLA_DV, SEQ // P, SEQ // CHUNK
    QK = 2 * DK
    with ExitStack() as ctx:
        ctx.callback(nc.all_engine_barrier)
        def sb(name, shape, dt=F32):
            return ctx.enter_context(nc.sbuf_tensor(f"{ph}_{name}", shape, dt))

        def sem(name):
            return phase_semaphore(nc, ctx, f"{ph}_{name}")

        w_raw = sb("w_raw", [P, DC, QK])
        w_hi, w_lo = sb("w_hi", [P, DC, QK], F32R), sb("w_lo", [P, DC, QK], F32R)
        rank = sb("rank", [GLA_RANK, SEQ])
        gate2 = sb("gate2", [GLA_RANK, GLA_HEADS * DK])
        bias = sb("bias", [DK, GLA_HEADS])
        keep = sb("keep", [DK, SEQ])
        z = sb("z", [DK, SEQ])
        soft = sb("soft", [DK, SEQ])
        cum = sb("cum", [DK, SEQ])
        from_mid, to_last = soft, z
        q_mid, k_mid = sb("q_mid", [DK, SEQ]), sb("k_mid", [DK, SEQ])
        q_in, k_out = sb("q_in", [DK, SEQ]), sb("k_out", [DK, SEQ])
        chunk_decay = sb("chunk_decay", [DK, CH])
        decay = sb("decay", [DK, PAIRS])
        att = sb("att", [P, PAIRS, P])
        k_rows = sb("k_rows", [P, PAIRS, DK])
        state = sb("state", [DK, PAIRS, DV])
        squares = sb("squares", [P, 2, DV])
        sums, rstd = sb("sums", [P, PAIRS]), sb("rstd", [P, PAIRS])

        small_loaded = sem("small_loaded")
        w_loaded, w_high, w_split = sem("w_loaded"), sem("w_high"), sem("w_split")
        kept = sem("kept")
        projected = sem("projected")
        rank_ready = sem("rank_ready")
        copied = sem("copied")
        z_ready = sem("z_ready")
        softened = sem("softened")
        act_link, link = sem("act_link"), sem("dve_link")
        shifted = sem("shifted")
        expd = sem("expd")
        timed = sem("timed")
        factored = sem("factored")
        mixed = sem("mixed")
        masked = sem("masked")
        state_ready = sem("state_ready")
        squared, mean, rstd_ready = sem("squared"), sem("mean"), sem("rstd_ready")
        by_act, by_dve = sem("ring_freed_by_act"), sem("ring_freed_by_dve")

        PER_HEAD = [("att", "act")] * 2 + [("cross", "dve")] + [("keys", "act")] * 2 + [("delta", "state")] * 4 + [("out", "dve")] * 4
        ring = [("z", "act")] * 2
        q_sb, k_sb = (Y[0:DK, :, D_MIX + i * P:D_MIX + (i + 1) * P] for i in range(2))
        first_of, z_of = [], [0]
        for h in range(GLA_HEADS):
            if h + 1 < GLA_HEADS:
                z_of.append(len(ring))
                ring += [("z", "act")] * 2
            first_of.append(len(ring))
            ring += PER_HEAD

        def freed(i):
            kind, who = ring[i]
            if kind == "delta":
                h = max(h for h in range(GLA_HEADS) if first_of[h] <= i)
                return state_ready, (PAIRS - 1) * h + min(2 * (i - first_of[h] - 5) + 2, PAIRS - 1)
            return (by_act if who == "act" else by_dve), sum(w == who for _, w in ring[:i + 1])

        def bank(i):
            return psum[:, 4 + i % 4, :]

        def mixes_before(i):
            return sum(kind != "z" for kind, _ in ring[:i])

        block = ctx.enter_context(nc.Block())
        w_view = w_in.rearrange("(d p) n -> p d n", p=P)

        @block.sync
        def _(sp):
            sp.dma_start(gate2[:, :], w_gate2).then_inc(small_loaded, 16)
            sp.dma_start(bias[:, :], b_gate.rearrange("(h k) -> k h", k=DK), allow_slow_non_contiguous=True).then_inc(small_loaded, 16)
            off = 2 * GLA_HEADS * DK + D_MIX
            sp.dma_start(w_raw[:, :, 0:P], w_view[:, :, off:off + P]).then_inc(w_loaded, 16)
            for h in range(GLA_HEADS):
                sp.wait_ge(w_split, h + 1)
                for part in range(2):
                    sp.dma_start(w_raw[:, :, part * DK:(part + 1) * DK],
                                 w_view[:, :, (part * GLA_HEADS + h) * DK:(part * GLA_HEADS + h + 1) * DK]).then_inc(w_loaded, 16)

        @block.gpsimd
        def _(pool):
            nc.gpsimd.memset(keep[:, :], 1.0).then_inc(kept, 1)
            pool.wait_ge(kept, 1)
            nc.gpsimd.memset(keep[:, :].rearrange("p (c i) -> p c i", i=CHUNK)[:, :, 0:1], 0.0).then_inc(kept, 1)
            for h in range(GLA_HEADS):
                pool.wait_ge(*freed(first_of[h] + 1))
                pool.wait_ge(*freed(first_of[h] + 2))
                nc.gpsimd.affine_select(out=att[:, :, :], in_=att[:, :, :], compare_op=ALU.is_ge, fill=0.0, base=0,
                                        pattern=[[0, PAIRS], [1, P]], channel_multiplier=-1).then_inc(masked, 1)
                pool.wait_ge(squared, PAIRS * (h + 1))
                nc.gpsimd.tensor_scalar(sums[:, :], sums[:, :], 1.0 / DV, EPS, ALU.mult, ALU.add).then_inc(mean, 1)
                pool.wait_ge(mean, h + 1)
                nc.gpsimd.tensor_tensor(rstd[:, :], sums[:, :], neg_half[:, 0:PAIRS], ALU.pow).then_inc(rstd_ready, 1)

        @block.scalar
        def _(act):
            links = [0]

            def high(s):
                act.wait_ge(w_loaded, 16 if s == 0 else 16 + 32 * s)
                if s:
                    act.wait_ge(projected, 2 * s - 1)
                n = P if s == 0 else QK
                nc.scalar.activation(w_hi[:, :, 0:n], w_raw[:, :, 0:n], ACT.Copy).then_inc(w_high, 1)

            def copy(h, i):
                act.wait_ge(projected, 2 * h + 2 + i)
                if h:
                    act.wait_ge(timed, 4 * h - i)
                nc.scalar.activation((q_sb, k_sb)[i], psum[0:DK, 2 * i:2 * i + 2, :].rearrange("p b (c n) -> p (b c) n", n=P),
                                     ACT.Copy).then_inc(copied, 1)

            def gate(h):
                if h:
                    act.wait_ge(expd, 4 * h)
                for half in range(2):
                    cols, src = slice(half * HALF, (half + 1) * HALF), bank(z_of[h] + half)[0:DK, :]
                    act.wait_ge(z_ready, 2 * h + half + 1)
                    nc.scalar.activation(z[:, cols], src, ACT.Identity, bias=bias[:, h:h + 1])
                    nc.scalar.activation(soft[:, cols], src, ACT.Abs, bias=bias[:, h:h + 1]).then_inc(by_act, 1)
                act.wait_ge(by_act, freed(z_of[h] + 1)[1])
                nc.scalar.activation(soft[:, :], soft[:, :], ACT.Exp, scale=-1.0).then_inc(act_link, 1)
                links[0] += 1
                act.wait_ge(act_link, links[0])
                nc.scalar.activation(soft[:, :], soft[:, :], ACT.Ln, bias=1.0).then_inc(softened, 1)

            def factor(h, i):
                out, src, s, entries = ((q_mid, from_mid, 1, 2), (k_mid, from_mid, -1, 2), (k_out, to_last, 1, 5), (q_in, cum, 1, 13))[i]
                act.wait_ge(shifted, h + 1)
                if h:
                    act.wait_ge(mixed, mixes_before(first_of[h - 1] + entries))
                nc.scalar.activation(out[:, :], src[:, :], ACT.Exp, scale=s / 16.0).then_inc(expd, 1)

            high(0)
            act.wait_ge(projected, 1)
            act.wait_ge(small_loaded, 32)
            for half in range(2):
                nc.scalar.activation(rank[:, half * HALF:(half + 1) * HALF], psum[0:GLA_RANK, half, :], ACT.Copy).then_inc(rank_ready, 1)
            high(1)
            gate(0)
            for i in range(4):
                factor(0, i)
            copy(0, 0)
            copy(0, 1)
            high(2)
            for h in range(GLA_HEADS):
                f, more = first_of[h], h + 1 < GLA_HEADS
                if more:
                    gate(h + 1)
                if h:
                    act.wait_ge(mixed, mixes_before(f))
                for i in range(2):
                    act.wait_ge(mixed, mixes_before(f + i) + 1)
                    nc.scalar.activation(att[:, 4 * i:4 * i + 4, :], bank(f + i).rearrange("p (c n) -> p c n", n=P), ACT.Copy).then_inc(by_act, 1)
                if more:
                    factor(h + 1, 0)
                    factor(h + 1, 1)
                    copy(h + 1, 0)
                for i in range(2):
                    act.wait_ge(mixed, mixes_before(f + 3 + i) + 1)
                    nc.scalar.activation(k_rows[:, 4 * i:4 * i + 4, :], bank(f + 3 + i)[:, 0:4 * DK].rearrange("p (c k) -> p c k", k=DK),
                                         ACT.Copy).then_inc(by_act, 1)
                if more:
                    factor(h + 1, 2)
                    copy(h + 1, 1)
                if h + 2 < GLA_HEADS:
                    high(h + 3)
                if h:
                    act.wait_ge(rstd_ready, h)
                for p in range(PAIRS):
                    act.wait_ge(mixed, mixes_before(f + 9 + p // 2) + 1)
                    if h or p >= 2:
                        act.wait_ge(squared, PAIRS * h + p - 1)
                    nc.scalar.activation(squares[:, p % 2, :], bank(f + 9 + p // 2)[:, (p % 2) * DV:(p % 2 + 1) * DV], ACT.Square,
                                         accum_out=sums[:, p:p + 1]).then_inc(squared, 1)
                if more:
                    factor(h + 1, 3)

        @block.vector
        def _(dve):
            links = [0]

            def chain(ins):
                ins.then_inc(link, 1)
                links[0] += 1
                dve.wait_ge(link, links[0])

            def low(s):
                dve.wait_ge(w_high, s + 1)
                n = P if s == 0 else QK
                nc.vector.tensor_tensor(w_lo[:, :, 0:n], w_raw[:, :, 0:n], w_hi[:, :, 0:n].bitcast(F32), ALU.subtract).then_inc(w_split, 1)

            def sums_of(h):
                dve.wait_ge(softened, h + 1)
                chain(nc.vector.scalar_tensor_tensor(soft[:, :], z[:, :], 0.0, soft[:, :], ALU.min, ALU.subtract))
                chain(nc.vector.tensor_tensor_scan(cum[:, :], keep[:, :], soft[:, :], 0.0, ALU.mult, ALU.add))
                c = cum[:, :].rearrange("p (c i) -> p c i", i=CHUNK)
                mid, last = (c[:, :, i:i + 1].broadcast_to([DK, CH, CHUNK]) for i in (CHUNK // 2 - 1, CHUNK - 1))
                nc.vector.tensor_tensor(from_mid[:, :].rearrange("p (c i) -> p c i", i=CHUNK), c, mid, ALU.subtract)
                nc.vector.tensor_tensor(to_last[:, :].rearrange("p (c i) -> p c i", i=CHUNK), last, c, ALU.subtract).then_inc(shifted, 1)

            def product(h, i):
                x, src = ((q_mid, q_sb), (k_mid, k_sb), (k_out, k_sb), (q_in, q_sb))[i]
                x = x[:, :].rearrange("p (c n) -> p c n", n=P)
                dve.wait_ge(expd, 4 * h + i + 1)
                if i == 3:
                    chain(nc.vector.tensor_copy(chunk_decay[:, :], q_in[:, :].rearrange("p (c i) -> p c i", i=CHUNK)[:, :, CHUNK - 1]))
                    cd = chunk_decay[:, :].rearrange("p (c two) -> p c two", two=2)
                    nc.vector.tensor_tensor(decay[:, :], cd[:, :, 0], cd[:, :, 1], ALU.mult)
                if src is q_sb:
                    dve.wait_ge(copied, 2 * h + 1)
                    nc.vector.scalar_tensor_tensor(x, src, float(DK) ** -0.5, x, ALU.mult, ALU.mult).then_inc(timed, 1)
                else:
                    dve.wait_ge(copied, 2 * h + 2)
                    nc.vector.tensor_tensor(x, src, x, ALU.mult).then_inc(timed, 1)

            def cross_pair(h):
                qi = q_in[:, :].rearrange("p (c two i) -> p c two i", two=2, i=CHUNK)
                ko = k_out[:, :].rearrange("p (c two i) -> p c two i", two=2, i=CHUNK)
                cd = chunk_decay[:, :].rearrange("p (c two) -> p c two", two=2)
                f = first_of[h]
                dve.wait_ge(mixed, mixes_before(f + 2) + 1)
                dve.wait_ge(timed, 4 * h + 4)
                nc.vector.tensor_tensor(qi[:, :, 1, :], qi[:, :, 1, :], cd[:, :, 0:1].broadcast_to([DK, PAIRS, CHUNK]), ALU.mult)
                nc.vector.tensor_tensor(ko[:, :, 0, :], ko[:, :, 0, :], cd[:, :, 1:2].broadcast_to([DK, PAIRS, CHUNK]), ALU.mult).then_inc(factored, 1)
                dve.wait_ge(*freed(f + 1))
                nc.vector.tensor_copy(att[0:CHUNK, :, CHUNK:P], bank(f + 2)[0:CHUNK, :].rearrange("p (c i) -> p c i", i=CHUNK)).then_inc(by_dve, 1)

            def states(h):
                f = first_of[h]
                for p in range(PAIRS - 1):
                    delta = bank(f + 5 + p // 2)[0:DK, (p % 2) * DV:(p % 2 + 1) * DV]
                    dve.wait_ge(mixed, mixes_before(f + 5 + p // 2) + 1)
                    if p == 0:
                        ins = nc.vector.tensor_copy(state[:, 1, :], delta)
                    else:
                        ins = nc.vector.scalar_tensor_tensor(state[:, p + 1, :], state[:, p, :], decay[:, p:p + 1], delta, ALU.mult, ALU.add)
                    ins.then_inc(state_ready, 1)
                    dve.wait_ge(state_ready, (PAIRS - 1) * h + p + 1)

            def outputs(h):
                f = first_of[h]
                dve.wait_ge(rstd_ready, h + 1)
                for p in range(PAIRS):
                    y = Y[:, p, h * DV:(h + 1) * DV]
                    ins = nc.vector.scalar_tensor_tensor(y, bank(f + 9 + p // 2)[:, (p % 2) * DV:(p % 2 + 1) * DV], rstd[:, p:p + 1], y,
                                                         ALU.mult, ALU.mult)
                    if p % 2:
                        ins.then_inc(by_dve, 1)

            dve.wait_ge(kept, 2)
            low(0)
            low(1)
            sums_of(0)
            for i in range(4):
                product(0, i)
            low(2)
            for h in range(GLA_HEADS):
                more = h + 1 < GLA_HEADS
                if more:
                    sums_of(h + 1)
                cross_pair(h)
                if more:
                    product(h + 1, 0)
                states(h)
                if more:
                    product(h + 1, 1)
                    product(h + 1, 2)
                if h + 2 < GLA_HEADS:
                    low(h + 3)
                outputs(h)
                if more:
                    product(h + 1, 3)

        @block.tensor
        def _(pe):
            def ring_wait(i):
                if i >= 4:
                    pe.wait_ge(*freed(i - 4))

            def project(s, part):
                pe.wait_ge(w_split, s + 1)
                if s == 1 and part == 0:
                    pe.wait_ge(rank_ready, 2)
                if s >= 2:
                    pe.wait_ge(copied, 2 * (s - 2) + part + 1)
                m = P if s == 0 else DK
                for d in range(DC):
                    for w, h, first, final in ((w_hi, hT_hi, d == 0, False), (w_hi, hT_lo, False, False), (w_lo, hT_hi, False, d == DC - 1)):
                        for half in range(2):
                            mm = nc.tensor.matmul(psum[0:m, 2 * part + half, :], w[:, d, part * DK:part * DK + m],
                                                  h[:, d, half * HALF:(half + 1) * HALF], start=first, stop=final)
                mm.then_inc(projected, 1)

            def gate(h):
                for half in range(2):
                    i = z_of[h] + half
                    ring_wait(i)
                    nc.tensor.matmul(bank(i)[0:DK, :], gate2[:, h * DK:(h + 1) * DK], rank[:, half * HALF:(half + 1) * HALF],
                                     start=True, stop=True).then_inc(z_ready, 1)

            def token_products(h):
                f = first_of[h]
                pe.wait_ge(timed, 4 * h + 2)
                for i in range(2):
                    ring_wait(f + i)
                    for c in range(4):
                        tok = slice((4 * i + c) * P, (4 * i + c + 1) * P)
                        mm = nc.tensor.matmul(bank(f + i)[:, c * P:(c + 1) * P], k_mid[:, tok], q_mid[:, tok], start=True, stop=True)
                    mm.then_inc(mixed, 1)
                ring_wait(f + 2)
                pe.wait_ge(timed, 4 * h + 4)
                for p in range(PAIRS):
                    mm = nc.tensor.matmul(bank(f + 2)[0:CHUNK, p * CHUNK:(p + 1) * CHUNK], k_out[:, p * P:p * P + CHUNK],
                                          q_in[:, p * P + CHUNK:(p + 1) * P], start=True, stop=True)
                mm.then_inc(mixed, 1)

            def state_changes(h):
                f = first_of[h]
                pe.wait_ge(factored, h + 1)
                for i in range(2):
                    ring_wait(f + 3 + i)
                    for c in range(4):
                        p = 4 * i + c
                        mm = nc.tensor.transpose(bank(f + 3 + i)[:, c * DK:(c + 1) * DK], k_out[:, p * P:(p + 1) * P], ident[0:DK, 0:DK])
                    mm.then_inc(mixed, 1)
                for p in range(PAIRS - 1):
                    i = f + 5 + p // 2
                    if p % 2 == 0:
                        ring_wait(i)
                    pe.wait_ge(by_act, freed(f + 3 + p // 4)[1])
                    mm = nc.tensor.matmul(bank(i)[0:DK, (p % 2) * DV:(p % 2 + 1) * DV], k_rows[:, p, :],
                                          V[:, p, h * DV:(h + 1) * DV], start=True, stop=True)
                    if p % 2 or p == PAIRS - 2:
                        mm.then_inc(mixed, 1)

            def outputs(h):
                f = first_of[h]
                pe.wait_ge(masked, h + 1)
                for p in range(PAIRS):
                    i = f + 9 + p // 2
                    if p % 2 == 0:
                        ring_wait(i)
                    out = bank(i)[:, (p % 2) * DV:(p % 2 + 1) * DV]
                    mm = nc.tensor.matmul(out, att[:, p, :], V[:, p, h * DV:(h + 1) * DV], start=True, stop=p == 0)
                    if p:
                        pe.wait_ge(state_ready, (PAIRS - 1) * h + p)
                        mm = nc.tensor.matmul(out, q_in[:, p * P:(p + 1) * P], state[:, p, :], start=False, stop=True)
                    if p % 2:
                        mm.then_inc(mixed, 1)

            project(0, 0)
            pe.wait_ge(rank_ready, 2)
            gate(0)
            project(1, 0)
            project(1, 1)
            for h in range(GLA_HEADS):
                more = h + 1 < GLA_HEADS
                if more:
                    gate(h + 1)
                token_products(h)
                if more:
                    project(h + 2, 0)
                state_changes(h)
                if more:
                    project(h + 2, 1)
                outputs(h)


def merge_phase(nc, ph, sources, lses, Y):
    G = len(sources)
    with ExitStack() as ctx:
        ctx.callback(nc.all_engine_barrier)
        def sb(name, shape):
            return ctx.enter_context(nc.sbuf_tensor(f"{ph}_{name}", shape, F32))

        def sem(name):
            return phase_semaphore(nc, ctx, f"{ph}_{name}")

        logs = sb("logs", [P, G, TT, DIL_HEADS])
        top, inv = sb("top", [P, TT, DIL_HEADS]), sb("inv", [P, TT, DIL_HEADS])
        outs = [sb(f"outs{i}", [P, G, D_DIL]) for i in range(2)]
        logs_loaded, link, expd = sem("logs_loaded"), sem("link"), sem("expd")
        loaded = [sem(f"loaded{i}") for i in range(2)]
        added = sem("added")
        block = ctx.enter_context(nc.Block())

        @block.sync
        def _(sp):
            for g in range(G):
                sp.dma_start(logs[:, g, :, :], lses[g].rearrange("(t p) h -> p t h", p=P)).then_inc(logs_loaded, 16)
            for t in range(TT):
                if t >= 2:
                    sp.wait_ge(added, t - 1)
                for g in range(G):
                    sp.dma_start(outs[t % 2][:, g, :], sources[g][t * P:(t + 1) * P, :]).then_inc(loaded[t % 2], 16)

        @block.scalar
        def _(act):
            act.wait_ge(link, 3)
            nc.scalar.activation(logs[:, :, :, :], logs[:, :, :, :], ACT.Exp).then_inc(expd, 1)

        @block.vector
        def _(dve):
            links = [0]

            def chain(ins):
                ins.then_inc(link, 1)
                links[0] += 1
                dve.wait_ge(link, links[0])

            dve.wait_ge(logs_loaded, 16 * G)
            chain(nc.vector.tensor_tensor(top[:, :, :], logs[:, 0, :, :], logs[:, 1, :, :], ALU.max))
            chain(nc.vector.tensor_tensor(top[:, :, :], top[:, :, :], logs[:, 2, :, :], ALU.max))
            for g in range(G):
                ins = nc.vector.tensor_tensor(logs[:, g, :, :], logs[:, g, :, :], top[:, :, :], ALU.subtract)
            chain(ins)
            dve.wait_ge(expd, 1)
            chain(nc.vector.tensor_tensor(inv[:, :, :], logs[:, 0, :, :], logs[:, 1, :, :], ALU.add))
            chain(nc.vector.tensor_tensor(inv[:, :, :], inv[:, :, :], logs[:, 2, :, :], ALU.add))
            chain(nc.vector.reciprocal(inv[:, :, :], inv[:, :, :]))
            for g in range(G):
                ins = nc.vector.tensor_tensor(logs[:, g, :, :], logs[:, g, :, :], inv[:, :, :], ALU.mult)
            chain(ins)
            for t in range(TT):
                dve.wait_ge(loaded[t % 2], 16 * G * (t // 2 + 1))
                for g in range(G):
                    for h in range(DIL_HEADS):
                        cols = slice(h * DIL_DIM, (h + 1) * DIL_DIM)
                        w, o = logs[:, g, t, h:h + 1], outs[t % 2][:, g, cols]
                        if g == 0:
                            ins = nc.vector.tensor_scalar(Y[:, t, cols], o, w, None, ALU.mult)
                        else:
                            ins = nc.vector.scalar_tensor_tensor(Y[:, t, cols], o, w, Y[:, t, cols], ALU.mult, ALU.add)
                    if g + 1 < G:
                        chain(ins)
                ins.then_inc(added, 1)
            dve.wait_ge(added, TT)


def rope_phase(nc, ph, neg_half, positions, inv_freq, cos, sin):
    HD = DIL_DIM // 2
    with ExitStack() as ctx:
        ctx.callback(nc.all_engine_barrier)
        def sb(name, shape, dt=F32):
            return ctx.enter_context(nc.sbuf_tensor(f"{ph}_{name}", shape, dt))

        def sem(name):
            return phase_semaphore(nc, ctx, f"{ph}_{name}")

        pos_i, pos = sb("pos_i", [P, TT], mybir.dt.int32), sb("pos", [P, TT])
        freq = sb("freq", [P, HD])
        turns = sb("turns", [P, TT, HD])
        angle = sb("angle", [P, TT, HD])
        loaded, link, reduced, sined = sem("loaded"), sem("link"), sem("reduced"), sem("sined")
        block = ctx.enter_context(nc.Block())

        @block.sync
        def _(sp):
            sp.dma_start(pos_i[:, :], positions[0, :].rearrange("(t p) -> p t", p=P), allow_slow_non_contiguous=True).then_inc(loaded, 16)
            sp.dma_start(freq[:, :], inv_freq.partition_broadcast(P)).then_inc(loaded, 16)

        @block.vector
        def _(dve):
            links = [0]

            def chain(ins):
                ins.then_inc(link, 1)
                links[0] += 1
                dve.wait_ge(link, links[0])

            two_pi = 2 * math.pi
            parts, left = [], two_pi
            for bits in (5, 13, 21):
                parts.append(math.floor(left * 2 ** bits) / 2 ** bits)
                left -= parts[-1]
            parts.append(left)
            ROUND = 1.5 * 2 ** 23
            dve.wait_ge(loaded, 32)
            chain(nc.vector.tensor_copy(pos[:, :], pos_i[:, :]))
            for shift, out in ((0.0, sin), (math.pi / 2, cos)):
                for t in range(TT):
                    ins = nc.vector.tensor_scalar(angle[:, t, :], freq[:, :], pos[:, t:t + 1], None, ALU.mult)
                chain(ins)
                chain(nc.vector.tensor_scalar(turns[:, :, :], angle[:, :, :], 1 / two_pi, shift / two_pi, ALU.mult, ALU.add))
                chain(nc.vector.tensor_scalar(turns[:, :, :], turns[:, :, :], ROUND, ROUND, ALU.add, ALU.subtract))
                for part in parts:
                    chain(nc.vector.scalar_tensor_tensor(angle[:, :, :], turns[:, :, :], -part, angle[:, :, :], ALU.mult, ALU.add))
                chain(nc.vector.tensor_scalar(angle[:, :, :], angle[:, :, :], shift, 3.1415925, ALU.add, ALU.min))
                nc.vector.tensor_scalar(out[:, :, :], angle[:, :, :], -3.1415925, None, ALU.max).then_inc(reduced, 1)
                dve.wait_ge(reduced, 1 if out is sin else 2)

        @block.scalar
        def _(act):
            for i, out in enumerate((sin, cos)):
                act.wait_ge(reduced, i + 1)
                nc.scalar.activation(out[:, :, :], out[:, :, :], ACT.Sin).then_inc(sined, 1)
            act.wait_ge(sined, 2)


APART_STEP = 8


def setup_phase(nc, psum, ident, neg_half, band, split, zeros, keys0, broadcasts):
    with ExitStack() as ctx:
        ctx.callback(nc.all_engine_barrier)
        done = phase_semaphore(nc, ctx, "setup_done")
        loaded = phase_semaphore(nc, ctx, "setup_loaded")
        parity = phase_semaphore(nc, ctx, "setup_parity")
        apart = ctx.enter_context(nc.sbuf_tensor("apart", [P, P], mybir.dt.int32))
        block = ctx.enter_context(nc.Block())

        @block.vector
        def _(dve):
            dve.wait_ge(done, APART_STEP)
            nc.vector.tensor_scalar(apart[:, :], apart[:, :], 1, None, ALU.bitwise_and).then_inc(parity, 1)
            dve.wait_ge(parity, 1)
            nc.vector.tensor_scalar(split[:, :], apart[:, :], NEG, None, ALU.mult).then_inc(parity, 1)

        @block.sync
        def _(sp):
            for out, row in broadcasts:
                sp.dma_start(out, row.partition_broadcast(P)).then_inc(loaded, 16)
            sp.wait_ge(loaded, 16 * len(broadcasts))

        @block.gpsimd
        def _(pool):
            steps = [0]

            def step(ins):
                ins.then_inc(done, 1)
                steps[0] += 1
                pool.wait_ge(done, steps[0])

            def select(x, op, fill, base, pattern, channel):
                step(nc.gpsimd.affine_select(out=x, in_=x, compare_op=op, fill=fill, base=base, pattern=pattern,
                                             channel_multiplier=channel))

            step(nc.gpsimd.memset(ident[:, :], 0.0))
            select(ident[:, :], ALU.not_equal, 1.0, 0, [[-1, P]], 1)
            step(nc.gpsimd.memset(neg_half[:, :], -0.5))
            step(nc.gpsimd.memset(zeros[:, :], 0.0))
            step(nc.gpsimd.memset(band[:, :], 0.0))
            select(band[:, :], ALU.is_ge, NEG, 0, [[1, 2 * P]], -1)
            select(band[:, :], ALU.is_ge, NEG, P, [[-1, 2 * P]], 1)
            step(nc.gpsimd.iota(apart[:, :], pattern=[[-1, P]], base=2 * P, channel_multiplier=1))
            pool.wait_ge(parity, 2)
            select(split[:, :], ALU.is_ge, NEG, 0, [[-1, P]], 1)
            for k in keys0:
                step(nc.gpsimd.memset(k, 0.0))


class Stage:

    def __init__(self, dilation, stage, out_dram, lse, lse_dram):
        self.dilation, self.stage, self.out, self.lse, self.lse_dram = dilation, stage, out_dram, lse, lse_dram
        self.parts = 1

    def rows(self, dram, t):
        r = min(self.dilation, SEQ // P)
        per = SEQ // r // P
        return dram.rearrange("(a r) c -> r a c", r=r)[t // per, (t % per) * P:(t % per + 1) * P, :]

    def __call__(self, sp, t, stored):
        sp.dma_start(self.rows(self.out, t), self.stage[t % 2][:, :]).then_inc(stored, 16)

    def store_lse(self, sp, stored):
        for t in range(TT):
            sp.dma_start(self.rows(self.lse_dram, t), self.lse[:, 4 * t:4 * t + 4]).then_inc(stored, 16)
        return TT


def save_phase(nc, ph, pairs):
    with ExitStack() as ctx:
        ctx.callback(nc.all_engine_barrier)
        saved = phase_semaphore(nc, ctx, f"{ph}_saved")
        block = ctx.enter_context(nc.Block())

        @block.sync
        def _(sp):
            for out, src in pairs:
                sp.dma_start(out, src).then_inc(saved, 16)
            sp.wait_ge(saved, 16 * len(pairs))


def build(nc, a, out):
    with ExitStack() as ctx:
        def sb(name, shape, dt=F32, c=ctx):
            return c.enter_context(nc.sbuf_tensor(name, shape, dt))

        psum = ctx.enter_context(nc.psum_tensor("psum", [P, BANKS, HALF], F32))
        ident, neg_half = sb("ident", [P, P]), sb("neg_half", [P, TT])
        band, split, zeros = sb("band", [P, 2 * P]), sb("split", [P, P]), sb("zeros", [P, 2 * P])
        xa_gain = [[sb(f"xa_{n}_gain{i}", [P, XA_DIM]) for n in "qk"] for i in range(2)]
        o_gain = sb("o_gain", [P, GLA_DV])
        dil_gain = [sb("dil_q_gain", [P, DIL_DIM]), sb("dil_k_gain", [P, DIL_DIM])]
        hT_hi, hT_lo = sb("hT_hi", [P, DC, SEQ], F32R), sb("hT_lo", [P, DC, SEQ], F32R)
        XY = sb("XY", [P, TT, D])

        def dram(name, shape):
            return nc.dram_tensor(name, shape, F32, kind="Internal").ap()

        x1, x2 = dram("x_mid", [SEQ, D]), dram("x_layer1", [SEQ, D])
        keys_d = [dram(f"mem_keys{i}", [P, XA_HEADS * N_MEM]) for i in range(2)]
        vals_d = [dram(f"mem_values{i}", [P, 2 * D_XA]) for i in range(2)]
        outs_d = [dram(f"group_out{g}", [SEQ, D_DIL]) for g in range(3)]
        lses_d = [dram(f"group_lse{g}", [SEQ, DIL_HEADS]) for g in range(3)]

        def plain(x, d, t):
            return x[:, d, t * P:(t + 1) * P]

        with ExitStack() as c:
            mem_hi, mem_lo = sb("mem_hi", [P, DC, N_MEM], F32R, c), sb("mem_lo", [P, DC, N_MEM], F32R, c)
            keys = [sb(f"keys{i}", [P, XA_HEADS, N_MEM], F32, c) for i in range(2)]
            vals = [sb(f"vals{i}", [P, 2, D_XA], F32, c) for i in range(2)]
            setup_phase(nc, psum, ident, neg_half, band, split, zeros, [k[:, :, :] for k in keys],
                        [(xa_gain[i][0][:, :], a["xa_q_norm"][i, :]) for i in range(2)]
                        + [(xa_gain[i][1][:, :], a["xa_k_norm"][i, :]) for i in range(2)]
                        + [(o_gain[:, :], a["a_o_norm"]), (dil_gain[0][:, :], a["b_q_norm"]), (dil_gain[1][:, :], a["b_k_norm"])])
            norm_phase(nc, "mem", psum, ident, neg_half, a["mem"][0, :, :], N_MEM // P, a["mem_norm"], mem_hi, mem_lo)

            def key_dest(i):
                def dest(t, src):
                    s = src.rearrange("p (a n) -> p a n", n=P)
                    tok = slice(t * P, (t + 1) * P)
                    return [(keys[i][0:64, 0:XA_HEADS:2, tok], s[0:64, :, :]), (keys[i][64:P, 1:XA_HEADS:2, tok], s[64:P, :, :])]
                return dest

            blocks = []
            for i in range(2):
                w = a["xa_w_kv"][i, :, :]
                blocks += [dict(kind="heads", dim=XA_DIM, gain=xa_gain[i][1][:, :], w=w[:, 0:D_XA], pick=plain, dest=key_dest(i)),
                           dict(kind="copy", w=w[:, D_XA:2 * D_XA], pick=plain, dest=lambda t, i=i: vals[i][:, t, :])]
            project_phase(nc, "kv", psum, ident, neg_half, N_MEM // P, mem_hi, mem_lo, blocks)
            save_phase(nc, "kv", [(keys_d[i], keys[i][:, :, :].rearrange("p h n -> p (h n)")) for i in range(2)]
                       + [(vals_d[i], vals[i][:, :, :].rearrange("p h n -> p (h n)")) for i in range(2)])

        def xa_dest(xqT):
            def dest(t, src):
                return [(xqT[:, :, t * P:(t + 1) * P], src.rearrange("p (a n) -> p a n", n=P))]
            return dest

        def xa_units(xqT, keys, vals, base):
            return [(xqT[:, h // 2, t * P:(t + 1) * P], keys[:, h, :], N_MEM, zeros[:, :],
                     [vals[:, c, h * XA_DIM:(h + 1) * XA_DIM] for c in range(2)],
                     XY[:, t, base + h * XA_DIM:base + (h + 1) * XA_DIM]) for t in range(TT) for h in range(XA_HEADS)]

        norm_phase(nc, "n0", psum, ident, neg_half, a["x"][0, :, :], TT, a["mix_norm"][0, :], hT_hi, hT_lo)
        with ExitStack() as c:
            xqT = sb("xqT0", [P, 2, SEQ], F32, c)
            with ExitStack() as c2:
                V = sb("gla_v", [P, TT, D_MIX], F32, c2)
                w = a["a_w_in"]
                v0 = 2 * GLA_HEADS * GLA_DK
                g0 = v0 + D_MIX + GLA_RANK
                B = 2 * GLA_DV
                blocks = [dict(kind="copy", w=w[:, v0 + i * B:v0 + (i + 1) * B], pick=plain,
                               dest=lambda t, i=i: V[:, t, i * B:(i + 1) * B]) for i in range(2)]
                blocks += [dict(kind="gate", w=w[:, g0 + i * B:g0 + (i + 1) * B], pick=plain, gain=o_gain[:, :],
                                dest=lambda t, i=i: XY[:, t, i * B:(i + 1) * B]) for i in range(2)]
                blocks += [dict(kind="heads", dim=XA_DIM, gain=xa_gain[0][0][:, :], w=w[:, g0 + D_MIX:g0 + D_MIX + D_XA],
                                pick=plain, dest=xa_dest(xqT))]
                project_phase(nc, "p0", psum, ident, neg_half, TT, hT_hi, hT_lo, blocks)
                gla_phase(nc, "gla", psum, ident, neg_half, hT_hi, hT_lo, w, a["a_w_gate2"], a["a_b_gate"], V, XY)
            xa_phase(nc, "xa0", psum, ident, c, keys_d[0], vals_d[0], lambda k, v: xa_units(xqT, k, v, D_MIX))
        out_phase(nc, "o0", psum, ident, neg_half, XY, DC, a["a_w_out"], a["x"][0, :, :], a["ffn_norm"][0, :], hT_hi, hT_lo)
        ffn_phase(nc, "f0", psum, ident, XY, hT_hi, hT_lo, a["ffn_w_up"][0, :, :], a["ffn_conv_w"][0, :, :], a["ffn_conv_b"][0, :],
                  a["ffn_w_down"][0, :, :], x2)

        norm_phase(nc, "n1", psum, ident, neg_half, x2, TT, a["mix_norm"][1, :], hT_hi, hT_lo)
        with ExitStack() as c:
            cos, sin = sb("cos", [P, TT, DIL_DIM // 2], F32, c), sb("sin", [P, TT, DIL_DIM // 2], F32, c)
            rope_phase(nc, "rope", neg_half, a["positions"], a["inv_freq"], cos, sin)
            qT, kT = (sb(f"dil_{n}T", [P, DIL_HEADS, SEQ], F32, c) for n in "qk")
            V = XY[:, :, 0:D_DIL]
            w = a["b_w_in"]
            cols = 3 * D_DIL

            def head_dest(x):
                return lambda t, src: [(x[:, :, t * P:(t + 1) * P], src.rearrange("p (h n) -> p h n", n=P))]

            for g, r in enumerate(DILATIONS):
                def tokens(x, t, r=r):
                    r = min(r, SEQ // P)
                    v = x.rearrange("p (a r) -> p r a", r=r)
                    per = SEQ // r // P
                    return v[:, t // per, (t % per) * P:(t % per + 1) * P]

                def keys_of(x, t, r=r):
                    per = max(1, SEQ // r // P)
                    if r == 16 or t % per == 0:
                        return tokens(x, t), P, t
                    v = x.rearrange("p (a r) -> p r a", r=r)
                    b = t % per
                    return v[:, t // per, (b - 1) * P:(b + 1) * P], 2 * P, t - 1

                off = g * D_DIL
                blocks = [dict(kind="heads", dim=DIL_DIM, gain=dil_gain[i][:, :], rope=(cos, sin), w=w[:, i * cols + off:i * cols + off + D_DIL],
                               pick=plain, dest=head_dest(x)) for i, x in enumerate((qT, kT))]
                blocks += [dict(kind="copy", w=w[:, 2 * cols + off:2 * cols + off + D_DIL], pick=lambda x, d, t: tokens(x[:, d, :], t),
                                dest=lambda t: V[:, t, :])]
                project_phase(nc, f"p1_{g}", psum, ident, neg_half, TT, hT_hi, hT_lo, blocks)
                with ExitStack() as c2:
                    stage = [sb(f"stage{g}_{i}", [P, D_DIL], F32, c2) for i in range(2)]
                    lse = sb(f"lse{g}", [P, TT * DIL_HEADS], F32, c2)
                    units = []
                    for t in range(TT):
                        for h in range(DIL_HEADS):
                            k, n, first = keys_of(kT[:, h, :], t)
                            mask = split[:, :] if r == 16 else band[:, 2 * P - n:2 * P]
                            units.append((tokens(qT[:, h, :], t), k, n, mask,
                                          [V[:, first + i, h * P:(h + 1) * P] for i in range(n // P)],
                                          stage[t % 2][:, h * P:(h + 1) * P]))
                    attention_phase(nc, f"da{g}", psum, ident, float(DIL_DIM) ** -0.5, units,
                                    Stage(r, stage, outs_d[g], lse, lses_d[g]), lse)
        with ExitStack() as c:
            xqT = sb("xqT1", [P, 2, SEQ], F32, c)
            project_phase(nc, "p1_x", psum, ident, neg_half, TT, hT_hi, hT_lo,
                          [dict(kind="heads", dim=XA_DIM, gain=xa_gain[1][0][:, :], w=w[:, 3 * cols:3 * cols + D_XA], pick=plain, dest=xa_dest(xqT))])
            xa_phase(nc, "xa1", psum, ident, c, keys_d[1], vals_d[1], lambda k, v: xa_units(xqT, k, v, D_DIL))
        merge_phase(nc, "merge", outs_d, lses_d, XY)
        out_phase(nc, "o1", psum, ident, neg_half, XY, (D_DIL + D_XA) // P, a["b_w_out"], x2, a["ffn_norm"][1, :], hT_hi, hT_lo)
        ffn_phase(nc, "f1", psum, ident, XY, hT_hi, hT_lo, a["ffn_w_up"][1, :, :], a["ffn_conv_w"][1, :, :], a["ffn_conv_b"][1, :],
                  a["ffn_w_down"][1, :, :], out)


def xa_phase(nc, ph, psum, ident, ctx, keys_d, vals_d, units):
    keys = ctx.enter_context(nc.sbuf_tensor(f"{ph}_keys", [P, XA_HEADS, N_MEM], F32))
    vals = ctx.enter_context(nc.sbuf_tensor(f"{ph}_vals", [P, 2, D_XA], F32))
    save_phase(nc, ph, [(keys[:, :, :].rearrange("p h n -> p (h n)"), keys_d), (vals[:, :, :].rearrange("p h n -> p (h n)"), vals_d)])
    attention_phase(nc, ph, psum, ident, float(XA_DIM) ** -0.5, units(keys, vals))


_INS = ["x", "mem", "positions", "mem_norm", "mix_norm", "xa_w_kv", "xa_q_norm", "xa_k_norm", "ffn_norm", "ffn_w_up",
        "ffn_conv_w", "ffn_conv_b", "ffn_w_down", "a_w_in", "a_w_gate2", "a_b_gate", "a_o_norm", "a_w_out",
        "b_w_in", "b_q_norm", "b_k_norm", "b_w_out"]


def kernel(**inputs):
    import numpy as _np
    import concourse.bacc as _bacc
    from concourse import mybir as _mybir
    from concourse.bass_utils import run_bass_kernel_spmd as _run

    nc = _bacc.Bacc("TRN2", target_bir_lowering=False, num_devices=1)
    half = DIL_DIM // 2
    arrays, aps = {}, {}
    given = {name: _np.ascontiguousarray(inputs[name]) for name in _INS}
    given["inv_freq"] = _np.float32(10000.0) ** (-_np.arange(half, dtype=_np.float32) / _np.float32(half))
    for name, x in given.items():
        arrays[f"in_{name}_dram"] = x
        aps[name] = nc.dram_tensor(f"in_{name}_dram", x.shape, _mybir.dt.from_np(x.dtype), kind="ExternalInput").ap()
    out = nc.dram_tensor("out_0_dram", (1, SEQ, D), F32, kind="ExternalOutput").ap()
    build(nc, aps, out[0, :, :])
    r = _run(nc, [arrays], core_ids=[0])
    return r.results[0]["out_0_dram"]
```

```python
import concourse.bass as bass
from concourse import mybir
from concourse.alu_op_type import AluOpType as ALU
import math
from contextlib import ExitStack

F32 = mybir.dt.float32
F32R = mybir.dt.float32r
ACT = mybir.ActivationFunctionType
AX = mybir.AxisListType

P = 128
D = 1024
SEQ = 1024
DC = D // P
TT = SEQ // P
HALF = 512
FF = 2816
FC = FF // P
GROUPS = FC // 2
BANKS = 8


def phase_semaphore(nc, ctx, name):
    s = ctx.enter_context(nc.semaphore(name))
    ctx.callback(nc.gpsimd.sem_clear, s)
    return s


def split_matmul(nc, out, lhs_hi, lhs_lo, rhs_hi, rhs_lo, start, stop):
    nc.tensor.matmul(out, lhs_hi, rhs_hi, start=start, stop=False)
    nc.tensor.matmul(out, lhs_hi, rhs_lo, start=False, stop=False)
    return nc.tensor.matmul(out, lhs_lo, rhs_hi, start=False, stop=stop)


def ffn_phase(nc, ph, psum, ident, X, hT_hi, hT_lo, w_up, conv_w, conv_b, w_down, x_out):
    with ExitStack() as ctx:
        ctx.callback(nc.all_engine_barrier)
        def sb(name, shape, dt=F32):
            return ctx.enter_context(nc.sbuf_tensor(f"{ph}_{name}", shape, dt))

        def sem(name):
            return phase_semaphore(nc, ctx, f"{ph}_{name}")

        up_raw = [sb(f"up_raw{j}", [P, DC, P]) for j in range(2)]
        up_hi = [sb(f"up_hi{j}", [P, DC, P], F32R) for j in range(2)]
        up_lo = [sb(f"up_lo{j}", [P, DC, P], F32R) for j in range(2)]
        down_raw = sb("down_raw", [P, 2, D])
        down_hi = sb("down_hi", [P, 2, D], F32R)
        down_lo = sb("down_lo", [P, 2, D], F32R)
        act_hi = [sb(f"act_hi{j}", [P, 2, SEQ], F32R) for j in range(2)]
        act_lo = [sb(f"act_lo{j}", [P, 2, SEQ], F32R) for j in range(2)]
        conv_out = [sb("conv_gate", [P, SEQ]), sb("conv_value", [P, SEQ])]
        taps_rows = sb("taps_rows", [2 * FC, 4, P])
        taps = sb("taps", [P, 4, 2 * FC])

        up_loaded = [sem("up_loaded_gate"), sem("up_loaded_value")]
        down_loaded = sem("down_loaded")
        taps_loaded = sem("taps_loaded")
        taps_turned = sem("taps_turned")
        taps_ready = sem("taps_ready")
        up_high = sem("up_high")
        up_split = sem("up_split")
        down_high = sem("down_high")
        down_split = sem("down_split")
        up_done = sem("up_done")
        conv_started = sem("conv_started")
        conv_tap = sem("conv_tap")
        conv_done = sem("conv_done")
        gate_done = sem("gate_done")
        prod_done = sem("prod_done")
        act_high = sem("act_high")
        act_split = sem("act_split")
        down_done = sem("down_done")
        x_added = sem("x_added")
        stored = sem("stored")

        up_view = w_up.rearrange("(d p) c -> p d c", p=P)
        down_view = w_down.rearrange("(f p) n -> p f n", p=P)
        ups = [psum[:, 2 * j:2 * j + 2, :].rearrange("p b n -> p (b n)") for j in range(2)]

        def over_groups(eng, group):
            group(0, 0)
            group(1, 1)
            with eng.Fori(0, (GROUPS - 3) // 2) as it:
                group(it * 2 + 2, 0)
                group(it * 2 + 3, 1)
            group(GROUPS - 1, 0, last=True)

        def is_first(g):
            return isinstance(g, int) and g == 0

        block = ctx.enter_context(nc.Block())

        @block.sync
        def _(sp):
            def group(g, par, last=False):
                for c in range(2):
                    for j in range(2):
                        n = g * 4 + 2 * c + j
                        if not is_first(g) or c:
                            sp.wait_ge(up_split, n - 1)
                        sp.dma_start(up_raw[j][:, :, :],
                                     up_view[:, :, bass.ds(g * 2 * P + (j * FC + c) * P, P)]).then_inc(up_loaded[j], 16)
                if not is_first(g):
                    sp.wait_ge(down_split, g)
                sp.dma_start(down_raw[:, :, :], down_view[:, bass.ds(g * 2, 2), :]).then_inc(down_loaded, 16)

            over_groups(sp, group)
            for t in range(TT):
                sp.wait_ge(x_added, 2 * TT * (GROUPS - 1) + 2 * t + 2)
                sp.dma_start(x_out[t * P:(t + 1) * P, :], X[:, t, :]).then_inc(stored, 16)
            sp.wait_ge(stored, 16 * TT)

        @block.scalar
        def _(act):
            def high_up(n_slot, n):
                act.wait_ge(up_loaded[n_slot], n * 8 + (16 - 8 * n_slot))
                nc.scalar.activation(up_hi[n_slot][:, :, :], up_raw[n_slot][:, :, :], ACT.Copy).then_inc(up_high, 1)

            def high_down(g):
                act.wait_ge(down_loaded, g * 16 + 16)
                if not is_first(g):
                    act.wait_ge(down_done, g * (2 * TT))
                nc.scalar.activation(down_hi[:, :, :], down_raw[:, :, :], ACT.Copy).then_inc(down_high, 1)

            for k in range(3):
                act.dma_start(taps_rows[:, k, :], conv_w[k, :].rearrange("(c p) -> c p", p=P)).then_inc(taps_loaded, 16)
            act.dma_start(taps_rows[:, 3, :], conv_b.rearrange("(c p) -> c p", p=P)).then_inc(taps_loaded, 16)
            high_up(0, 0)
            high_up(1, 1)
            act.wait_ge(taps_ready, 1)

            def group(g, par, last=False):
                if not is_first(g):
                    high_down(g - 1)
                for c in range(2):
                    for j in range(2):
                        n = g * 4 + 2 * c + j
                        act.wait_ge(up_done, n + 1)
                        if not (last and c):
                            high_up(j, n + 2)
                        if not is_first(g) or c:
                            act.wait_ge(act_split, g * 2 + c)
                        f = g * 2 + (c + j * FC)
                        nc.scalar.activation(conv_out[j][:, :], ups[j], ACT.Identity,
                                             bias=taps[:, 3, bass.ds(f, 1)], scale=taps[:, 2, bass.ds(f, 1)]
                                             ).then_inc(conv_started, 1)
                        if j == 1:
                            act.wait_ge(conv_done, n)
                            nc.scalar.activation(conv_out[0][:, :], conv_out[0][:, :], ACT.Silu).then_inc(gate_done, 1)
                            act.wait_ge(prod_done, g * 2 + (c + 1))
                            if not is_first(g) and not (isinstance(g, int) and g == 1):
                                act.wait_ge(down_done, g * (2 * TT) - 2 * TT)
                            nc.scalar.activation(act_hi[par][:, c, :], conv_out[0][:, :], ACT.Copy).then_inc(act_high, 1)

            over_groups(act, group)
            high_down(GROUPS - 1)

        @block.vector
        def _(dve):
            def low_up(n_slot, n):
                dve.wait_ge(up_high, n + 1)
                nc.vector.tensor_tensor(up_lo[n_slot][:, :, :], up_raw[n_slot][:, :, :],
                                        up_hi[n_slot][:, :, :].bitcast(F32), ALU.subtract).then_inc(up_split, 1)

            def low_down(g):
                dve.wait_ge(down_high, g + 1)
                nc.vector.tensor_tensor(down_lo[:, :, :], down_raw[:, :, :], down_hi[:, :, :].bitcast(F32),
                                        ALU.subtract).then_inc(down_split, 1)

            def add_group(g, banks):
                for i in banks:
                    dve.wait_ge(down_done, g * (2 * TT) + i + 1)
                    xs = X[:, i // 2, (i % 2) * HALF:(i % 2 + 1) * HALF]
                    nc.vector.tensor_tensor(xs, xs, psum[:, 4 + i % 4, :], ALU.add).then_inc(x_added, 1)

            low_up(0, 0)
            low_up(1, 1)
            dve.wait_ge(taps_turned, 1)
            nc.vector.tensor_copy(taps[:, :, :], psum[:, 4, 0:8 * FC].rearrange("p (k f) -> p k f", k=4)).then_inc(taps_ready, 1)
            dve.wait_ge(taps_ready, 1)

            def group(g, par, last=False):
                if not is_first(g):
                    low_down(g - 1)
                for c in range(2):
                    for j in range(2):
                        n = g * 4 + 2 * c + j
                        if not (last and c):
                            low_up(j, n + 2)
                        f = g * 2 + (c + j * FC)
                        y = conv_out[j]
                        dve.wait_ge(conv_started, n + 1)
                        nc.vector.scalar_tensor_tensor(y[:, 1:SEQ], ups[j][:, 0:SEQ - 1], taps[:, 1, bass.ds(f, 1)],
                                                       y[:, 1:SEQ], ALU.mult, ALU.add).then_inc(conv_tap, 1)
                        dve.wait_ge(conv_tap, n + 1)
                        nc.vector.scalar_tensor_tensor(y[:, 2:SEQ], ups[j][:, 0:SEQ - 2], taps[:, 0, bass.ds(f, 1)],
                                                       y[:, 2:SEQ], ALU.mult, ALU.add).then_inc(conv_done, 1)
                    if c and not is_first(g):
                        add_group(g - 1, range(0, 4))
                    dve.wait_ge(conv_done, g * 4 + 2 * c + 2)
                    dve.wait_ge(gate_done, g * 2 + (c + 1))
                    nc.vector.tensor_tensor(conv_out[0][:, :], conv_out[0][:, :], conv_out[1][:, :],
                                            ALU.mult).then_inc(prod_done, 1)
                    if c and not is_first(g):
                        add_group(g - 1, range(4, 8))
                    dve.wait_ge(prod_done, g * 2 + (c + 1))
                    dve.wait_ge(act_high, g * 2 + (c + 1))
                    nc.vector.tensor_tensor(act_lo[par][:, c, :], conv_out[0][:, :],
                                            act_hi[par][:, c, :].bitcast(F32), ALU.subtract).then_inc(act_split, 1)
                if not is_first(g):
                    add_group(g - 1, range(8, 2 * TT))

            over_groups(dve, group)
            low_down(GROUPS - 1)
            add_group(GROUPS - 1, range(2 * TT))

        @block.tensor
        def _(pe):
            def turn_taps():
                pe.wait_ge(taps_loaded, 64)
                for k in range(4):
                    turn = nc.tensor.transpose(psum[:, 4, k * 2 * FC:(k + 1) * 2 * FC], taps_rows[:, k, :],
                                               ident[0:2 * FC, 0:2 * FC])
                turn.then_inc(taps_turned, 1)

            def down_group(g, par):
                pe.wait_ge(act_split, g * 2 + 2)
                pe.wait_ge(down_split, g + 1)
                for i in range(2 * TT):
                    t, half = i // 2, i % 2
                    if not is_first(g) or i >= 4:
                        pe.wait_ge(x_added, g * (2 * TT) + (i - 3))
                    for c in range(2):
                        tok = slice(t * P, (t + 1) * P)
                        cols = slice(half * HALF, (half + 1) * HALF)
                        last = split_matmul(nc, psum[:, 4 + i % 4, :], act_hi[par][:, c, tok], act_lo[par][:, c, tok],
                                            down_hi[:, c, cols], down_lo[:, c, cols], c == 0, c == 1)
                    last.then_inc(down_done, 1)

            def group(g, par, last=False):
                for c in range(2):
                    for j in range(2):
                        n = g * 4 + 2 * c + j
                        pe.wait_ge(up_split, n + 1)
                        if not is_first(g) or c:
                            pe.wait_ge(conv_done, n - 1)
                        for d in range(DC):
                            for w, h, first, final in ((up_hi, hT_hi, d == 0, False), (up_hi, hT_lo, False, False),
                                                       (up_lo, hT_hi, False, d == DC - 1)):
                                for half in range(2):
                                    mm = nc.tensor.matmul(psum[:, 2 * j + half, :], w[j][:, d, :],
                                                          h[:, d, half * HALF:(half + 1) * HALF],
                                                          start=first, stop=final)
                        mm.then_inc(up_done, 1)
                        if is_first(g) and c == 0 and j == 0:
                            turn_taps()
                if isinstance(g, int) and g == 1:
                    pe.wait_ge(taps_ready, 1)
                if not is_first(g):
                    down_group(g - 1, 1 - par)

            over_groups(pe, group)
            down_group(GROUPS - 1, (GROUPS - 1) % 2)


EPS = 1e-6
N_MEM = 256
XA_HEADS, XA_DIM = 4, 64
D_XA = XA_HEADS * XA_DIM
D_MIX = 768
GLA_HEADS, GLA_DK, GLA_DV, GLA_RANK = 4, 96, 192, 16
CHUNK = 64
DIL_DIM, DIL_HEADS = 128, 4
D_DIL = DIL_DIM * DIL_HEADS
DILATIONS = (1, 4, 16)
NEG = -1e30


class Norm:

    def __init__(self, nc, ctx, ph, psum, bank0, ident, gain_t, neg_half, out_hi, out_lo):
        self.nc, self.psum, self.bank0, self.ident = nc, psum, bank0, ident
        self.gain_t, self.neg_half, self.hi, self.lo = gain_t, neg_half, out_hi, out_lo

        def sb(name, shape):
            return ctx.enter_context(nc.sbuf_tensor(f"{ph}_{name}", shape, F32))

        def sem(name):
            return phase_semaphore(nc, ctx, f"{ph}_{name}")

        self.scaled_rows = [sb(f"scaled_rows{i}", [P, D]) for i in range(2)]
        self.gained_cols = [sb(f"gained_cols{i}", [P, DC, P]) for i in range(1)]
        self.sums = sb("norm_sums", [P, TT])
        self.rstd = sb("norm_rstd", [P, TT])
        self.squared = sem("squared")
        self.mean = sem("mean")
        self.rstd_ready = sem("rstd_ready")
        self.scaled = sem("scaled")
        self.turned = sem("turned")
        self.gained = sem("gained")
        self.high = sem("norm_high")
        self.low = sem("norm_low")

    def act_scale(self, act, t, rows):
        nc, buf = self.nc, self.scaled_rows[t % 2]
        if t >= 2:
            act.wait_ge(self.turned, t - 1)
        nc.scalar.activation(buf[:, :], rows, ACT.Square, accum_out=self.sums[:, t:t + 1]).then_inc(self.squared, 1)
        act.wait_ge(self.rstd_ready, t + 1)
        nc.scalar.activation(buf[:, :], rows, ACT.Copy, scale=self.rstd[:, t:t + 1]).then_inc(self.scaled, 1)

    def pool(self, pool, t):
        nc, s, r = self.nc, self.sums[:, t:t + 1], self.rstd[:, t:t + 1]
        pool.wait_ge(self.squared, t + 1)
        nc.gpsimd.tensor_scalar(s, s, 1.0 / D, EPS, ALU.mult, ALU.add).then_inc(self.mean, 1)
        pool.wait_ge(self.mean, t + 1)
        nc.gpsimd.tensor_tensor(r, s, self.neg_half[:, 0:1], ALU.pow).then_inc(self.rstd_ready, 1)

    def pe(self, pe, t):
        pe.wait_ge(self.scaled, t + 1)
        if t >= 2:
            pe.wait_ge(self.gained, t - 1)
        for d in range(DC):
            turn = self.nc.tensor.transpose(self.psum[:, self.bank0 + 2 * (t % 2) + d // 4, (d % 4) * P:(d % 4 + 1) * P],
                                            self.scaled_rows[t % 2][:, d * P:(d + 1) * P], self.ident[:, :])
        turn.then_inc(self.turned, 1)

    def dve_gain(self, dve, t):
        dve.wait_ge(self.turned, t + 1)
        if t >= 1:
            dve.wait_ge(self.low, t)
        b = self.bank0 + 2 * (t % 2)
        self.nc.vector.tensor_tensor(self.gained_cols[0][:, :, :],
                                     self.psum[:, b:b + 2, :].rearrange("p b (d n) -> p (b d) n", d=4),
                                     self.gain_t[:, :].unsqueeze(2).broadcast_to([P, DC, P]), ALU.mult).then_inc(self.gained, 1)

    def act_high(self, act, t):
        act.wait_ge(self.gained, t + 1)
        self.nc.scalar.activation(self.hi[:, :, t * P:(t + 1) * P], self.gained_cols[0][:, :, :], ACT.Copy).then_inc(self.high, 1)

    def dve_low(self, dve, t):
        dve.wait_ge(self.high, t + 1)
        self.nc.vector.tensor_tensor(self.lo[:, :, t * P:(t + 1) * P], self.gained_cols[0][:, :, :],
                                     self.hi[:, :, t * P:(t + 1) * P].bitcast(F32), ALU.subtract).then_inc(self.low, 1)


def norm_phase(nc, ph, psum, ident, neg_half, rows_dram, tiles, gain, out_hi, out_lo):
    with ExitStack() as ctx:
        ctx.callback(nc.all_engine_barrier)
        rows = [ctx.enter_context(nc.sbuf_tensor(f"{ph}_rows{i}", [P, D], F32)) for i in range(2)]
        gain_t = ctx.enter_context(nc.sbuf_tensor(f"{ph}_gain", [P, DC], F32))
        loaded = [phase_semaphore(nc, ctx, f"{ph}_loaded{i}") for i in range(2)]
        gain_loaded = phase_semaphore(nc, ctx, f"{ph}_gain_loaded")
        norm = Norm(nc, ctx, ph, psum, 0, ident, gain_t, neg_half, out_hi, out_lo)
        block = ctx.enter_context(nc.Block())

        @block.sync
        def _(sp):
            for t in range(tiles):
                if t >= 2:
                    sp.wait_ge(norm.scaled, t - 1)
                sp.dma_start(rows[t % 2][:, :], rows_dram[t * P:(t + 1) * P, :]).then_inc(loaded[t % 2], 16)

        @block.scalar
        def _(act):
            act.dma_start(gain_t[:, :], gain.rearrange("(d p) -> p d", p=P), allow_slow_non_contiguous=True).then_inc(gain_loaded, 16)
            for t in range(tiles):
                act.wait_ge(loaded[t % 2], 16 * (t // 2 + 1))
                norm.act_scale(act, t, rows[t % 2][:, :])
                if t >= 1:
                    norm.act_high(act, t - 1)
            norm.act_high(act, tiles - 1)

        @block.gpsimd
        def _(pool):
            for t in range(tiles):
                norm.pool(pool, t)

        @block.tensor
        def _(pe):
            for t in range(tiles):
                norm.pe(pe, t)

        @block.vector
        def _(dve):
            dve.wait_ge(gain_loaded, 16)
            for t in range(tiles):
                norm.dve_gain(dve, t)
                norm.dve_low(dve, t)


def out_phase(nc, ph, psum, ident, neg_half, XY, chunks, w_out, x_dram, gain, out_hi, out_lo, stage=None):
    with ExitStack() as ctx:
        ctx.callback(nc.all_engine_barrier)
        def sb(name, shape, dt=F32):
            return ctx.enter_context(nc.sbuf_tensor(f"{ph}_{name}", shape, dt))

        def sem(name):
            return phase_semaphore(nc, ctx, f"{ph}_{name}")

        w_raw = [sb(f"w_raw{i}", [P, D]) for i in range(2)]
        w_hi = sb("w_hi", [P, chunks, D], F32R)
        w_lo = sb("w_lo", [P, chunks, D], F32R)
        y_hi = sb("y_hi", [P, chunks, P], F32R)
        y_lo = sb("y_lo", [P, chunks, P], F32R)
        x_old = sb("x_old", [P, D])
        gain_t = sb("gain", [P, DC])
        w_loaded = [sem(f"w_loaded{i}") for i in range(2)]
        gain_loaded = sem("gain_loaded")
        x_loaded = sem("x_loaded")
        w_high, w_split = sem("w_high"), sem("w_split")
        y_turned = sem("y_turned")
        y_high, y_split = sem("y_high"), sem("y_split")
        summed = sem("summed")
        x_ready = sem("x_ready")
        norm = Norm(nc, ctx, ph, psum, 4, ident, gain_t, neg_half, out_hi, out_lo)
        merge = Merge(nc, ctx, ph, stage, XY) if stage is not None else None
        block = ctx.enter_context(nc.Block())

        @block.sync
        def _(sp):
            if merge:
                stage.wait_all(sp)
                merge.load_logs(sp)
                merge.load(sp, 0)
            for k in range(chunks):
                if merge and k == 2:
                    merge.load(sp, 1)
                if k >= 2:
                    sp.wait_ge(w_split, k - 1)
                sp.dma_start(w_raw[k % 2][:, :], w_out[k * P:(k + 1) * P, :]).then_inc(w_loaded[k % 2], 16)
            for t in range(TT):
                if merge and t + 2 < TT:
                    merge.load(sp, t + 2)
                if t >= 1:
                    sp.wait_ge(x_ready, 2 * t)
                sp.dma_start(x_old[:, :], x_dram[t * P:(t + 1) * P, :]).then_inc(x_loaded, 16)

        def y_cols(t):
            b = 2 * (t % 2)
            return psum[:, b:b + 2, :].rearrange("p b (d n) -> p (b d) n", d=4)[:, 0:chunks, :]

        @block.scalar
        def _(act):
            act.dma_start(gain_t[:, :], gain.rearrange("(d p) -> p d", p=P), allow_slow_non_contiguous=True).then_inc(gain_loaded, 16)

            def y_part(t):
                act.wait_ge(y_turned, t + 1)
                if t >= 1:
                    act.wait_ge(summed, 2 * t)
                nc.scalar.activation(y_hi[:, :, :], y_cols(t), ACT.Copy).then_inc(y_high, 1)

            if merge:
                merge.act_exp(act)
            for k in range(chunks):
                act.wait_ge(w_loaded[k % 2], 16 * (k // 2 + 1))
                nc.scalar.activation(w_hi[:, k, :], w_raw[k % 2][:, :], ACT.Copy).then_inc(w_high, 1)
                if k == 0:
                    y_part(0)
            for t in range(TT):
                if t + 1 < TT:
                    y_part(t + 1)
                act.wait_ge(x_ready, 2 * t + 2)
                norm.act_scale(act, t, XY[:, t, :])
                if t >= 1:
                    norm.act_high(act, t - 1)
            norm.act_high(act, TT - 1)

        @block.gpsimd
        def _(pool):
            for t in range(TT):
                norm.pool(pool, t)

        @block.vector
        def _(dve):
            dve.wait_ge(gain_loaded, 16)

            def y_part(t):
                dve.wait_ge(y_high, t + 1)
                nc.vector.tensor_tensor(y_lo[:, :, :], y_cols(t), y_hi[:, :, :].bitcast(F32), ALU.subtract).then_inc(y_split, 1)

            if merge:
                merge.dve_weights(dve)
                merge.dve_add(dve, 0)
            for k in range(chunks):
                dve.wait_ge(w_high, k + 1)
                nc.vector.tensor_tensor(w_lo[:, k, :], w_raw[k % 2][:, :], w_hi[:, k, :].bitcast(F32), ALU.subtract).then_inc(w_split, 1)
                if k == 0:
                    y_part(0)
                    if merge:
                        merge.dve_add(dve, 1)
            for t in range(TT):
                if merge and t + 2 < TT:
                    merge.dve_add(dve, t + 2)
                dve.wait_ge(x_loaded, 16 * (t + 1))
                for half in range(2):
                    cols = slice(half * HALF, (half + 1) * HALF)
                    dve.wait_ge(summed, 2 * t + half + 1)
                    nc.vector.tensor_tensor(XY[:, t, cols], psum[:, 2 * (t % 2) + half, :], x_old[:, cols], ALU.add).then_inc(x_ready, 1)
                if t + 1 < TT:
                    y_part(t + 1)
                if t >= 1:
                    norm.dve_gain(dve, t - 1)
                    norm.dve_low(dve, t - 1)
            norm.dve_gain(dve, TT - 1)
            norm.dve_low(dve, TT - 1)

        @block.tensor
        def _(pe):
            def y_turn(t):
                if merge:
                    pe.wait_ge(merge.added, t + 1)
                if t >= 2:
                    pe.wait_ge(x_ready, 2 * t - 2)
                for k in range(chunks):
                    turn = nc.tensor.transpose(psum[:, 2 * (t % 2) + k // 4, (k % 4) * P:(k % 4 + 1) * P],
                                               XY[:, t, k * P:(k + 1) * P], ident[:, :])
                turn.then_inc(y_turned, 1)

            y_turn(0)
            for t in range(TT):
                if t + 1 < TT:
                    y_turn(t + 1)
                pe.wait_ge(y_split, t + 1)
                for half in range(2):
                    cols = slice(half * HALF, (half + 1) * HALF)
                    for k in range(chunks):
                        if t == 0 and half == 0:
                            pe.wait_ge(w_split, k + 1)
                        last = split_matmul(nc, psum[:, 2 * (t % 2) + half, :], y_hi[:, k, :], y_lo[:, k, :],
                                            w_hi[:, k, cols], w_lo[:, k, cols], k == 0, k == chunks - 1)
                    last.then_inc(summed, 1)
                if t >= 1:
                    norm.pe(pe, t - 1)
            norm.pe(pe, TT - 1)


class WeightSlots:

    def __init__(self, nc, ctx, name, width):
        def sb(n, dt=F32):
            return [ctx.enter_context(nc.sbuf_tensor(f"{name}_{n}{i}", [P, DC // 2, width], dt)) for i in range(2)]

        self.nc, self.width = nc, width
        self.raw, self.hi, self.lo = sb("raw"), sb("hi", F32R), sb("lo", F32R)
        self.loaded = [phase_semaphore(nc, ctx, f"{name}_loaded{i}") for i in range(2)]
        self.high = phase_semaphore(nc, ctx, f"{name}_high")
        self.split = phase_semaphore(nc, ctx, f"{name}_split")
        self.base = 0
        self.ahead = 0

    def load(self, sp, s, w):
        S, kh, half = self.base + s, s % 2, DC // 2
        if S >= 2:
            sp.wait_ge(self.split, S - 1)
        sp.dma_start(self.raw[kh][:, :, 0:w.shape[1]],
                     w.rearrange("(d p) n -> p d n", p=P)[:, kh * half:(kh + 1) * half, :]).then_inc(self.loaded[kh], 16)

    def wait_loaded(self, eng, s):
        eng.wait_ge(self.loaded[s % 2], 16 * ((self.base + s) // 2 + 1))

    def split_ahead(self, pool, w):
        for s in range(2):
            raw, hi, lo = (x[s][:, :, 0:w.shape[1]] for x in (self.raw, self.hi, self.lo))
            self.wait_loaded(pool, s)
            self.nc.gpsimd.tensor_copy(hi, raw).then_inc(self.high, 1)
            pool.wait_ge(self.high, self.base + s + 1)
            self.nc.gpsimd.tensor_tensor(lo, raw, hi.bitcast(F32), ALU.subtract).then_inc(self.split, 1)


def project_phase(nc, ph, psum, ident, neg_half, tiles, stat_hi, stat_lo, blocks, extra_loads=(), slots=None):
    half_d = DC // 2
    groups, t = [], 0
    while t < tiles:
        groups.append(list(range(t, min(t + 3, tiles))))
        t += 3
    n_groups = len(groups)
    dve_kinds = ("heads",)
    freed, count = [], {"act": 0, "dve": 0}
    heads_before = []
    n_heads = 0
    for b in blocks:
        for t in range(tiles):
            who = "dve" if b["kind"] in dve_kinds else "act"
            count[who] += 1
            freed.append((who, count[who]))
            heads_before.append(n_heads)
            n_heads += b["kind"] == "heads"
    gates_before, n = [], 0
    for b in blocks:
        gates_before.append(n)
        n += tiles * (b["kind"] == "gate")

    with ExitStack() as ctx:
        ctx.callback(nc.all_engine_barrier)
        def sb(name, shape, dt=F32):
            return ctx.enter_context(nc.sbuf_tensor(f"{ph}_{name}", shape, dt))

        def sem(name):
            return phase_semaphore(nc, ctx, f"{ph}_{name}")

        if slots is None:
            slots = WeightSlots(nc, ctx, f"{ph}_w", max(b["w"].shape[1] for b in blocks))
        w_raw, w_hi, w_lo, base, ahead = slots.raw, slots.hi, slots.lo, slots.base, slots.ahead
        extra_loaded = sem("extra_loaded")
        first_read = sem("first_read")
        done = sem("done")
        gate_free = sem("gate_gained")
        if n_heads:
            hw = max(b["w"].shape[1] for b in blocks if b["kind"] == "heads")
            squares = sb("squares", [P, 2, hw])
            sums = sb("head_sums", [P, 2, 4])
            rstd = sb("head_rstd", [P, 2, 4])
            rows = sb("head_rows", [P, hw])
            roped = [sb(f"head_roped{i}", [P, hw]) for i in range(3)]
            cross = sb("rope_cross", [P, hw])
        squared, mean, rstd_ready = sem("squared"), sem("mean"), sem("rstd_ready")
        rows_ready, link = sem("rows_ready"), sem("rope_link")
        turned, turn_out = sem("turned"), sem("turn_out")
        free = {"act": sem("freed_by_act"), "dve": rows_ready}

        def bank_of(T):
            b, t = divmod(T, tiles)
            g = t // 3
            return 3 * ((b * n_groups + g) % 2) + t % 3

        block = ctx.enter_context(nc.Block())

        @block.sync
        def _(sp):
            for out, src in extra_loads:
                sp.dma_start(out, src).then_inc(extra_loaded, 16)
            for s in range(ahead, 2 * len(blocks)):
                slots.load(sp, s, blocks[s // 2]["w"])

        def slots_free(eng, s):
            b, kh = divmod(s, 2)
            if b >= 1:
                if kh == 0:
                    eng.wait_ge(first_read, b)
                else:
                    eng.wait_ge(done, tiles * b)

        def over_tiles(split, tile, turn):
            for s in range(ahead, 2):
                split(s)
            before = []
            for b in range(len(blocks)):
                for g, group in enumerate(groups):
                    for bt in before:
                        turn(*bt)
                    if g == n_groups - 1 and b + 1 < len(blocks):
                        split(2 * b + 2)
                    for t in group:
                        tile(b, t)
                    if g == n_groups - 1 and b + 1 < len(blocks):
                        split(2 * b + 3)
                    before = [(b, t) for t in group]
            for bt in before:
                turn(*bt)

        @block.scalar
        def _(act):
            if extra_loads:
                act.wait_ge(extra_loaded, 16 * len(extra_loads))

            def split(s):
                b, kh = divmod(s, 2)
                n = blocks[b]["w"].shape[1]
                slots.wait_loaded(act, s)
                slots_free(act, s)
                nc.scalar.activation(w_hi[kh][:, :, 0:n], w_raw[kh][:, :, 0:n], ACT.Copy).then_inc(slots.high, 1)

            def tile(b, t):
                blk, T = blocks[b], b * tiles + t
                n = blk["w"].shape[1]
                acc = psum[:, bank_of(T), 0:n]
                act.wait_ge(done, T + 1)
                if blk["kind"] == "heads":
                    H, dim = heads_before[T], blk["dim"]
                    if H >= 2:
                        act.wait_ge(rows_ready, H - 1)
                    for h in range(n // dim):
                        nc.scalar.activation(squares[:, H % 2, h * dim:(h + 1) * dim], acc[:, h * dim:(h + 1) * dim], ACT.Square,
                                             accum_out=sums[:, H % 2, h:h + 1]).then_inc(squared, 1)
                else:
                    nc.scalar.activation(blk["dest"](t), acc, ACT.Silu if blk["kind"] == "gate" else ACT.Copy).then_inc(free["act"], 1)

            def turn(b, t):
                blk, T = blocks[b], b * tiles + t
                if blk["kind"] != "heads":
                    return
                H, n = heads_before[T], blk["w"].shape[1]
                act.wait_ge(turned, H + 1)
                for i, (dst, src) in enumerate(blk["dest"](t, psum[:, 6 + H % 2, 0:n])):
                    ins = nc.scalar.activation(dst, src, ACT.Copy)
                ins.then_inc(turn_out, 1)

            over_tiles(split, tile, turn)

        @block.gpsimd
        def _(pool):
            n_sq = 0
            for b, blk in enumerate(blocks):
                if blk["kind"] != "heads":
                    continue
                for t in range(tiles):
                    H, nh, dim = heads_before[b * tiles + t], blk["w"].shape[1] // blk["dim"], blk["dim"]
                    n_sq += nh
                    s, r = sums[:, H % 2, 0:nh], rstd[:, H % 2, 0:nh]
                    pool.wait_ge(squared, n_sq)
                    if H >= 2:
                        pool.wait_ge(rows_ready, H - 1)
                    nc.gpsimd.tensor_scalar(s, s, 1.0 / dim, EPS, ALU.mult, ALU.add).then_inc(mean, 1)
                    pool.wait_ge(mean, H + 1)
                    nc.gpsimd.tensor_tensor(r, s, neg_half[:, 0:nh], ALU.pow).then_inc(rstd_ready, 1)

        @block.vector
        def _(dve):
            if extra_loads:
                dve.wait_ge(extra_loaded, 16 * len(extra_loads))
            links = [0]

            def split(s):
                b, kh = divmod(s, 2)
                n = blocks[b]["w"].shape[1]
                dve.wait_ge(slots.high, base + s + 1)
                nc.vector.tensor_tensor(w_lo[kh][:, :, 0:n], w_raw[kh][:, :, 0:n], w_hi[kh][:, :, 0:n].bitcast(F32),
                                        ALU.subtract).then_inc(slots.split, 1)

            def tile(b, t):
                blk, T = blocks[b], b * tiles + t
                n = blk["w"].shape[1]
                acc = psum[:, bank_of(T), 0:n]
                if blk["kind"] == "gate":
                    dve.wait_ge(free["act"], freed[T][1])
                    out = blk["dest"](t).rearrange("p (h v) -> p h v", v=GLA_DV)
                    nc.vector.tensor_tensor(out, out, blk["gain"].unsqueeze(1).broadcast_to([P, n // GLA_DV, GLA_DV]),
                                            ALU.mult).then_inc(gate_free, 1)
                if blk["kind"] != "heads":
                    return
                H, dim = heads_before[T], blk["dim"]
                nh, buf = n // dim, rows if blk.get("rope") else roped[H % 3]
                dve.wait_ge(rstd_ready, H + 1)
                if H >= 3:
                    dve.wait_ge(turned, H - 2)
                for h in range(nh):
                    cols = slice(h * dim, (h + 1) * dim)
                    ins = nc.vector.scalar_tensor_tensor(buf[:, cols], acc[:, cols], rstd[:, H % 2, h:h + 1],
                                                         blk["gain"], ALU.mult, ALU.mult)
                if not blk.get("rope"):
                    ins.then_inc(rows_ready, 1)
                    return
                links[0] += 1
                ins.then_inc(link, 1)
                dve.wait_ge(link, links[0])
                half = dim // 2
                cos, sin = (x[:, t, :].unsqueeze(1).broadcast_to([P, nh, half]) for x in blk["rope"])
                x = buf[:, 0:n].rearrange("p (h two k) -> p h two k", two=2, k=half)
                o = roped[H % 3][:, 0:n].rearrange("p (h two k) -> p h two k", two=2, k=half)
                c = cross[:, 0:n].rearrange("p (h two k) -> p h two k", two=2, k=half)
                for two in range(2):
                    nc.vector.tensor_tensor(o[:, :, two, :], x[:, :, two, :], cos, ALU.mult)
                    ins = nc.vector.tensor_tensor(c[:, :, two, :], x[:, :, 1 - two, :], sin, ALU.mult)
                links[0] += 1
                ins.then_inc(link, 1)
                dve.wait_ge(link, links[0])
                nc.vector.tensor_tensor(o[:, :, 0, :], o[:, :, 0, :], c[:, :, 0, :], ALU.subtract)
                nc.vector.tensor_tensor(o[:, :, 1, :], o[:, :, 1, :], c[:, :, 1, :], ALU.add).then_inc(rows_ready, 1)

            over_tiles(split, tile, lambda b, t: None)

        @block.tensor
        def _(pe):
            before = []

            def turns():
                for b, t in before:
                    blk, T = blocks[b], b * tiles + t
                    if blk["kind"] != "heads":
                        continue
                    H, n = heads_before[T], blk["w"].shape[1]
                    pe.wait_ge(rows_ready, H + 1)
                    if H >= 2:
                        pe.wait_ge(turn_out, H - 1)
                    for i in range(n // P):
                        ins = nc.tensor.transpose(psum[:, 6 + H % 2, i * P:(i + 1) * P],
                                                  roped[H % 3][:, i * P:(i + 1) * P], ident[:, :])
                    ins.then_inc(turned, 1)

            for b, blk in enumerate(blocks):
                n = blk["w"].shape[1]
                for g, group in enumerate(groups):
                    G = b * n_groups + g
                    if G >= 2:
                        b2, g2 = divmod(G - 2, n_groups)
                        for who in ("act", "dve"):
                            upto = [v for w, v in freed[:b2 * tiles + groups[g2][-1] + 1] if w == who]
                            if upto:
                                pe.wait_ge(free[who], upto[-1])
                    for kh in range(2):
                        pe.wait_ge(slots.split, base + 2 * b + kh + 1)
                        for t in group:
                            for d in range(half_d):
                                dd = kh * half_d + d
                                last = split_matmul(nc, psum[:, bank_of(b * tiles + t), 0:n],
                                                    blk["pick"](stat_hi, dd, t), blk["pick"](stat_lo, dd, t),
                                                    w_hi[kh][:, d, 0:n], w_lo[kh][:, d, 0:n], dd == 0, dd == DC - 1)
                            if kh == 1:
                                last.then_inc(done, 1)
                        if kh == 0 and g == n_groups - 1:
                            last.then_inc(first_read, 1)
                        if kh == 0:
                            turns()
                    before[:] = [(b, t) for t in group]
            turns()

        slots.base += 2 * len(blocks)
        slots.ahead = 0


def attention_phase(nc, ph, psum, ident, units, stage=None, loads=(), load_unit=0, ahead=None):
    U = len(units)
    staged = TT * DIL_HEADS if stage is not None else 0
    with ExitStack() as ctx:
        ctx.callback(nc.all_engine_barrier)
        def sb(name, shape, dt=F32):
            return ctx.enter_context(nc.sbuf_tensor(f"{ph}_{name}", shape, dt))

        def sem(name):
            return phase_semaphore(nc, ctx, f"{ph}_{name}")

        S, T, O = 3, 2, 2
        masked = [sb(f"masked{i}", [P, 2 * P]) for i in range(3)]
        probs = [sb(f"probs{i}", [P, 2 * P]) for i in range(3)]
        probs_t = [sb(f"probs_t{i}", [P, 2 * P]) for i in range(3)]
        top = sb("top", [P, U])
        neg_top = sb("neg_top", [P, U])
        total = sb("total", [P, U])
        inv = sb("inv", [P, U])
        scored = sem("scored")
        topped = sem("topped")
        negated = sem("negated")
        expd = sem("expd")
        turned = sem("turned")
        turn_out = sem("turn_out")
        mixed = sem("mixed")
        inverted = sem("inverted")
        out_done = sem("out_done")
        logged, lse_done = sem("logged"), sem("lse_done")
        loaded = sem("loaded")
        block = ctx.enter_context(nc.Block())
        T_LAG, O_LAG = 2, 3

        @block.tensor
        def _(pe):
            for i in range(U + O_LAG):
                if i < U:
                    q, k, n = units[i][0:3]
                    if loads and i == load_unit:
                        pe.wait_ge(loaded, 16 * len(loads))
                    if i >= S:
                        pe.wait_ge(topped, i - S + 1)
                    nc.tensor.matmul(psum[:, i % S, 0:n], q, k, start=True, stop=True).then_inc(scored, 1)
                u = i - T_LAG
                if 0 <= u < U:
                    n = units[u][2]
                    pe.wait_ge(expd, u + 1)
                    if u >= T:
                        pe.wait_ge(turn_out, u - T + 1)
                    for c in range(n // P):
                        ins = nc.tensor.transpose(psum[:, S + u % T, c * P:(c + 1) * P], probs[u % 3][:, c * P:(c + 1) * P], ident[:, :])
                    ins.then_inc(turned, 1)
                u = i - O_LAG
                if 0 <= u < U:
                    n, vals = units[u][2], units[u][4]
                    pe.wait_ge(turn_out, u + 1)
                    if u >= O:
                        pe.wait_ge(out_done, u - O + 1)
                    for c, v in enumerate(vals):
                        ins = nc.tensor.matmul(psum[:, S + T + u % O, 0:v.shape[-1]], probs_t[u % 3][:, c * P:(c + 1) * P], v,
                                               start=c == 0, stop=c == len(vals) - 1)
                    ins.then_inc(mixed, 1)

        @block.vector
        def _(dve):
            for i in range(U + O_LAG):
                if i < U:
                    n, mask, scale = units[i][2], units[i][3], units[i][6]
                    dve.wait_ge(scored, i + 1)
                    if i >= 3:
                        dve.wait_ge(expd, i - 2)
                    nc.vector.tensor_tensor_reduce(masked[i % 3][:, 0:n], psum[:, i % S, 0:n], mask, 1.0, -3e38,
                                                   ALU.add, ALU.max, top[:, i:i + 1]).then_inc(topped, 1)
                    dve.wait_ge(topped, i + 1)
                    nc.vector.tensor_scalar(neg_top[:, i:i + 1], top[:, i:i + 1], -scale, None, ALU.mult).then_inc(negated, 1)
                u = i - T_LAG
                if 0 <= u < U:
                    n = units[u][2]
                    dve.wait_ge(turned, u + 1)
                    if u >= 3:
                        dve.wait_ge(mixed, u - 2)
                    nc.vector.tensor_copy(probs_t[u % 3][:, 0:n], psum[:, S + u % T, 0:n]).then_inc(turn_out, 1)
                    nc.vector.reciprocal(inv[:, u:u + 1], total[:, u:u + 1]).then_inc(inverted, 1)
                if i == staged + T_LAG and staged:
                    dve.wait_ge(logged, 1)
                    nc.vector.scalar_tensor_tensor(stage.lse[:, :], top[:, 0:staged], units[0][6], total[:, 0:staged],
                                                   ALU.mult, ALU.add).then_inc(lse_done, 1)

        @block.scalar
        def _(act):
            for i in range(U + O_LAG):
                if i < U:
                    n, scale = units[i][2], units[i][6]
                    act.wait_ge(negated, i + 1)
                    if i >= 3:
                        act.wait_ge(turned, i - 2)
                    nc.scalar.activation(probs[i % 3][:, 0:n], masked[i % 3][:, 0:n], ACT.Exp, bias=neg_top[:, i:i + 1],
                                         scale=scale, accum_out=total[:, i:i + 1]).then_inc(expd, 1)
                u = i - O_LAG
                if 0 <= u < U:
                    w, out = units[u][4][0].shape[-1], units[u][5]
                    act.wait_ge(mixed, u + 1)
                    act.wait_ge(inverted, u + 1)
                    if u < staged and u % 4 == 0 and stage.before(u // 4):
                        act.wait_ge(stage.stored[u // 4 % 2], stage.before(u // 4))
                    nc.scalar.activation(out, psum[:, S + T + u % O, 0:w], ACT.Copy, scale=inv[:, u:u + 1]).then_inc(out_done, 1)
                if i == staged + T_LAG - 1 and staged:
                    act.wait_ge(inverted, staged)
                    nc.scalar.activation(total[:, 0:staged], total[:, 0:staged], ACT.Ln).then_inc(logged, 1)

        @block.sync
        def _(sp):
            for out, src in loads:
                sp.dma_start(out, src).then_inc(loaded, 16)
            if ahead is not None:
                for s in range(2):
                    ahead[0].load(sp, s, ahead[1])
            if staged:
                for t in range(TT):
                    sp.wait_ge(out_done, 4 * t + 4)
                    stage.store(sp, t)
                sp.wait_ge(lse_done, 1)
                stage.store_lse(sp)

        if ahead is not None:
            @block.gpsimd
            def _(pool):
                ahead[0].split_ahead(pool, ahead[1])

            ahead[0].ahead = 2
        if staged:
            stage.groups += 1


def gla_phase(nc, ph, psum, ident, neg_half, hT_hi, hT_lo, w_in, w_gate2, b_gate, V, Y):
    DK, DV, PAIRS, CH = GLA_DK, GLA_DV, SEQ // P, SEQ // CHUNK
    QK = 2 * DK
    with ExitStack() as ctx:
        ctx.callback(nc.all_engine_barrier)
        def sb(name, shape, dt=F32):
            return ctx.enter_context(nc.sbuf_tensor(f"{ph}_{name}", shape, dt))

        def sem(name):
            return phase_semaphore(nc, ctx, f"{ph}_{name}")

        w_raw = sb("w_raw", [P, DC, QK])
        w_hi, w_lo = sb("w_hi", [P, DC, QK], F32R), sb("w_lo", [P, DC, QK], F32R)
        rank = sb("rank", [GLA_RANK, SEQ])
        gate2 = sb("gate2", [GLA_RANK, GLA_HEADS * DK])
        bias = sb("bias", [DK, GLA_HEADS])
        keep = sb("keep", [DK, SEQ])
        z = sb("z", [DK, SEQ])
        soft = sb("soft", [DK, SEQ])
        cum = sb("cum", [DK, SEQ])
        from_mid, to_last = soft, z
        q_mid, k_mid = sb("q_mid", [DK, SEQ]), sb("k_mid", [DK, SEQ])
        q_in, k_out = sb("q_in", [DK, SEQ]), sb("k_out", [DK, SEQ])
        chunk_decay = sb("chunk_decay", [DK, CH])
        decay = sb("decay", [DK, PAIRS])
        att = sb("att", [P, PAIRS, P])
        k_rows = sb("k_rows", [P, PAIRS, DK])
        state = sb("state", [DK, PAIRS, DV])
        squares = sb("squares", [P, 2, DV])
        sums, rstd = sb("sums", [P, PAIRS]), sb("rstd", [P, PAIRS])

        small_loaded = sem("small_loaded")
        w_loaded, w_high, w_split = sem("w_loaded"), sem("w_high"), sem("w_split")
        kept = sem("kept")
        projected = sem("projected")
        rank_ready = sem("rank_ready")
        copied = sem("copied")
        z_ready = sem("z_ready")
        softened = sem("softened")
        act_link, link = sem("act_link"), sem("dve_link")
        shifted = sem("shifted")
        expd = sem("expd")
        timed = sem("timed")
        factored = sem("factored")
        mixed = sem("mixed")
        masked = sem("masked")
        state_ready = sem("state_ready")
        squared, mean, rstd_ready = sem("squared"), sem("mean"), sem("rstd_ready")
        by_act, by_dve = sem("ring_freed_by_act"), sem("ring_freed_by_dve")

        PER_HEAD = [("att", "act")] * 2 + [("cross", "dve")] + [("keys", "act")] * 2 + [("delta", "state")] * 4 + [("out", "dve")] * 4
        ring = [("z", "act")] * 2
        q_sb, k_sb = (Y[0:DK, :, D_MIX + i * P:D_MIX + (i + 1) * P] for i in range(2))
        first_of, z_of = [], [0]
        for h in range(GLA_HEADS):
            if h + 1 < GLA_HEADS:
                z_of.append(len(ring))
                ring += [("z", "act")] * 2
            first_of.append(len(ring))
            ring += PER_HEAD

        def freed(i):
            kind, who = ring[i]
            if kind == "delta":
                h = max(h for h in range(GLA_HEADS) if first_of[h] <= i)
                return state_ready, (PAIRS - 1) * h + min(2 * (i - first_of[h] - 5) + 2, PAIRS - 1)
            return (by_act if who == "act" else by_dve), sum(w == who for _, w in ring[:i + 1])

        def bank(i):
            return psum[:, 4 + i % 4, :]

        def mixes_before(i):
            return sum(kind != "z" for kind, _ in ring[:i])

        block = ctx.enter_context(nc.Block())
        w_view = w_in.rearrange("(d p) n -> p d n", p=P)

        @block.sync
        def _(sp):
            sp.dma_start(gate2[:, :], w_gate2).then_inc(small_loaded, 16)
            sp.dma_start(bias[:, :], b_gate.rearrange("(h k) -> k h", k=DK), allow_slow_non_contiguous=True).then_inc(small_loaded, 16)
            off = 2 * GLA_HEADS * DK + D_MIX
            sp.dma_start(w_raw[:, :, 0:P], w_view[:, :, off:off + P]).then_inc(w_loaded, 16)
            for h in range(GLA_HEADS):
                sp.wait_ge(w_split, h + 1)
                for part in range(2):
                    sp.dma_start(w_raw[:, :, part * DK:(part + 1) * DK],
                                 w_view[:, :, (part * GLA_HEADS + h) * DK:(part * GLA_HEADS + h + 1) * DK]).then_inc(w_loaded, 16)

        @block.gpsimd
        def _(pool):
            nc.gpsimd.memset(keep[:, :], 1.0).then_inc(kept, 1)
            pool.wait_ge(kept, 1)
            nc.gpsimd.memset(keep[:, :].rearrange("p (c i) -> p c i", i=CHUNK)[:, :, 0:1], 0.0).then_inc(kept, 1)
            for h in range(GLA_HEADS):
                pool.wait_ge(*freed(first_of[h] + 1))
                pool.wait_ge(*freed(first_of[h] + 2))
                nc.gpsimd.affine_select(out=att[:, :, :], in_=att[:, :, :], compare_op=ALU.is_ge, fill=0.0, base=0,
                                        pattern=[[0, PAIRS], [1, P]], channel_multiplier=-1).then_inc(masked, 1)
                pool.wait_ge(squared, PAIRS * (h + 1))
                nc.gpsimd.tensor_scalar(sums[:, :], sums[:, :], 1.0 / DV, EPS, ALU.mult, ALU.add).then_inc(mean, 1)
                pool.wait_ge(mean, h + 1)
                nc.gpsimd.tensor_tensor(rstd[:, :], sums[:, :], neg_half[:, 0:PAIRS], ALU.pow).then_inc(rstd_ready, 1)

        @block.scalar
        def _(act):
            links = [0]

            def high(s):
                act.wait_ge(w_loaded, 16 if s == 0 else 16 + 32 * s)
                if s:
                    act.wait_ge(projected, 2 * s - 1)
                n = P if s == 0 else QK
                nc.scalar.activation(w_hi[:, :, 0:n], w_raw[:, :, 0:n], ACT.Copy).then_inc(w_high, 1)

            def copy(h, i):
                act.wait_ge(projected, 2 * h + 2 + i)
                if h:
                    act.wait_ge(timed, 4 * h - i)
                nc.scalar.activation((q_sb, k_sb)[i], psum[0:DK, 2 * i:2 * i + 2, :].rearrange("p b (c n) -> p (b c) n", n=P),
                                     ACT.Copy).then_inc(copied, 1)

            def gate(h):
                if h:
                    act.wait_ge(expd, 4 * h)
                for half in range(2):
                    cols, src = slice(half * HALF, (half + 1) * HALF), bank(z_of[h] + half)[0:DK, :]
                    act.wait_ge(z_ready, 2 * h + half + 1)
                    nc.scalar.activation(z[:, cols], src, ACT.Identity, bias=bias[:, h:h + 1])
                    nc.scalar.activation(soft[:, cols], src, ACT.Abs, bias=bias[:, h:h + 1]).then_inc(by_act, 1)
                act.wait_ge(by_act, freed(z_of[h] + 1)[1])
                nc.scalar.activation(soft[:, :], soft[:, :], ACT.Exp, scale=-1.0).then_inc(act_link, 1)
                links[0] += 1
                act.wait_ge(act_link, links[0])
                nc.scalar.activation(soft[:, :], soft[:, :], ACT.Ln, bias=1.0).then_inc(softened, 1)

            def factor(h, i):
                out, src, s, entries = ((q_mid, from_mid, 1, 2), (k_mid, from_mid, -1, 2), (k_out, to_last, 1, 5), (q_in, cum, 1, 13))[i]
                act.wait_ge(shifted, h + 1)
                if h:
                    act.wait_ge(mixed, mixes_before(first_of[h - 1] + entries))
                nc.scalar.activation(out[:, :], src[:, :], ACT.Exp, scale=s / 16.0).then_inc(expd, 1)

            high(0)
            act.wait_ge(projected, 1)
            act.wait_ge(small_loaded, 32)
            for half in range(2):
                nc.scalar.activation(rank[:, half * HALF:(half + 1) * HALF], psum[0:GLA_RANK, half, :], ACT.Copy).then_inc(rank_ready, 1)
            high(1)
            gate(0)
            for i in range(4):
                factor(0, i)
            copy(0, 0)
            copy(0, 1)
            high(2)
            for h in range(GLA_HEADS):
                f, more = first_of[h], h + 1 < GLA_HEADS
                if more:
                    gate(h + 1)
                if h:
                    act.wait_ge(mixed, mixes_before(f))
                for i in range(2):
                    act.wait_ge(mixed, mixes_before(f + i) + 1)
                    nc.scalar.activation(att[:, 4 * i:4 * i + 4, :], bank(f + i).rearrange("p (c n) -> p c n", n=P), ACT.Copy).then_inc(by_act, 1)
                if more:
                    factor(h + 1, 0)
                    factor(h + 1, 1)
                    copy(h + 1, 0)
                for i in range(2):
                    act.wait_ge(mixed, mixes_before(f + 3 + i) + 1)
                    nc.scalar.activation(k_rows[:, 4 * i:4 * i + 4, :], bank(f + 3 + i)[:, 0:4 * DK].rearrange("p (c k) -> p c k", k=DK),
                                         ACT.Copy).then_inc(by_act, 1)
                if more:
                    factor(h + 1, 2)
                    copy(h + 1, 1)
                if h + 2 < GLA_HEADS:
                    high(h + 3)
                if h:
                    act.wait_ge(rstd_ready, h)
                for p in range(PAIRS):
                    act.wait_ge(mixed, mixes_before(f + 9 + p // 2) + 1)
                    if h or p >= 2:
                        act.wait_ge(squared, PAIRS * h + p - 1)
                    nc.scalar.activation(squares[:, p % 2, :], bank(f + 9 + p // 2)[:, (p % 2) * DV:(p % 2 + 1) * DV], ACT.Square,
                                         accum_out=sums[:, p:p + 1]).then_inc(squared, 1)
                if more:
                    factor(h + 1, 3)

        @block.vector
        def _(dve):
            links = [0]

            def chain(ins):
                ins.then_inc(link, 1)
                links[0] += 1
                dve.wait_ge(link, links[0])

            def low(s):
                dve.wait_ge(w_high, s + 1)
                n = P if s == 0 else QK
                nc.vector.tensor_tensor(w_lo[:, :, 0:n], w_raw[:, :, 0:n], w_hi[:, :, 0:n].bitcast(F32), ALU.subtract).then_inc(w_split, 1)

            def sums_of(h):
                dve.wait_ge(softened, h + 1)
                chain(nc.vector.scalar_tensor_tensor(soft[:, :], z[:, :], 0.0, soft[:, :], ALU.min, ALU.subtract))
                chain(nc.vector.tensor_tensor_scan(cum[:, :], keep[:, :], soft[:, :], 0.0, ALU.mult, ALU.add))
                c = cum[:, :].rearrange("p (c i) -> p c i", i=CHUNK)
                mid, last = (c[:, :, i:i + 1].broadcast_to([DK, CH, CHUNK]) for i in (CHUNK // 2 - 1, CHUNK - 1))
                nc.vector.tensor_tensor(from_mid[:, :].rearrange("p (c i) -> p c i", i=CHUNK), c, mid, ALU.subtract)
                nc.vector.tensor_tensor(to_last[:, :].rearrange("p (c i) -> p c i", i=CHUNK), last, c, ALU.subtract).then_inc(shifted, 1)

            def product(h, i):
                x, src = ((q_mid, q_sb), (k_mid, k_sb), (k_out, k_sb), (q_in, q_sb))[i]
                x = x[:, :].rearrange("p (c n) -> p c n", n=P)
                dve.wait_ge(expd, 4 * h + i + 1)
                if i == 3:
                    chain(nc.vector.tensor_copy(chunk_decay[:, :], q_in[:, :].rearrange("p (c i) -> p c i", i=CHUNK)[:, :, CHUNK - 1]))
                    cd = chunk_decay[:, :].rearrange("p (c two) -> p c two", two=2)
                    nc.vector.tensor_tensor(decay[:, :], cd[:, :, 0], cd[:, :, 1], ALU.mult)
                if src is q_sb:
                    dve.wait_ge(copied, 2 * h + 1)
                    nc.vector.scalar_tensor_tensor(x, src, float(DK) ** -0.5, x, ALU.mult, ALU.mult).then_inc(timed, 1)
                else:
                    dve.wait_ge(copied, 2 * h + 2)
                    nc.vector.tensor_tensor(x, src, x, ALU.mult).then_inc(timed, 1)

            def cross_pair(h):
                qi = q_in[:, :].rearrange("p (c two i) -> p c two i", two=2, i=CHUNK)
                ko = k_out[:, :].rearrange("p (c two i) -> p c two i", two=2, i=CHUNK)
                cd = chunk_decay[:, :].rearrange("p (c two) -> p c two", two=2)
                f = first_of[h]
                dve.wait_ge(mixed, mixes_before(f + 2) + 1)
                dve.wait_ge(timed, 4 * h + 4)
                nc.vector.tensor_tensor(qi[:, :, 1, :], qi[:, :, 1, :], cd[:, :, 0:1].broadcast_to([DK, PAIRS, CHUNK]), ALU.mult)
                nc.vector.tensor_tensor(ko[:, :, 0, :], ko[:, :, 0, :], cd[:, :, 1:2].broadcast_to([DK, PAIRS, CHUNK]), ALU.mult).then_inc(factored, 1)
                dve.wait_ge(*freed(f + 1))
                nc.vector.tensor_copy(att[0:CHUNK, :, CHUNK:P], bank(f + 2)[0:CHUNK, :].rearrange("p (c i) -> p c i", i=CHUNK)).then_inc(by_dve, 1)

            def states(h):
                f = first_of[h]
                for p in range(PAIRS - 1):
                    delta = bank(f + 5 + p // 2)[0:DK, (p % 2) * DV:(p % 2 + 1) * DV]
                    dve.wait_ge(mixed, mixes_before(f + 5 + p // 2) + 1)
                    if p == 0:
                        ins = nc.vector.tensor_copy(state[:, 1, :], delta)
                    else:
                        ins = nc.vector.scalar_tensor_tensor(state[:, p + 1, :], state[:, p, :], decay[:, p:p + 1], delta, ALU.mult, ALU.add)
                    ins.then_inc(state_ready, 1)
                    dve.wait_ge(state_ready, (PAIRS - 1) * h + p + 1)

            def outputs(h):
                f = first_of[h]
                dve.wait_ge(rstd_ready, h + 1)
                for p in range(PAIRS):
                    y = Y[:, p, h * DV:(h + 1) * DV]
                    ins = nc.vector.scalar_tensor_tensor(y, bank(f + 9 + p // 2)[:, (p % 2) * DV:(p % 2 + 1) * DV], rstd[:, p:p + 1], y,
                                                         ALU.mult, ALU.mult)
                    if p % 2:
                        ins.then_inc(by_dve, 1)

            dve.wait_ge(kept, 2)
            low(0)
            low(1)
            sums_of(0)
            for i in range(4):
                product(0, i)
            low(2)
            for h in range(GLA_HEADS):
                more = h + 1 < GLA_HEADS
                if more:
                    sums_of(h + 1)
                cross_pair(h)
                if more:
                    product(h + 1, 0)
                states(h)
                if more:
                    product(h + 1, 1)
                    product(h + 1, 2)
                if h + 2 < GLA_HEADS:
                    low(h + 3)
                outputs(h)
                if more:
                    product(h + 1, 3)

        @block.tensor
        def _(pe):
            def ring_wait(i):
                if i >= 4:
                    pe.wait_ge(*freed(i - 4))

            def project(s, part):
                pe.wait_ge(w_split, s + 1)
                if s == 1 and part == 0:
                    pe.wait_ge(rank_ready, 2)
                if s >= 2:
                    pe.wait_ge(copied, 2 * (s - 2) + part + 1)
                m = P if s == 0 else DK
                for d in range(DC):
                    for w, h, first, final in ((w_hi, hT_hi, d == 0, False), (w_hi, hT_lo, False, False), (w_lo, hT_hi, False, d == DC - 1)):
                        for half in range(2):
                            mm = nc.tensor.matmul(psum[0:m, 2 * part + half, :], w[:, d, part * DK:part * DK + m],
                                                  h[:, d, half * HALF:(half + 1) * HALF], start=first, stop=final)
                mm.then_inc(projected, 1)

            def gate(h):
                for half in range(2):
                    i = z_of[h] + half
                    ring_wait(i)
                    nc.tensor.matmul(bank(i)[0:DK, :], gate2[:, h * DK:(h + 1) * DK], rank[:, half * HALF:(half + 1) * HALF],
                                     start=True, stop=True).then_inc(z_ready, 1)

            def token_products(h):
                f = first_of[h]
                pe.wait_ge(timed, 4 * h + 2)
                for i in range(2):
                    ring_wait(f + i)
                    for c in range(4):
                        tok = slice((4 * i + c) * P, (4 * i + c + 1) * P)
                        mm = nc.tensor.matmul(bank(f + i)[:, c * P:(c + 1) * P], k_mid[:, tok], q_mid[:, tok], start=True, stop=True)
                    mm.then_inc(mixed, 1)
                ring_wait(f + 2)
                pe.wait_ge(timed, 4 * h + 4)
                for p in range(PAIRS):
                    mm = nc.tensor.matmul(bank(f + 2)[0:CHUNK, p * CHUNK:(p + 1) * CHUNK], k_out[:, p * P:p * P + CHUNK],
                                          q_in[:, p * P + CHUNK:(p + 1) * P], start=True, stop=True)
                mm.then_inc(mixed, 1)

            def state_changes(h):
                f = first_of[h]
                pe.wait_ge(factored, h + 1)
                for i in range(2):
                    ring_wait(f + 3 + i)
                    for c in range(4):
                        p = 4 * i + c
                        mm = nc.tensor.transpose(bank(f + 3 + i)[:, c * DK:(c + 1) * DK], k_out[:, p * P:(p + 1) * P], ident[0:DK, 0:DK])
                    mm.then_inc(mixed, 1)
                for p in range(PAIRS - 1):
                    i = f + 5 + p // 2
                    if p % 2 == 0:
                        ring_wait(i)
                    pe.wait_ge(by_act, freed(f + 3 + p // 4)[1])
                    mm = nc.tensor.matmul(bank(i)[0:DK, (p % 2) * DV:(p % 2 + 1) * DV], k_rows[:, p, :],
                                          V[:, p, h * DV:(h + 1) * DV], start=True, stop=True)
                    if p % 2 or p == PAIRS - 2:
                        mm.then_inc(mixed, 1)

            def outputs(h):
                f = first_of[h]
                pe.wait_ge(masked, h + 1)
                for p in range(PAIRS):
                    i = f + 9 + p // 2
                    if p % 2 == 0:
                        ring_wait(i)
                    out = bank(i)[:, (p % 2) * DV:(p % 2 + 1) * DV]
                    mm = nc.tensor.matmul(out, att[:, p, :], V[:, p, h * DV:(h + 1) * DV], start=True, stop=p == 0)
                    if p:
                        pe.wait_ge(state_ready, (PAIRS - 1) * h + p)
                        mm = nc.tensor.matmul(out, q_in[:, p * P:(p + 1) * P], state[:, p, :], start=False, stop=True)
                    if p % 2:
                        mm.then_inc(mixed, 1)

            project(0, 0)
            pe.wait_ge(rank_ready, 2)
            gate(0)
            project(1, 0)
            project(1, 1)
            for h in range(GLA_HEADS):
                more = h + 1 < GLA_HEADS
                if more:
                    gate(h + 1)
                token_products(h)
                if more:
                    project(h + 2, 0)
                state_changes(h)
                if more:
                    project(h + 2, 1)
                outputs(h)


class Merge:

    def __init__(self, nc, ctx, ph, stage, Y):
        def sb(name, shape):
            return ctx.enter_context(nc.sbuf_tensor(f"{ph}_{name}", shape, F32))

        def sem(name):
            return phase_semaphore(nc, ctx, f"{ph}_{name}")

        self.nc, self.stage, self.Y, self.G = nc, stage, Y, len(stage.outs)
        self.logs = sb("logs", [P, self.G, TT, DIL_HEADS])
        self.top, self.inv = sb("top", [P, TT, DIL_HEADS]), sb("inv", [P, TT, DIL_HEADS])
        self.outs = [sb(f"outs{i}", [P, self.G, D_DIL]) for i in range(2)]
        self.logs_loaded, self.link, self.expd = sem("logs_loaded"), sem("link"), sem("expd")
        self.loaded = [sem(f"group_outs_loaded{i}") for i in range(2)]
        self.added = sem("added")
        self.links = 0

    def load_logs(self, sp):
        for g in range(self.G):
            sp.dma_start(self.logs[:, g, :, :], self.stage.lses[g].rearrange("(t p) h -> p t h", p=P)).then_inc(self.logs_loaded, 16)

    def load(self, sp, t):
        if t >= 2:
            sp.wait_ge(self.added, t - 1)
        for g in range(self.G):
            sp.dma_start(self.outs[t % 2][:, g, :], self.stage.outs[g][t * P:(t + 1) * P, :]).then_inc(self.loaded[t % 2], 16)

    def act_exp(self, act):
        act.wait_ge(self.link, 3)
        self.nc.scalar.activation(self.logs[:, :, :, :], self.logs[:, :, :, :], ACT.Exp).then_inc(self.expd, 1)

    def chain(self, dve, ins):
        ins.then_inc(self.link, 1)
        self.links += 1
        dve.wait_ge(self.link, self.links)

    def dve_weights(self, dve):
        nc, logs, top, inv = self.nc, self.logs, self.top[:, :, :], self.inv[:, :, :]
        dve.wait_ge(self.logs_loaded, 16 * self.G)
        self.chain(dve, nc.vector.tensor_tensor(top, logs[:, 0, :, :], logs[:, 1, :, :], ALU.max))
        self.chain(dve, nc.vector.tensor_tensor(top, top, logs[:, 2, :, :], ALU.max))
        for g in range(self.G):
            ins = nc.vector.tensor_tensor(logs[:, g, :, :], logs[:, g, :, :], top, ALU.subtract)
        self.chain(dve, ins)
        dve.wait_ge(self.expd, 1)
        self.chain(dve, nc.vector.tensor_tensor(inv, logs[:, 0, :, :], logs[:, 1, :, :], ALU.add))
        self.chain(dve, nc.vector.tensor_tensor(inv, inv, logs[:, 2, :, :], ALU.add))
        self.chain(dve, nc.vector.reciprocal(inv, inv))
        for g in range(self.G):
            ins = nc.vector.tensor_tensor(logs[:, g, :, :], logs[:, g, :, :], inv, ALU.mult)
        self.chain(dve, ins)

    def dve_add(self, dve, t):
        nc, Y = self.nc, self.Y
        dve.wait_ge(self.loaded[t % 2], 16 * self.G * (t // 2 + 1))
        for g in range(self.G):
            for h in range(DIL_HEADS):
                cols = slice(h * DIL_DIM, (h + 1) * DIL_DIM)
                w, o = self.logs[:, g, t, h:h + 1], self.outs[t % 2][:, g, cols]
                if g == 0:
                    ins = nc.vector.tensor_scalar(Y[:, t, cols], o, w, None, ALU.mult)
                else:
                    ins = nc.vector.scalar_tensor_tensor(Y[:, t, cols], o, w, Y[:, t, cols], ALU.mult, ALU.add)
            if g + 1 < self.G:
                self.chain(dve, ins)
        ins.then_inc(self.added, 1)


def rope_phase(nc, ph, neg_half, positions, inv_freq, cos, sin):
    HD = DIL_DIM // 2
    with ExitStack() as ctx:
        ctx.callback(nc.all_engine_barrier)
        def sb(name, shape, dt=F32):
            return ctx.enter_context(nc.sbuf_tensor(f"{ph}_{name}", shape, dt))

        def sem(name):
            return phase_semaphore(nc, ctx, f"{ph}_{name}")

        pos_i, pos = sb("pos_i", [P, TT], mybir.dt.int32), sb("pos", [P, TT])
        freq = sb("freq", [P, HD])
        turns = sb("turns", [P, TT, HD])
        angle = sb("angle", [P, TT, HD])
        loaded, link, reduced, sined = sem("loaded"), sem("link"), sem("reduced"), sem("sined")
        block = ctx.enter_context(nc.Block())

        @block.sync
        def _(sp):
            sp.dma_start(pos_i[:, :], positions[0, :].rearrange("(t p) -> p t", p=P), allow_slow_non_contiguous=True).then_inc(loaded, 16)
            sp.dma_start(freq[:, :], inv_freq.partition_broadcast(P)).then_inc(loaded, 16)

        @block.vector
        def _(dve):
            links = [0]

            def chain(ins):
                ins.then_inc(link, 1)
                links[0] += 1
                dve.wait_ge(link, links[0])

            two_pi = 2 * math.pi
            parts, left = [], two_pi
            for bits in (5, 13, 21):
                parts.append(math.floor(left * 2 ** bits) / 2 ** bits)
                left -= parts[-1]
            parts.append(left)
            ROUND = 1.5 * 2 ** 23
            dve.wait_ge(loaded, 32)
            chain(nc.vector.tensor_copy(pos[:, :], pos_i[:, :]))
            for shift, out in ((0.0, sin), (math.pi / 2, cos)):
                for t in range(TT):
                    ins = nc.vector.tensor_scalar(angle[:, t, :], freq[:, :], pos[:, t:t + 1], None, ALU.mult)
                chain(ins)
                chain(nc.vector.tensor_scalar(turns[:, :, :], angle[:, :, :], 1 / two_pi, shift / two_pi, ALU.mult, ALU.add))
                chain(nc.vector.tensor_scalar(turns[:, :, :], turns[:, :, :], ROUND, ROUND, ALU.add, ALU.subtract))
                for part in parts:
                    chain(nc.vector.scalar_tensor_tensor(angle[:, :, :], turns[:, :, :], -part, angle[:, :, :], ALU.mult, ALU.add))
                chain(nc.vector.tensor_scalar(angle[:, :, :], angle[:, :, :], shift, 3.1415925, ALU.add, ALU.min))
                nc.vector.tensor_scalar(out[:, :, :], angle[:, :, :], -3.1415925, None, ALU.max).then_inc(reduced, 1)
                dve.wait_ge(reduced, 1 if out is sin else 2)

        @block.scalar
        def _(act):
            for i, out in enumerate((sin, cos)):
                act.wait_ge(reduced, i + 1)
                nc.scalar.activation(out[:, :, :], out[:, :, :], ACT.Sin).then_inc(sined, 1)
            act.wait_ge(sined, 2)


APART_STEP = 8


def setup_phase(nc, psum, ident, neg_half, band, split, zeros, keys0, broadcasts):
    with ExitStack() as ctx:
        ctx.callback(nc.all_engine_barrier)
        done = phase_semaphore(nc, ctx, "setup_done")
        loaded = phase_semaphore(nc, ctx, "setup_loaded")
        parity = phase_semaphore(nc, ctx, "setup_parity")
        apart = ctx.enter_context(nc.sbuf_tensor("apart", [P, P], mybir.dt.int32))
        block = ctx.enter_context(nc.Block())

        @block.vector
        def _(dve):
            dve.wait_ge(done, APART_STEP)
            nc.vector.tensor_scalar(apart[:, :], apart[:, :], 1, None, ALU.bitwise_and).then_inc(parity, 1)
            dve.wait_ge(parity, 1)
            nc.vector.tensor_scalar(split[:, :], apart[:, :], NEG, None, ALU.mult).then_inc(parity, 1)

        @block.sync
        def _(sp):
            for out, row in broadcasts:
                sp.dma_start(out, row.partition_broadcast(P)).then_inc(loaded, 16)
            sp.wait_ge(loaded, 16 * len(broadcasts))

        @block.gpsimd
        def _(pool):
            steps = [0]

            def step(ins):
                ins.then_inc(done, 1)
                steps[0] += 1
                pool.wait_ge(done, steps[0])

            def select(x, op, fill, base, pattern, channel):
                step(nc.gpsimd.affine_select(out=x, in_=x, compare_op=op, fill=fill, base=base, pattern=pattern,
                                             channel_multiplier=channel))

            step(nc.gpsimd.memset(ident[:, :], 0.0))
            select(ident[:, :], ALU.not_equal, 1.0, 0, [[-1, P]], 1)
            step(nc.gpsimd.memset(neg_half[:, :], -0.5))
            step(nc.gpsimd.memset(zeros[:, :], 0.0))
            step(nc.gpsimd.memset(band[:, :], 0.0))
            select(band[:, :], ALU.is_ge, NEG, 0, [[1, 2 * P]], -1)
            select(band[:, :], ALU.is_ge, NEG, P, [[-1, 2 * P]], 1)
            step(nc.gpsimd.iota(apart[:, :], pattern=[[-1, P]], base=2 * P, channel_multiplier=1))
            pool.wait_ge(parity, 2)
            select(split[:, :], ALU.is_ge, NEG, 0, [[-1, P]], 1)
            for k in keys0:
                step(nc.gpsimd.memset(k, 0.0))


class Stage:

    def __init__(self, nc, ctx, outs, lses):
        self.outs, self.lses = outs, lses
        self.tile = [ctx.enter_context(nc.sbuf_tensor(f"stage{i}", [P, D_DIL], F32)) for i in range(2)]
        self.lse_tiles = [ctx.enter_context(nc.sbuf_tensor(f"stage_lse{g}", [P, TT * DIL_HEADS], F32)) for g in range(len(outs))]
        self.stored = [phase_semaphore(nc, ctx, f"stage_stored{i}") for i in range(2)]
        self.lse_stored = phase_semaphore(nc, ctx, "stage_lse_stored")
        self.groups = 0

    @property
    def lse(self):
        return self.lse_tiles[self.groups]

    def before(self, t):
        return 16 * (self.groups * TT // 2 + t // 2)

    def rows(self, dram, t):
        r = min(DILATIONS[self.groups], SEQ // P)
        per = SEQ // r // P
        return dram.rearrange("(a r) c -> r a c", r=r)[t // per, (t % per) * P:(t % per + 1) * P, :]

    def store(self, sp, t):
        sp.dma_start(self.rows(self.outs[self.groups], t), self.tile[t % 2][:, :]).then_inc(self.stored[t % 2], 16)

    def store_lse(self, sp):
        for t in range(TT):
            sp.dma_start(self.rows(self.lses[self.groups], t), self.lse[:, 4 * t:4 * t + 4]).then_inc(self.lse_stored, 16)

    def wait_all(self, eng):
        for sem in self.stored:
            eng.wait_ge(sem, self.before(0))
        eng.wait_ge(self.lse_stored, 16 * TT * self.groups)


def save_phase(nc, ph, pairs):
    with ExitStack() as ctx:
        ctx.callback(nc.all_engine_barrier)
        saved = phase_semaphore(nc, ctx, f"{ph}_saved")
        block = ctx.enter_context(nc.Block())

        @block.sync
        def _(sp):
            for out, src in pairs:
                sp.dma_start(out, src).then_inc(saved, 16)
            sp.wait_ge(saved, 16 * len(pairs))


def build(nc, a, out):
    with ExitStack() as ctx:
        def sb(name, shape, dt=F32, c=ctx):
            return c.enter_context(nc.sbuf_tensor(name, shape, dt))

        psum = ctx.enter_context(nc.psum_tensor("psum", [P, BANKS, HALF], F32))
        ident, neg_half = sb("ident", [P, P]), sb("neg_half", [P, TT])
        band, split, zeros = sb("band", [P, 2 * P]), sb("split", [P, P]), sb("zeros", [P, 2 * P])
        xa_gain = [[sb(f"xa_{n}_gain{i}", [P, XA_DIM]) for n in "qk"] for i in range(2)]
        o_gain = sb("o_gain", [P, GLA_DV])
        dil_gain = [sb("dil_q_gain", [P, DIL_DIM]), sb("dil_k_gain", [P, DIL_DIM])]
        hT_hi, hT_lo = sb("hT_hi", [P, DC, SEQ], F32R), sb("hT_lo", [P, DC, SEQ], F32R)
        XY = sb("XY", [P, TT, D])

        def dram(name, shape):
            return nc.dram_tensor(name, shape, F32, kind="Internal").ap()

        x1, x2 = dram("x_mid", [SEQ, D]), dram("x_layer1", [SEQ, D])
        keys_d = [dram(f"mem_keys{i}", [P, XA_HEADS * N_MEM]) for i in range(2)]
        vals_d = [dram(f"mem_values{i}", [P, 2 * D_XA]) for i in range(2)]
        outs_d = [dram(f"group_out{g}", [SEQ, D_DIL]) for g in range(3)]
        lses_d = [dram(f"group_lse{g}", [SEQ, DIL_HEADS]) for g in range(3)]

        def plain(x, d, t):
            return x[:, d, t * P:(t + 1) * P]

        with ExitStack() as c:
            mem_hi, mem_lo = sb("mem_hi", [P, DC, N_MEM], F32R, c), sb("mem_lo", [P, DC, N_MEM], F32R, c)
            keys = [sb(f"keys{i}", [P, XA_HEADS, N_MEM], F32, c) for i in range(2)]
            vals = [sb(f"vals{i}", [P, 2, D_XA], F32, c) for i in range(2)]
            setup_phase(nc, psum, ident, neg_half, band, split, zeros, [k[:, :, :] for k in keys],
                        [(xa_gain[i][0][:, :], a["xa_q_norm"][i, :]) for i in range(2)]
                        + [(xa_gain[i][1][:, :], a["xa_k_norm"][i, :]) for i in range(2)]
                        + [(o_gain[:, :], a["a_o_norm"]), (dil_gain[0][:, :], a["b_q_norm"]), (dil_gain[1][:, :], a["b_k_norm"])])
            norm_phase(nc, "mem", psum, ident, neg_half, a["mem"][0, :, :], N_MEM // P, a["mem_norm"], mem_hi, mem_lo)

            def key_dest(i):
                def dest(t, src):
                    s = src.rearrange("p (a n) -> p a n", n=P)
                    tok = slice(t * P, (t + 1) * P)
                    return [(keys[i][0:64, 0:XA_HEADS:2, tok], s[0:64, :, :]), (keys[i][64:P, 1:XA_HEADS:2, tok], s[64:P, :, :])]
                return dest

            blocks = []
            for i in range(2):
                w = a["xa_w_kv"][i, :, :]
                blocks += [dict(kind="heads", dim=XA_DIM, gain=xa_gain[i][1][:, :], w=w[:, 0:D_XA], pick=plain, dest=key_dest(i)),
                           dict(kind="copy", w=w[:, D_XA:2 * D_XA], pick=plain, dest=lambda t, i=i: vals[i][:, t, :])]
            project_phase(nc, "kv", psum, ident, neg_half, N_MEM // P, mem_hi, mem_lo, blocks)
            save_phase(nc, "kv", [(keys_d[i], keys[i][:, :, :].rearrange("p h n -> p (h n)")) for i in range(2)]
                       + [(vals_d[i], vals[i][:, :, :].rearrange("p h n -> p (h n)")) for i in range(2)])

        def xa_dest(xqT):
            def dest(t, src):
                return [(xqT[:, :, t * P:(t + 1) * P], src.rearrange("p (a n) -> p a n", n=P))]
            return dest

        def xa_units(q_of, keys, vals, base):
            return [(q_of(h, t), keys[:, h, :], N_MEM, zeros[:, :],
                     [vals[:, c, h * XA_DIM:(h + 1) * XA_DIM] for c in range(2)],
                     XY[:, t, base + h * XA_DIM:base + (h + 1) * XA_DIM], float(XA_DIM) ** -0.5) for t in range(TT) for h in range(XA_HEADS)]

        def xa_keys(i, c):
            return sb(f"xa_keys{i}", [P, XA_HEADS, N_MEM], F32, c), sb(f"xa_values{i}", [P, 2, D_XA], F32, c)

        def xa_loads(i, keys, vals):
            return [(keys[:, :, :].rearrange("p h n -> p (h n)"), keys_d[i]), (vals[:, :, :].rearrange("p h n -> p (h n)"), vals_d[i])]

        def tokens(x, t, r):
            r = min(r, SEQ // P)
            v = x.rearrange("p (a r) -> p r a", r=r)
            per = SEQ // r // P
            return v[:, t // per, (t % per) * P:(t % per + 1) * P]

        def keys_of(x, t, r):
            per = max(1, SEQ // r // P)
            if r == 16 or t % per == 0:
                return tokens(x, t, r), P, t
            v = x.rearrange("p (a r) -> p r a", r=r)
            b = t % per
            return v[:, t // per, (b - 1) * P:(b + 1) * P], 2 * P, t - 1

        norm_phase(nc, "n0", psum, ident, neg_half, a["x"][0, :, :], TT, a["mix_norm"][0, :], hT_hi, hT_lo)
        with ExitStack() as c:
            xqT = sb("xqT0", [P, 2, SEQ], F32, c)
            with ExitStack() as c2:
                V = sb("gla_v", [P, TT, D_MIX], F32, c2)
                w = a["a_w_in"]
                v0 = 2 * GLA_HEADS * GLA_DK
                g0 = v0 + D_MIX + GLA_RANK
                B = 2 * GLA_DV
                blocks = [dict(kind="copy", w=w[:, v0 + i * B:v0 + (i + 1) * B], pick=plain,
                               dest=lambda t, i=i: V[:, t, i * B:(i + 1) * B]) for i in range(2)]
                blocks += [dict(kind="gate", w=w[:, g0 + i * B:g0 + (i + 1) * B], pick=plain, gain=o_gain[:, :],
                                dest=lambda t, i=i: XY[:, t, i * B:(i + 1) * B]) for i in range(2)]
                blocks += [dict(kind="heads", dim=XA_DIM, gain=xa_gain[0][0][:, :], w=w[:, g0 + D_MIX:g0 + D_MIX + D_XA],
                                pick=plain, dest=xa_dest(xqT))]
                project_phase(nc, "p0", psum, ident, neg_half, TT, hT_hi, hT_lo, blocks)
                gla_phase(nc, "gla", psum, ident, neg_half, hT_hi, hT_lo, w, a["a_w_gate2"], a["a_b_gate"], V, XY)
            keys, vals = xa_keys(0, c)
            attention_phase(nc, "xa0", psum, ident, xa_units(lambda h, t: xqT[:, h // 2, t * P:(t + 1) * P], keys, vals, D_MIX),
                            loads=xa_loads(0, keys, vals))
        out_phase(nc, "o0", psum, ident, neg_half, XY, DC, a["a_w_out"], a["x"][0, :, :], a["ffn_norm"][0, :], hT_hi, hT_lo)
        ffn_phase(nc, "f0", psum, ident, XY, hT_hi, hT_lo, a["ffn_w_up"][0, :, :], a["ffn_conv_w"][0, :, :], a["ffn_conv_b"][0, :],
                  a["ffn_w_down"][0, :, :], x2)

        stage = Stage(nc, ctx, outs_d, lses_d)
        norm_phase(nc, "n1", psum, ident, neg_half, x2, TT, a["mix_norm"][1, :], hT_hi, hT_lo)
        with ExitStack() as c:
            cos, sin = sb("cos", [P, TT, DIL_DIM // 2], F32, c), sb("sin", [P, TT, DIL_DIM // 2], F32, c)
            rope_phase(nc, "rope", neg_half, a["positions"], a["inv_freq"], cos, sin)
            qT, kT = (sb(f"dil_{n}T", [P, DIL_HEADS, SEQ], F32, c) for n in "qk")
            V = XY[:, :, 0:D_DIL]
            XQ = XY[:, :, D_DIL + D_XA:]
            w = a["b_w_in"]
            cols = 3 * D_DIL
            slots = WeightSlots(nc, c, "w", HALF)

            def head_dest(x):
                return lambda t, src: [(x[:, :, t * P:(t + 1) * P], src.rearrange("p (h n) -> p h n", n=P))]

            def group_blocks(g):
                off, r = g * D_DIL, DILATIONS[g]
                blocks = [dict(kind="heads", dim=DIL_DIM, gain=dil_gain[i][:, :], rope=(cos, sin), w=w[:, i * cols + off:i * cols + off + D_DIL],
                               pick=plain, dest=head_dest(x)) for i, x in enumerate((qT, kT))]
                return blocks + [dict(kind="copy", w=w[:, 2 * cols + off:2 * cols + off + D_DIL],
                                      pick=lambda x, d, t: tokens(x[:, d, :], t, r), dest=lambda t: V[:, t, :])]

            for g, r in enumerate(DILATIONS):
                blocks = group_blocks(g)
                if g == 0:
                    blocks.insert(0, dict(kind="heads", dim=XA_DIM, gain=xa_gain[1][0][:, :], w=w[:, 3 * cols:3 * cols + D_XA],
                                          pick=plain, dest=lambda t, src: [(XQ[:, t, :], src)]))
                project_phase(nc, f"p1_{g}", psum, ident, neg_half, TT, hT_hi, hT_lo, blocks, slots=slots)
                with ExitStack() as c2:
                    units = []
                    for t in range(TT):
                        for h in range(DIL_HEADS):
                            k, n, first = keys_of(kT[:, h, :], t, r)
                            mask = split[:, :] if r == 16 else band[:, 2 * P - n:2 * P]
                            units.append((tokens(qT[:, h, :], t, r), k, n, mask,
                                          [V[:, first + i, h * P:(h + 1) * P] for i in range(n // P)],
                                          stage.tile[t % 2][:, h * P:(h + 1) * P], float(DIL_DIM) ** -0.5))
                    loads = ()
                    if g == 0:
                        keys, vals = xa_keys(1, c2)
                        loads = xa_loads(1, keys, vals)
                        units += xa_units(lambda h, t: XQ[:, t, h // 2 * P:(h // 2 + 1) * P], keys, vals, D_DIL)
                    attention_phase(nc, f"da{g}", psum, ident, units, stage, loads, TT * DIL_HEADS,
                                    ahead=(slots, group_blocks(g + 1)[0]["w"]) if g + 1 < len(DILATIONS) else None)
        out_phase(nc, "o1", psum, ident, neg_half, XY, (D_DIL + D_XA) // P, a["b_w_out"], x2, a["ffn_norm"][1, :], hT_hi, hT_lo,
                  stage)
        ffn_phase(nc, "f1", psum, ident, XY, hT_hi, hT_lo, a["ffn_w_up"][1, :, :], a["ffn_conv_w"][1, :, :], a["ffn_conv_b"][1, :],
                  a["ffn_w_down"][1, :, :], out)


_INS = ["x", "mem", "positions", "mem_norm", "mix_norm", "xa_w_kv", "xa_q_norm", "xa_k_norm", "ffn_norm", "ffn_w_up",
        "ffn_conv_w", "ffn_conv_b", "ffn_w_down", "a_w_in", "a_w_gate2", "a_b_gate", "a_o_norm", "a_w_out",
        "b_w_in", "b_q_norm", "b_k_norm", "b_w_out"]


def kernel(**inputs):
    import numpy as _np
    import concourse.bacc as _bacc
    from concourse import mybir as _mybir
    from concourse.bass_utils import run_bass_kernel_spmd as _run

    nc = _bacc.Bacc("TRN2", target_bir_lowering=False, num_devices=1)
    half = DIL_DIM // 2
    arrays, aps = {}, {}
    given = {name: _np.ascontiguousarray(inputs[name]) for name in _INS}
    given["inv_freq"] = _np.float32(10000.0) ** (-_np.arange(half, dtype=_np.float32) / _np.float32(half))
    for name, x in given.items():
        arrays[f"in_{name}_dram"] = x
        aps[name] = nc.dram_tensor(f"in_{name}_dram", x.shape, _mybir.dt.from_np(x.dtype), kind="ExternalInput").ap()
    out = nc.dram_tensor("out_0_dram", (1, SEQ, D), F32, kind="ExternalOutput").ap()
    build(nc, aps, out[0, :, :])
    r = _run(nc, [arrays], core_ids=[0])
    return r.results[0]["out_0_dram"]
```

```python
import concourse.bass as bass
from concourse import mybir
from concourse.alu_op_type import AluOpType as ALU
import math
from contextlib import ExitStack

F32 = mybir.dt.float32
F32R = mybir.dt.float32r
ACT = mybir.ActivationFunctionType
AX = mybir.AxisListType

P = 128
D = 1024
SEQ = 1024
DC = D // P
TT = SEQ // P
HALF = 512
FF = 2816
FC = FF // P
GROUPS = FC // 2
BANKS = 8


def phase_semaphore(nc, ctx, name):
    s = ctx.enter_context(nc.semaphore(name))
    ctx.callback(nc.gpsimd.sem_clear, s)
    return s


def split_matmul(nc, out, lhs_hi, lhs_lo, rhs_hi, rhs_lo, start, stop):
    nc.tensor.matmul(out, lhs_hi, rhs_hi, start=start, stop=False)
    nc.tensor.matmul(out, lhs_hi, rhs_lo, start=False, stop=False)
    return nc.tensor.matmul(out, lhs_lo, rhs_hi, start=False, stop=stop)


class RawPair:

    def __init__(self, nc, ctx):
        self.tiles = [ctx.enter_context(nc.sbuf_tensor(f"raw{i}", [P, D], F32)) for i in range(2)]
        self.loaded = [phase_semaphore(nc, ctx, f"raw_loaded{i}") for i in range(2)]
        self.count = [0, 0]

    def load(self, eng, i, src):
        shape = src.shape
        out = self.tiles[i][:, :]
        if len(shape) == 3:
            out = out.rearrange("p (d n) -> p d n", d=shape[1])
        eng.dma_start(out, src).then_inc(self.loaded[i], 16)


def up_unit(w_up, f, c):
    return w_up.rearrange("(d p) c -> p d c", p=P)[:, :, bass.ds((f * FC + c) * P, P)]


def ffn_phase(nc, ph, psum, ident, neg_half, X, hT_hi, hT_lo, w_up, conv_w, conv_b, w_down, x_out, raws, next_gain=None, next_w=None):
    with ExitStack() as ctx:
        ctx.callback(nc.all_engine_barrier)
        def sb(name, shape, dt=F32):
            return ctx.enter_context(nc.sbuf_tensor(f"{ph}_{name}", shape, dt))

        def sem(name):
            return phase_semaphore(nc, ctx, f"{ph}_{name}")

        up_raw = [x[:, :].rearrange("p (d n) -> p d n", d=DC) for x in raws.tiles]
        up_hi = [sb(f"up_hi{j}", [P, DC, P], F32R) for j in range(2)]
        up_lo = [sb(f"up_lo{j}", [P, DC, P], F32R) for j in range(2)]
        down_raw = sb("down_raw", [P, 2, D])
        down_hi = sb("down_hi", [P, 2, D], F32R)
        down_lo = sb("down_lo", [P, 2, D], F32R)
        act_hi = [sb(f"act_hi{j}", [P, 2, SEQ], F32R) for j in range(2)]
        act_lo = [sb(f"act_lo{j}", [P, 2, SEQ], F32R) for j in range(2)]
        conv_out = [sb("conv_gate", [P, SEQ]), sb("conv_value", [P, SEQ])]
        taps_rows = sb("taps_rows", [2 * FC, 4, P])
        taps = sb("taps", [P, 4, 2 * FC])

        up_loaded, loaded_before = raws.loaded, list(raws.count)
        down_loaded = sem("down_loaded")
        taps_loaded = sem("taps_loaded")
        taps_turned = sem("taps_turned")
        taps_ready = sem("taps_ready")
        up_high = sem("up_high")
        up_split = sem("up_split")
        down_high = sem("down_high")
        down_split = sem("down_split")
        up_done = sem("up_done")
        conv_started = sem("conv_started")
        conv_tap = sem("conv_tap")
        conv_done = sem("conv_done")
        gate_done = sem("gate_done")
        prod_done = sem("prod_done")
        act_high = sem("act_high")
        act_split = sem("act_split")
        down_done = sem("down_done")
        x_added = sem("x_added")
        stored = sem("stored")
        norm = None
        if next_gain is not None:
            gain_t = sb("next_gain", [P, DC])
            gain_loaded = sem("next_gain_loaded")
            norm = Norm(nc, ctx, ph, psum, (0, 2), ident, neg_half, norm_plan(hT_hi, hT_lo, gain_t),
                        [x[:, :] for x in conv_out], [down_raw[:, i, :].rearrange("p (d n) -> p d n", d=DC) for i in range(2)])
        LAG = 2

        last_down = [[x[:, :, :].rearrange("p d n -> p (d n)") for x in xs] for xs in (up_hi, up_lo)]

        down_view = w_down.rearrange("(f p) n -> p f n", p=P)
        ups = [psum[:, 2 * j:2 * j + 2, :].rearrange("p b n -> p (b n)") for j in range(2)]

        def over_groups(eng, group):
            group(0, 0)
            group(1, 1)
            with eng.Fori(0, (GROUPS - 3) // 2) as it:
                group(it * 2 + 2, 0)
                group(it * 2 + 3, 1)
            group(GROUPS - 1, (GROUPS - 1) % 2, last=True)

        def is_first(g):
            return isinstance(g, int) and g == 0

        block = ctx.enter_context(nc.Block())

        @block.sync
        def _(sp):
            def group(g, par, last=False):
                for c in range(2):
                    for j in range(2):
                        n = g * 4 + 2 * c + j
                        if is_first(g) and c == 0:
                            continue
                        sp.wait_ge(up_split, n - 1)
                        raws.load(sp, j, up_unit(w_up, j, g * 2 + c))
                if not is_first(g):
                    sp.wait_ge(down_split, g)
                sp.dma_start(down_raw[:, :, :], down_view[:, bass.ds(g * 2, 2), :]).then_inc(down_loaded, 16)

            for k in range(3):
                sp.dma_start(taps_rows[:, k, :], conv_w[k, :].rearrange("(c p) -> c p", p=P)).then_inc(taps_loaded, 16)
            sp.dma_start(taps_rows[:, 3, :], conv_b.rearrange("(c p) -> c p", p=P)).then_inc(taps_loaded, 16)
            if norm:
                sp.dma_start(gain_t[:, :], next_gain.rearrange("(d p) -> p d", p=P), allow_slow_non_contiguous=True).then_inc(gain_loaded, 16)
            over_groups(sp, group)
            for j in range(2 if next_w else 0):
                sp.wait_ge(up_split, 2 * FC)
                raws.load(sp, j, next_w[j])
            for t in range(TT):
                sp.wait_ge(x_added, 2 * TT * (GROUPS - 1) + 2 * t + 2)
                sp.dma_start(x_out[t * P:(t + 1) * P, :], X[:, t, :]).then_inc(stored, 16)
            sp.wait_ge(stored, 16 * TT)

        @block.scalar
        def _(act):
            def high_up(n_slot, n):
                act.wait_ge(up_loaded[n_slot], n * 8 + (loaded_before[n_slot] - 8 * n_slot))
                nc.scalar.activation(up_hi[n_slot][:, :, :], up_raw[n_slot], ACT.Copy).then_inc(up_high, 1)

            def high_down(g):
                act.wait_ge(down_loaded, g * 16 + 16)
                if not is_first(g):
                    act.wait_ge(down_done, g * (2 * TT))
                nc.scalar.activation(down_hi[:, :, :], down_raw[:, :, :], ACT.Copy).then_inc(down_high, 1)

            def high_last_down():
                act.wait_ge(down_loaded, GROUPS * 16)
                for c in range(2):
                    nc.scalar.activation(last_down[0][c], down_raw[:, c, :], ACT.Copy).then_inc(down_high, 1)

            high_up(0, 0)
            high_up(1, 1)
            act.wait_ge(taps_ready, 1)

            def group(g, par, last=False):
                if not is_first(g):
                    high_down(g - 1)
                for c in range(2):
                    for j in range(2):
                        n = g * 4 + 2 * c + j
                        act.wait_ge(up_done, n + 1)
                        if not (last and c):
                            high_up(j, n + 2)
                        if not is_first(g) or c:
                            act.wait_ge(act_split, g * 2 + c)
                        f = g * 2 + (c + j * FC)
                        nc.scalar.activation(conv_out[j][:, :], ups[j], ACT.Identity,
                                             bias=taps[:, 3, bass.ds(f, 1)], scale=taps[:, 2, bass.ds(f, 1)]
                                             ).then_inc(conv_started, 1)
                        if j == 1:
                            act.wait_ge(conv_done, n)
                            nc.scalar.activation(conv_out[0][:, :], conv_out[0][:, :], ACT.Silu).then_inc(gate_done, 1)
                            act.wait_ge(prod_done, g * 2 + (c + 1))
                            if not is_first(g) and not (isinstance(g, int) and g == 1):
                                act.wait_ge(down_done, g * (2 * TT) - 2 * TT)
                            nc.scalar.activation(act_hi[par][:, c, :], conv_out[0][:, :], ACT.Copy).then_inc(act_high, 1)

            over_groups(act, group)
            high_last_down()
            if norm:
                for t in range(TT + LAG):
                    if t < TT:
                        act.wait_ge(x_added, 2 * TT * (GROUPS - 1) + 2 * t + 2)
                        norm.act_square(act, t, X[:, t, :])
                    if t >= LAG:
                        norm.act_high(act, t - LAG)
                    if t < TT:
                        norm.act_scale(act, t, X[:, t, :])

        @block.vector
        def _(dve):
            def low_up(n_slot, n):
                dve.wait_ge(up_high, n + 1)
                nc.vector.tensor_tensor(up_lo[n_slot][:, :, :], up_raw[n_slot],
                                        up_hi[n_slot][:, :, :].bitcast(F32), ALU.subtract).then_inc(up_split, 1)

            def low_down(g):
                dve.wait_ge(down_high, g + 1)
                nc.vector.tensor_tensor(down_lo[:, :, :], down_raw[:, :, :], down_hi[:, :, :].bitcast(F32),
                                        ALU.subtract).then_inc(down_split, 1)

            def low_last_down():
                for c in range(2):
                    dve.wait_ge(down_high, GROUPS + c)
                    nc.vector.tensor_tensor(last_down[1][c], down_raw[:, c, :], last_down[0][c].bitcast(F32), ALU.subtract).then_inc(down_split, 1)

            def add_group(g, banks):
                for i in banks:
                    dve.wait_ge(down_done, g * (2 * TT) + i + 1)
                    xs = X[:, i // 2, (i % 2) * HALF:(i % 2 + 1) * HALF]
                    nc.vector.tensor_tensor(xs, xs, psum[:, 4 + i % 4, :], ALU.add).then_inc(x_added, 1)

            low_up(0, 0)
            low_up(1, 1)
            dve.wait_ge(taps_turned, 1)
            nc.vector.tensor_copy(taps[:, :, :], psum[:, 4, 0:8 * FC].rearrange("p (k f) -> p k f", k=4)).then_inc(taps_ready, 1)
            dve.wait_ge(taps_ready, 1)

            def group(g, par, last=False):
                if not is_first(g):
                    low_down(g - 1)
                for c in range(2):
                    for j in range(2):
                        n = g * 4 + 2 * c + j
                        if not (last and c):
                            low_up(j, n + 2)
                        f = g * 2 + (c + j * FC)
                        y = conv_out[j]
                        dve.wait_ge(conv_started, n + 1)
                        nc.vector.scalar_tensor_tensor(y[:, 1:SEQ], ups[j][:, 0:SEQ - 1], taps[:, 1, bass.ds(f, 1)],
                                                       y[:, 1:SEQ], ALU.mult, ALU.add).then_inc(conv_tap, 1)
                        if c and j and not is_first(g):
                            add_group(g - 1, range(0, 1))
                        dve.wait_ge(conv_tap, n + 1)
                        nc.vector.scalar_tensor_tensor(y[:, 2:SEQ], ups[j][:, 0:SEQ - 2], taps[:, 0, bass.ds(f, 1)],
                                                       y[:, 2:SEQ], ALU.mult, ALU.add).then_inc(conv_done, 1)
                    if c and not is_first(g):
                        add_group(g - 1, range(1, 4))
                    dve.wait_ge(conv_done, g * 4 + 2 * c + 2)
                    dve.wait_ge(gate_done, g * 2 + (c + 1))
                    nc.vector.tensor_tensor(conv_out[0][:, :], conv_out[0][:, :], conv_out[1][:, :],
                                            ALU.mult).then_inc(prod_done, 1)
                    if c and not is_first(g):
                        add_group(g - 1, range(4, 8))
                    dve.wait_ge(prod_done, g * 2 + (c + 1))
                    dve.wait_ge(act_high, g * 2 + (c + 1))
                    nc.vector.tensor_tensor(act_lo[par][:, c, :], conv_out[0][:, :],
                                            act_hi[par][:, c, :].bitcast(F32), ALU.subtract).then_inc(act_split, 1)
                if not is_first(g):
                    add_group(g - 1, range(8, 12))
                    if last:
                        low_last_down()
                    add_group(g - 1, range(12, 2 * TT))

            over_groups(dve, group)
            if norm:
                dve.wait_ge(gain_loaded, 16)
            for t in range(TT + (LAG + 1 if norm else 0)):
                if t < TT:
                    add_group(GROUPS - 1, (2 * t, 2 * t + 1))
                if norm and LAG <= t < TT + LAG:
                    norm.dve_gain(dve, t - LAG)
                if norm and t > LAG:
                    norm.dve_low(dve, t - LAG - 1)

        if norm:
            @block.gpsimd
            def _(pool):
                for t in range(TT):
                    norm.pool(pool, t)

        @block.tensor
        def _(pe):
            def turn_taps():
                pe.wait_ge(taps_loaded, 64)
                for k in range(4):
                    turn = nc.tensor.transpose(psum[:, 4, k * 2 * FC:(k + 1) * 2 * FC], taps_rows[:, k, :],
                                               ident[0:2 * FC, 0:2 * FC])
                turn.then_inc(taps_turned, 1)

            def down_group(g, par, norm=None):
                pe.wait_ge(act_split, g * 2 + 2)
                pe.wait_ge(down_split, g + 1 if not (isinstance(g, int) and g == GROUPS - 1) else GROUPS + 1)
                for i in range(2 * TT):
                    t, half = i // 2, i % 2
                    if not is_first(g) or i >= 4:
                        pe.wait_ge(x_added, g * (2 * TT) + (i - 3))
                    for c in range(2):
                        tok = slice(t * P, (t + 1) * P)
                        cols = slice(half * HALF, (half + 1) * HALF)
                        hi, lo = down_hi[:, c, cols], down_lo[:, c, cols]
                        if isinstance(g, int) and g == GROUPS - 1:
                            hi, lo = (x[c][:, cols] for x in last_down)
                        last = split_matmul(nc, psum[:, 4 + i % 4, :], act_hi[par][:, c, tok], act_lo[par][:, c, tok],
                                            hi, lo, c == 0, c == 1)
                    last.then_inc(down_done, 1)
                    if norm and half and t >= LAG:
                        norm.pe(pe, t - LAG)

            def group(g, par, last=False):
                for c in range(2):
                    for j in range(2):
                        n = g * 4 + 2 * c + j
                        pe.wait_ge(up_split, n + 1)
                        if not is_first(g) or c:
                            pe.wait_ge(conv_done, n - 1)
                        for d in range(DC):
                            for w, h, first, final in ((up_hi, hT_hi, d == 0, False), (up_hi, hT_lo, False, False),
                                                       (up_lo, hT_hi, False, d == DC - 1)):
                                for half in range(2):
                                    mm = nc.tensor.matmul(psum[:, 2 * j + half, :], w[j][:, d, :],
                                                          h[:, d, half * HALF:(half + 1) * HALF],
                                                          start=first, stop=final)
                        mm.then_inc(up_done, 1)
                        if is_first(g) and c == 0 and j == 0:
                            turn_taps()
                if isinstance(g, int) and g == 1:
                    pe.wait_ge(taps_ready, 1)
                if not is_first(g):
                    down_group(g - 1, 1 - par)

            over_groups(pe, group)
            down_group(GROUPS - 1, (GROUPS - 1) % 2, norm)
            if norm:
                for t in range(TT - LAG, TT):
                    norm.pe(pe, t)

        for j in range(2):
            raws.count[j] += 16 * (FC - 1 + (next_w is not None))


EPS = 1e-6
N_MEM = 256
XA_HEADS, XA_DIM = 4, 64
D_XA = XA_HEADS * XA_DIM
D_MIX = 768
GLA_HEADS, GLA_DK, GLA_DV, GLA_RANK = 4, 96, 192, 16
CHUNK = 64
DIL_DIM, DIL_HEADS = 128, 4
D_DIL = DIL_DIM * DIL_HEADS
DILATIONS = (1, 4, 16)
NEG = -1e30


class Norm:

    def __init__(self, nc, ctx, ph, psum, pairs, ident, neg_half, plan, scaled_rows=None, gained_cols=None):
        self.nc, self.psum, self.pairs, self.ident, self.neg_half, self.plan = nc, psum, pairs, ident, neg_half, plan

        def sb(name, shape):
            return ctx.enter_context(nc.sbuf_tensor(f"{ph}_{name}", shape, F32))

        def sem(name):
            return phase_semaphore(nc, ctx, f"{ph}_{name}")

        self.scaled_rows = scaled_rows or [sb(f"scaled_rows{i}", [P, D]) for i in range(2)]
        self.gained_cols = gained_cols or [sb(f"gained_cols{i}", [P, DC, P]) for i in range(1)]
        self.sums = sb("norm_sums", [P, len(plan)])
        self.rstd = sb("norm_rstd", [P, len(plan)])
        self.squared = sem("squared")
        self.mean = sem("mean")
        self.rstd_ready = sem("rstd_ready")
        self.scaled = sem("scaled")
        self.turned = sem("turned")
        self.gained = sem("gained")
        self.high = sem("norm_high")
        self.low = sem("norm_low")

    def act_square(self, act, t, rows):
        if t >= 2:
            act.wait_ge(self.turned, t - 1)
        self.nc.scalar.activation(self.scaled_rows[t % 2][:, :], rows, ACT.Square,
                                  accum_out=self.sums[:, t:t + 1]).then_inc(self.squared, 1)

    def act_scale(self, act, t, rows):
        act.wait_ge(self.rstd_ready, t + 1)
        self.nc.scalar.activation(self.scaled_rows[t % 2][:, :], rows, ACT.Copy, scale=self.rstd[:, t:t + 1]).then_inc(self.scaled, 1)

    def pool(self, pool, t):
        nc, s, r = self.nc, self.sums[:, t:t + 1], self.rstd[:, t:t + 1]
        pool.wait_ge(self.squared, t + 1)
        nc.gpsimd.tensor_scalar(s, s, 1.0 / D, EPS, ALU.mult, ALU.add).then_inc(self.mean, 1)
        pool.wait_ge(self.mean, t + 1)
        nc.gpsimd.tensor_tensor(r, s, self.neg_half[:, 0:1], ALU.pow).then_inc(self.rstd_ready, 1)

    def parts(self, t):
        return [(i, slice(4 * i, 4 * i + 4)) for i in range(2)] if t == len(self.plan) - 1 else [(0, slice(0, DC))]

    def banks(self, t):
        b = self.pairs[t % len(self.pairs)]
        return self.psum[:, b:b + 2, :].rearrange("p b (d n) -> p (b d) n", d=4)

    def cols(self, t):
        return self.gained_cols[t % len(self.gained_cols)]

    def pe(self, pe, t):
        pe.wait_ge(self.scaled, t + 1)
        if t >= len(self.pairs):
            pe.wait_ge(self.gained, t - len(self.pairs) + 1)
        for _, ds in self.parts(t):
            for d in range(ds.start, ds.stop):
                turn = self.nc.tensor.transpose(self.banks(t)[:, d, :], self.scaled_rows[t % 2][:, d * P:(d + 1) * P], self.ident[:, :])
            turn.then_inc(self.turned, 1)

    def dve_gain(self, dve, t):
        n = len(self.gained_cols)
        if t >= n:
            dve.wait_ge(self.low, t - n + 1)
        for i, ds in self.parts(t):
            dve.wait_ge(self.turned, t + 1 + i)
            gain = self.plan[t][2][:, ds].unsqueeze(2)
            self.nc.vector.tensor_tensor(self.cols(t)[:, ds, :], self.banks(t)[:, ds, :],
                                         gain.broadcast_to([P, ds.stop - ds.start, P]), ALU.mult).then_inc(self.gained, 1)

    def act_high(self, act, t):
        for i, ds in self.parts(t):
            act.wait_ge(self.gained, t + 1 + i)
            self.nc.scalar.activation(self.plan[t][0][:, ds, :], self.cols(t)[:, ds, :], ACT.Copy).then_inc(self.high, 1)

    def dve_low(self, dve, t):
        hi, lo = self.plan[t][0:2]
        for i, ds in self.parts(t):
            dve.wait_ge(self.high, t + 1 + i)
            self.nc.vector.tensor_tensor(lo[:, ds, :], self.cols(t)[:, ds, :], hi[:, ds, :].bitcast(F32), ALU.subtract).then_inc(self.low, 1)


def norm_plan(hi, lo, gain_t, tiles=TT):
    return [(hi[:, :, t * P:(t + 1) * P], lo[:, :, t * P:(t + 1) * P], gain_t) for t in range(tiles)]


class OutWeights:

    def __init__(self, nc, ctx, ph, chunks, w_out, raws, ahead):
        def sb(name):
            return ctx.enter_context(nc.sbuf_tensor(f"{ph}_{name}", [P, chunks, D], F32R, side="right"))

        self.nc, self.chunks, self.w, self.raws, self.ahead = nc, chunks, w_out, raws, ahead
        self.hi, self.lo = sb("w_hi"), sb("w_lo")
        self.high, self.split = (phase_semaphore(nc, ctx, f"{ph}_w_{n}") for n in ("high", "split"))
        self.before = list(raws.count)
        for k in range(chunks):
            raws.count[k % 2] += 16

    def load(self, eng, k):
        if k >= 2:
            eng.wait_ge(self.split, k - 1)
        self.raws.load(eng, k % 2, self.w[k * P:(k + 1) * P, :])

    def wait_loaded(self, eng, k):
        eng.wait_ge(self.raws.loaded[k % 2], self.before[k % 2] + 16 * (k // 2 + 1))

    def high_part(self, act, k):
        self.wait_loaded(act, k)
        self.nc.scalar.activation(self.hi[:, k, :], self.raws.tiles[k % 2][:, :], ACT.Copy).then_inc(self.high, 1)

    def low_part(self, dve, k):
        dve.wait_ge(self.high, k + 1)
        self.nc.vector.tensor_tensor(self.lo[:, k, :], self.raws.tiles[k % 2][:, :], self.hi[:, k, :].bitcast(F32),
                                     ALU.subtract).then_inc(self.split, 1)

    def load_ahead(self, sp, k):
        if k < min(self.ahead + 2, self.chunks):
            self.load(sp, k)

    def split_ahead(self, pool):
        for k in range(self.ahead):
            raw = self.raws.tiles[k % 2][:, :]
            self.wait_loaded(pool, k)
            self.nc.gpsimd.tensor_copy(self.hi[:, k, :], raw).then_inc(self.high, 1)
            pool.wait_ge(self.high, k + 1)
            self.nc.gpsimd.tensor_tensor(self.lo[:, k, :], raw, self.hi[:, k, :].bitcast(F32), ALU.subtract).then_inc(self.split, 1)


def out_phase(nc, ph, psum, ident, neg_half, XY, weights, x_dram, gain, out_hi, out_lo, w_up, stage=None):
    chunks, raws, w_split = weights.chunks, weights.raws, weights.split
    with ExitStack() as ctx:
        ctx.callback(nc.all_engine_barrier)
        def sb(name, shape, dt=F32):
            return ctx.enter_context(nc.sbuf_tensor(f"{ph}_{name}", shape, dt))

        def sem(name):
            return phase_semaphore(nc, ctx, f"{ph}_{name}")

        w_hi, w_lo = weights.hi, weights.lo
        y_hi = [sb(f"y_hi{i}", [P, chunks, P], F32R) for i in range(2)]
        y_lo = [sb(f"y_lo{i}", [P, chunks, P], F32R) for i in range(2)]
        x_old = sb("x_old", [P, D])
        gain_t = sb("gain", [P, DC])
        gain_loaded = sem("gain_loaded")
        x_loaded = sem("x_loaded")
        y_turned = sem("y_turned")
        y_high, y_split = sem("y_high"), sem("y_split")
        summed = sem("summed")
        x_ready = sem("x_ready")
        norm = Norm(nc, ctx, ph, psum, (4, 6), ident, neg_half, norm_plan(out_hi, out_lo, gain_t))
        merge = Merge(nc, ctx, ph, stage, XY) if stage is not None else None
        block = ctx.enter_context(nc.Block())

        @block.sync
        def _(sp):
            for k in range(weights.ahead + 2, chunks - 1 if merge else chunks):
                weights.load(sp, k)
            if merge:
                stage.wait_logs(sp)
                merge.load_logs(sp)
                stage.wait_outputs(sp)
                merge.load(sp, 0)
                for k in range(max(weights.ahead + 2, chunks - 1), chunks):
                    weights.load(sp, k)
                merge.load(sp, 1)
            for j in range(2):
                sp.wait_ge(w_split, chunks)
                raws.load(sp, j, up_unit(w_up, j, 0))
            for t in range(TT):
                if merge and t + 2 < TT:
                    merge.load(sp, t + 2)
                if t >= 1:
                    sp.wait_ge(x_ready, 2 * t)
                sp.dma_start(x_old[:, :], x_dram[t * P:(t + 1) * P, :]).then_inc(x_loaded, 16)

        def y_cols(t):
            b = 2 * (t % 2)
            return psum[:, b:b + 2, :].rearrange("p b (d n) -> p (b d) n", d=4)[:, 0:chunks, :]

        @block.scalar
        def _(act):
            act.dma_start(gain_t[:, :], gain.rearrange("(d p) -> p d", p=P), allow_slow_non_contiguous=True).then_inc(gain_loaded, 16)

            def y_part(t):
                act.wait_ge(y_turned, t + 1)
                if t >= 2:
                    act.wait_ge(summed, 2 * t - 2)
                nc.scalar.activation(y_hi[t % 2][:, :, :], y_cols(t), ACT.Copy).then_inc(y_high, 1)

            if merge:
                for k in range(weights.ahead, chunks - 1):
                    weights.high_part(act, k)
                merge.act_exp(act)
            y_part(0)
            for k in range(chunks - 1 if merge else weights.ahead, chunks):
                weights.high_part(act, k)
            for t in range(TT):
                if t + 1 < TT:
                    y_part(t + 1)
                act.wait_ge(x_ready, 2 * t + 2)
                norm.act_square(act, t, XY[:, t, :])
                norm.act_scale(act, t, XY[:, t, :])
                if t >= 1:
                    norm.act_high(act, t - 1)
            norm.act_high(act, TT - 1)

        @block.gpsimd
        def _(pool):
            for t in range(TT):
                norm.pool(pool, t)

        @block.vector
        def _(dve):
            dve.wait_ge(gain_loaded, 16)

            def y_part(t):
                dve.wait_ge(y_high, t + 1)
                nc.vector.tensor_tensor(y_lo[t % 2][:, :, :], y_cols(t), y_hi[t % 2][:, :, :].bitcast(F32), ALU.subtract).then_inc(y_split, 1)

            if merge:
                for k in range(weights.ahead, chunks - 1):
                    weights.low_part(dve, k)
                merge.dve_weights(dve)
                merge.dve_add(dve, 0)
            y_part(0)
            for k in range(chunks - 1 if merge else weights.ahead, chunks):
                weights.low_part(dve, k)
            if merge:
                merge.dve_add(dve, 1)
            for t in range(TT):
                dve.wait_ge(x_loaded, 16 * (t + 1))
                for half in range(2):
                    if half and t + 1 < TT:
                        y_part(t + 1)
                    cols = slice(half * HALF, (half + 1) * HALF)
                    dve.wait_ge(summed, 2 * t + half + 1)
                    nc.vector.tensor_tensor(XY[:, t, cols], psum[:, 2 * (t % 2) + half, :], x_old[:, cols], ALU.add).then_inc(x_ready, 1)
                if merge and t + 2 < TT:
                    merge.dve_add(dve, t + 2)
                if t >= 1:
                    norm.dve_gain(dve, t - 1)
                    norm.dve_low(dve, t - 1)
            norm.dve_gain(dve, TT - 1)
            norm.dve_low(dve, TT - 1)

        @block.tensor
        def _(pe):
            def y_turn(t):
                if merge:
                    pe.wait_ge(merge.added, t + 1)
                if t >= 2:
                    pe.wait_ge(x_ready, 2 * t - 2)
                for k in range(chunks):
                    turn = nc.tensor.transpose(psum[:, 2 * (t % 2) + k // 4, (k % 4) * P:(k % 4 + 1) * P],
                                               XY[:, t, k * P:(k + 1) * P], ident[:, :])
                turn.then_inc(y_turned, 1)

            y_turn(0)
            for t in range(TT):
                pe.wait_ge(y_split, t + 1)
                for half in range(2):
                    if half and t + 1 < TT:
                        y_turn(t + 1)
                    cols = slice(half * HALF, (half + 1) * HALF)
                    for k in range(chunks):
                        if t == 0 and half == 0:
                            pe.wait_ge(w_split, k + 1)
                        last = split_matmul(nc, psum[:, 2 * (t % 2) + half, :], y_hi[t % 2][:, k, :], y_lo[t % 2][:, k, :],
                                            w_hi[:, k, cols], w_lo[:, k, cols], k == 0, k == chunks - 1)
                    last.then_inc(summed, 1)
                if t >= 1:
                    norm.pe(pe, t - 1)
            norm.pe(pe, TT - 1)

        for j in range(2):
            raws.count[j] += 16


def half_rows(w, kh):
    half = DC // 2
    return w.rearrange("(d p) n -> p d n", p=P)[:, kh * half:(kh + 1) * half, :]


class WeightSlots:

    def __init__(self, nc, ctx, name, width, early=None):
        def sb(n, dt=F32):
            return [ctx.enter_context(nc.sbuf_tensor(f"{name}_{n}{i}", [P, DC // 2, width], dt, side="right")) for i in range(2)]

        self.nc = nc
        self.raw, self.hi, self.lo = sb("raw"), sb("hi", F32R), sb("lo", F32R)
        self.loaded = [phase_semaphore(nc, ctx, f"{name}_loaded{i}") for i in range(2)]
        self.high = phase_semaphore(nc, ctx, f"{name}_high")
        self.split = phase_semaphore(nc, ctx, f"{name}_split")
        self.base = 0
        self.ahead = 0
        self.early = early

    def load(self, sp, s, w):
        S, kh = self.base + s, s % 2
        if S < 2 and self.early:
            return
        if S >= 2:
            sp.wait_ge(self.split, S - 1)
        sp.dma_start(self.raw[kh][:, :, 0:w.shape[1]], half_rows(w, kh)).then_inc(self.loaded[kh], 16)

    def wait_loaded(self, eng, s):
        S = self.base + s
        if S < 2 and self.early:
            eng.wait_ge(self.early.loaded[S], self.early.count[S])
        else:
            eng.wait_ge(self.loaded[s % 2], 16 * (S // 2 + (0 if self.early else 1)))

    def parts(self, s, w):
        if self.base + s < 2 and self.early:
            raw = self.early.tiles[s][:, :].rearrange("p (d n) -> p d n", d=DC // 2)
            return raw, self.hi[s][:, :, 0:w.shape[1]], self.lo[s][:, :, 0:w.shape[1]]
        return (x[s % 2][:, :, 0:w.shape[1]] for x in (self.raw, self.hi, self.lo))

    def high_part(self, act, s, w):
        raw, hi, _ = self.parts(s, w)
        self.wait_loaded(act, s)
        self.nc.scalar.activation(hi, raw, ACT.Copy).then_inc(self.high, 1)

    def low_part(self, dve, s, w):
        raw, hi, lo = self.parts(s, w)
        dve.wait_ge(self.high, self.base + s + 1)
        self.nc.vector.tensor_tensor(lo, raw, hi.bitcast(F32), ALU.subtract).then_inc(self.split, 1)


class SlotsAhead:

    def __init__(self, slots, w):
        self.slots, self.w = slots, w

    def load_ahead(self, sp, s):
        if s < 2:
            self.slots.load(sp, s, self.w)

    def split_ahead(self, pool):
        slots, nc = self.slots, self.slots.nc
        for s in range(2):
            raw, hi, lo = slots.parts(s, self.w)
            slots.wait_loaded(pool, s)
            nc.gpsimd.tensor_copy(hi, raw).then_inc(slots.high, 1)
            pool.wait_ge(slots.high, slots.base + s + 1)
            nc.gpsimd.tensor_tensor(lo, raw, hi.bitcast(F32), ALU.subtract).then_inc(slots.split, 1)
        slots.ahead = 2


def project_phase(nc, ph, psum, ident, neg_half, blocks, slots, extra_loads=(), guest=None, saves=None,
                  room=None):
    half_d = DC // 2
    all_groups, first_tile, first_group = [], [], []
    freed, count = [], {"act": 0, "dve": 0}
    heads_before = []
    n_heads = 0
    for b, blk in enumerate(blocks):
        first_tile.append(len(freed))
        first_group.append(len(all_groups))
        all_groups += [(b, list(range(t, min(t + 3, blk["tiles"])))) for t in range(0, blk["tiles"], 3)]
        for t in range(blk["tiles"]):
            who = "dve" if blk["kind"] == "heads" else "act"
            count[who] += 1
            freed.append((who, count[who]))
            heads_before.append(n_heads)
            n_heads += blk["kind"] == "heads"

    with ExitStack() as ctx:
        ctx.callback(nc.all_engine_barrier)
        def sb(name, shape, dt=F32):
            return ctx.enter_context(nc.sbuf_tensor(f"{ph}_{name}", shape, dt))

        def sem(name):
            return phase_semaphore(nc, ctx, f"{ph}_{name}")

        w_hi, w_lo, base, ahead = slots.hi, slots.lo, slots.base, slots.ahead
        weights = [b["w"] for b in blocks]
        extra_loaded, saved = sem("extra_loaded"), sem("saved")
        first_read = sem("first_read")
        done = sem("done")
        gate_gained = sem("gate_gained")
        if n_heads:
            hw = max(b["w"].shape[1] for b in blocks if b["kind"] == "heads")
            squares = sb("squares", [P, 2, hw]) if room is None else room[0][:, :].rearrange("p (two n) -> p two n", two=2)
            sums = sb("head_sums", [P, 2, 4])
            rstd = sb("head_rstd", [P, 2, 4])
            rows = sb("head_rows", [P, hw]) if room is None else room[1][:, 0:HALF]
            roped = [sb(f"head_roped{i}", [P, hw]) for i in range(3)]
            cross = sb("rope_cross", [P, hw]) if room is None else room[1][:, HALF:]
        squared, mean, rstd_ready = sem("squared"), sem("mean"), sem("rstd_ready")
        rows_ready, link = sem("rows_ready"), sem("rope_link")
        turned, turn_out = sem("turned"), sem("turn_out")
        free = {"act": sem("freed_by_act"), "dve": rows_ready}

        def bank_of(b, t):
            return 3 * ((first_group[b] + t // 3) % 2) + t % 3

        def groups_of(b):
            return [(ts, ts[-1] + 1 == blocks[b]["tiles"]) for bb, ts in all_groups if bb == b]

        block = ctx.enter_context(nc.Block())

        @block.sync
        def _(sp):
            for s in range(ahead, 2 * len(weights)):
                if s == 2:
                    for out, src in extra_loads:
                        sp.dma_start(out, src).then_inc(extra_loaded, 16)
                if guest:
                    guest.load(sp, s)
                slots.load(sp, s, weights[s // 2])
            if guest:
                guest.store(sp)
            if saves:
                upto = first_tile[saves[0] + 1]
                sp.wait_ge(free["act"], max(v for who, v in freed[:upto] if who == "act"))
                sp.wait_ge(turn_out, heads_before[upto])
                for out, src in saves[1]:
                    sp.dma_start(out, src).then_inc(saved, 16)
                sp.wait_ge(saved, 16 * len(saves[1]))

        def slots_free(eng, s):
            b, kh = divmod(s, 2)
            if b >= 1:
                if kh == 0:
                    eng.wait_ge(first_read, b)
                else:
                    eng.wait_ge(done, first_tile[b])

        def over_tiles(split, tile, turn, visit):
            for s in range(ahead, 2):
                split(s)
            before = []
            for b in range(len(blocks)):
                for group, last in groups_of(b):
                    for bt in before[:2]:
                        turn(*bt)
                    if last and b + 1 < len(blocks):
                        split(2 * b + 2)
                    for bt in before[2:]:
                        turn(*bt)
                    for t in group:
                        tile(b, t)
                    if last and b + 1 < len(blocks):
                        split(2 * b + 3)
                    before = [(b, t) for t in group]
                visit(b)
            for bt in before:
                turn(*bt)

        @block.scalar
        def _(act):
            def split(s):
                slots_free(act, s)
                slots.high_part(act, s, weights[s // 2])

            def tile(b, t):
                blk, T = blocks[b], first_tile[b] + t
                n = blk["w"].shape[1]
                acc = psum[:, bank_of(b, t), 0:n]
                act.wait_ge(done, T + 1)
                if blk["kind"] == "heads":
                    H, dim = heads_before[T], blk["dim"]
                    if H >= 2:
                        act.wait_ge(rows_ready, H - 1)
                    for h in range(n // dim):
                        nc.scalar.activation(squares[:, H % 2, h * dim:(h + 1) * dim], acc[:, h * dim:(h + 1) * dim], ACT.Square,
                                             accum_out=sums[:, H % 2, h:h + 1]).then_inc(squared, 1)
                else:
                    nc.scalar.activation(blk["dest"](t), acc, ACT.Silu if blk["kind"] == "gate" else ACT.Copy).then_inc(free["act"], 1)

            def turn(b, t):
                blk, T = blocks[b], first_tile[b] + t
                if blk["kind"] != "heads":
                    return
                H, n = heads_before[T], blk["w"].shape[1]
                act.wait_ge(turned, H + 1)
                for dst, src in blk["dest"](t, psum[:, 6 + H % 2, 0:n]):
                    ins = nc.scalar.activation(dst, src, ACT.Copy)
                ins.then_inc(turn_out, 1)

            over_tiles(split, tile, turn, lambda k: guest and guest.act(act, k))

        @block.gpsimd
        def _(pool):
            n_sq = 0
            for b, blk in enumerate(blocks):
                for t in range(blk["tiles"] if blk["kind"] == "heads" else 0):
                    H, nh, dim = heads_before[first_tile[b] + t], blk["w"].shape[1] // blk["dim"], blk["dim"]
                    n_sq += nh
                    s, r = sums[:, H % 2, 0:nh], rstd[:, H % 2, 0:nh]
                    pool.wait_ge(squared, n_sq)
                    if H >= 2:
                        pool.wait_ge(rows_ready, H - 1)
                    nc.gpsimd.tensor_scalar(s, s, 1.0 / dim, EPS, ALU.mult, ALU.add).then_inc(mean, 1)
                    pool.wait_ge(mean, H + 1)
                    nc.gpsimd.tensor_tensor(r, s, neg_half[:, 0:nh], ALU.pow).then_inc(rstd_ready, 1)

        @block.vector
        def _(dve):
            links = [0]

            def split(s):
                slots.low_part(dve, s, weights[s // 2])

            def tile(b, t):
                blk, T = blocks[b], first_tile[b] + t
                n = blk["w"].shape[1]
                acc = psum[:, bank_of(b, t), 0:n]
                if blk["kind"] == "gate":
                    dve.wait_ge(free["act"], freed[T][1])
                    out = blk["dest"](t).rearrange("p (h v) -> p h v", v=GLA_DV)
                    nc.vector.tensor_tensor(out, out, blk["gain"].unsqueeze(1).broadcast_to([P, n // GLA_DV, GLA_DV]),
                                            ALU.mult).then_inc(gate_gained, 1)
                if blk["kind"] != "heads":
                    return
                H, dim = heads_before[T], blk["dim"]
                nh, buf = n // dim, rows if blk.get("rope") else roped[H % 3]
                dve.wait_ge(rstd_ready, H + 1)
                if H >= 3:
                    dve.wait_ge(turned, H - 2)
                for h in range(nh):
                    cols = slice(h * dim, (h + 1) * dim)
                    ins = nc.vector.scalar_tensor_tensor(buf[:, cols], acc[:, cols], rstd[:, H % 2, h:h + 1],
                                                         blk["gain"], ALU.mult, ALU.mult)
                if not blk.get("rope"):
                    ins.then_inc(rows_ready, 1)
                    return
                links[0] += 1
                ins.then_inc(link, 1)
                dve.wait_ge(link, links[0])
                half = dim // 2
                if extra_loads and links[0] == 1:
                    dve.wait_ge(extra_loaded, 16 * len(extra_loads))
                cos, sin = (x[:, t, :].unsqueeze(1).broadcast_to([P, nh, half]) for x in blk["rope"])
                x = buf[:, 0:n].rearrange("p (h two k) -> p h two k", two=2, k=half)
                o = roped[H % 3][:, 0:n].rearrange("p (h two k) -> p h two k", two=2, k=half)
                c = cross[:, 0:n].rearrange("p (h two k) -> p h two k", two=2, k=half)
                for two in range(2):
                    nc.vector.tensor_tensor(o[:, :, two, :], x[:, :, two, :], cos, ALU.mult)
                    ins = nc.vector.tensor_tensor(c[:, :, two, :], x[:, :, 1 - two, :], sin, ALU.mult)
                links[0] += 1
                ins.then_inc(link, 1)
                dve.wait_ge(link, links[0])
                nc.vector.tensor_tensor(o[:, :, 0, :], o[:, :, 0, :], c[:, :, 0, :], ALU.subtract)
                nc.vector.tensor_tensor(o[:, :, 1, :], o[:, :, 1, :], c[:, :, 1, :], ALU.add).then_inc(rows_ready, 1)

            over_tiles(split, tile, lambda b, t: None, lambda k: guest and guest.dve(dve, k))

        @block.tensor
        def _(pe):
            before = []

            def turns(group):
                for b, t in group:
                    blk, T = blocks[b], first_tile[b] + t
                    if blk["kind"] != "heads":
                        continue
                    H, n = heads_before[T], blk["w"].shape[1]
                    pe.wait_ge(rows_ready, H + 1)
                    if H >= 2:
                        pe.wait_ge(turn_out, H - 1)
                    for i in range(n // P):
                        ins = nc.tensor.transpose(psum[:, 6 + H % 2, i * P:(i + 1) * P],
                                                  roped[H % 3][:, i * P:(i + 1) * P], ident[:, :])
                    ins.then_inc(turned, 1)

            for b, blk in enumerate(blocks):
                n = blk["w"].shape[1]
                for g, (group, last_group) in enumerate(groups_of(b)):
                    G = first_group[b] + g
                    if G >= 2:
                        b2, tiles2 = all_groups[G - 2]
                        for who in ("act", "dve"):
                            upto = [v for w, v in freed[:first_tile[b2] + tiles2[-1] + 1] if w == who]
                            if upto:
                                pe.wait_ge(free[who], upto[-1])
                    for kh in range(2):
                        pe.wait_ge(slots.split, base + 2 * b + kh + 1)
                        for t in group:
                            for d in range(half_d):
                                dd = kh * half_d + d
                                last = split_matmul(nc, psum[:, bank_of(b, t), 0:n],
                                                    blk["pick"](blk["stat"][0], dd, t), blk["pick"](blk["stat"][1], dd, t),
                                                    w_hi[kh][:, d, 0:n], w_lo[kh][:, d, 0:n], dd == 0, dd == DC - 1)
                            if kh == 1:
                                last.then_inc(done, 1)
                                if t == group[0]:
                                    turns(before[2:])
                        if kh == 0 and last_group:
                            last.then_inc(first_read, 1)
                        if kh == 0:
                            turns(before[:2])
                    before[:] = [(b, t) for t in group]
            turns(before)

        slots.base += 2 * len(blocks)
        slots.ahead = 0


def attention_phase(nc, ph, psum, ident, units, stage=None, loads=(), load_unit=0, ahead=None, room=()):
    U = len(units)
    staged = TT * DIL_HEADS if stage is not None else 0
    with ExitStack() as ctx:
        ctx.callback(nc.all_engine_barrier)
        def sb(name, shape, dt=F32):
            return ctx.enter_context(nc.sbuf_tensor(f"{ph}_{name}", shape, dt))

        def sem(name):
            return phase_semaphore(nc, ctx, f"{ph}_{name}")

        S, T, O = 3, 2, 2
        spare = [x[:, i * 2 * P:(i + 1) * 2 * P] for x in room for i in range(D // (2 * P))]
        buffers = [spare[i] if i < len(spare) else sb(f"buffer{i}", [P, 2 * P])[:, :] for i in range(9)]
        masked, probs, probs_t = buffers[0:3], buffers[3:6], buffers[6:9]
        neg_top = sb("neg_top", [P, U])
        total = sb("total", [P, U])
        inv = sb("inv", [P, U])
        scored = sem("scored")
        topped = sem("topped")
        expd = sem("expd")
        turned = sem("turned")
        turn_out = sem("turn_out")
        mixed = sem("mixed")
        inverted = sem("inverted")
        out_done = sem("out_done")
        logged, lse_done = sem("logged"), sem("lse_done")
        loaded = sem("loaded")
        block = ctx.enter_context(nc.Block())
        T_LAG, O_LAG = 2, 3

        @block.tensor
        def _(pe):
            for i in range(U + O_LAG):
                if i < U:
                    q, k, n = units[i][0:3]
                    if loads and i == load_unit:
                        pe.wait_ge(loaded, 16 * len(loads))
                    if i >= S:
                        pe.wait_ge(topped, i - S + 1)
                    nc.tensor.matmul(psum[:, i % S, 0:n], q, k, start=True, stop=True).then_inc(scored, 1)
                u = i - T_LAG
                if 0 <= u < U:
                    n = units[u][2]
                    pe.wait_ge(expd, u + 1)
                    if u >= T:
                        pe.wait_ge(turn_out, u - T + 1)
                    for c in range(n // P):
                        ins = nc.tensor.transpose(psum[:, S + u % T, c * P:(c + 1) * P], probs[u % 3][:, c * P:(c + 1) * P], ident[:, :])
                    ins.then_inc(turned, 1)
                u = i - O_LAG
                if 0 <= u < U:
                    n, vals = units[u][2], units[u][4]
                    pe.wait_ge(turn_out, u + 1)
                    if u >= O:
                        pe.wait_ge(out_done, u - O + 1)
                    for c, v in enumerate(vals):
                        ins = nc.tensor.matmul(psum[:, S + T + u % O, 0:v.shape[-1]], probs_t[u % 3][:, c * P:(c + 1) * P], v,
                                               start=c == 0, stop=c == len(vals) - 1)
                    ins.then_inc(mixed, 1)

        @block.vector
        def _(dve):
            for i in range(U + O_LAG):
                if i < U:
                    n, mask, scale = units[i][2], units[i][3], units[i][6]
                    dve.wait_ge(scored, i + 1)
                    if i >= 3:
                        dve.wait_ge(expd, i - 2)
                    nc.vector.tensor_tensor_reduce(masked[i % 3][:, 0:n], psum[:, i % S, 0:n], mask, -scale, 3e38,
                                                   ALU.add, ALU.min, neg_top[:, i:i + 1]).then_inc(topped, 1)
                u = i - T_LAG
                if 0 <= u < U:
                    n = units[u][2]
                    dve.wait_ge(turned, u + 1)
                    if u >= 3:
                        dve.wait_ge(mixed, u - 2)
                    nc.vector.tensor_copy(probs_t[u % 3][:, 0:n], psum[:, S + u % T, 0:n]).then_inc(turn_out, 1)
                    nc.vector.reciprocal(inv[:, u:u + 1], total[:, u:u + 1]).then_inc(inverted, 1)
                if i == staged + T_LAG and staged:
                    dve.wait_ge(logged, 1)
                    nc.vector.tensor_tensor(stage.lse[:, :], total[:, 0:staged], neg_top[:, 0:staged], ALU.subtract).then_inc(lse_done, 1)

        @block.scalar
        def _(act):
            for i in range(U + O_LAG):
                if i < U:
                    n = units[i][2]
                    act.wait_ge(topped, i + 1)
                    if i >= 3:
                        act.wait_ge(turned, i - 2)
                    nc.scalar.activation(probs[i % 3][:, 0:n], masked[i % 3][:, 0:n], ACT.Exp, bias=neg_top[:, i:i + 1],
                                         scale=-1.0, accum_out=total[:, i:i + 1]).then_inc(expd, 1)
                u = i - O_LAG
                if 0 <= u < U:
                    w, out = units[u][4][0].shape[-1], units[u][5]
                    act.wait_ge(mixed, u + 1)
                    act.wait_ge(inverted, u + 1)
                    if u < staged and u % 4 == 0 and stage.before(u // 4):
                        act.wait_ge(stage.stored[u // 4 % 2], stage.before(u // 4))
                    nc.scalar.activation(out, psum[:, S + T + u % O, 0:w], ACT.Copy, scale=inv[:, u:u + 1]).then_inc(out_done, 1)
                if i == staged + T_LAG - 1 and staged:
                    act.wait_ge(inverted, staged)
                    nc.scalar.activation(total[:, 0:staged], total[:, 0:staged], ACT.Ln).then_inc(logged, 1)

        @block.sync
        def _(sp):
            for out, src in loads:
                sp.dma_start(out, src).then_inc(loaded, 16)
            if ahead is not None:
                for k in range(2 if staged else DC):
                    ahead.load_ahead(sp, k)
            if staged:
                for t in range(TT):
                    sp.wait_ge(out_done, 4 * t + 4)
                    stage.store(sp, t)
                    if ahead is not None and t % 2 == 1:
                        ahead.load_ahead(sp, 2 + t // 2)
                sp.wait_ge(lse_done, 1)
                stage.store_lse(sp)

        if ahead is not None:
            @block.gpsimd
            def _(pool):
                ahead.split_ahead(pool)

        if staged:
            stage.groups += 1


def gla_phase(nc, ph, psum, ident, neg_half, hT_hi, hT_lo, w_in, w_gate2, b_gate, V, Y, room, kv_room, kv_loads):
    DK, DV, PAIRS, CH = GLA_DK, GLA_DV, SEQ // P, SEQ // CHUNK
    QK = 2 * DK
    with ExitStack() as ctx:
        ctx.callback(nc.all_engine_barrier)
        def sb(name, shape, dt=F32):
            return ctx.enter_context(nc.sbuf_tensor(f"{ph}_{name}", shape, dt))

        def sem(name):
            return phase_semaphore(nc, ctx, f"{ph}_{name}")

        w_raw = kv_room[:, :].rearrange("p (d n) -> p d n", d=DC)
        w_hi, w_lo = sb("w_hi", [P, DC, QK], F32R), sb("w_lo", [P, DC, QK], F32R)
        rank = sb("rank", [GLA_RANK, SEQ])
        gate2 = sb("gate2", [GLA_RANK, GLA_HEADS * DK])
        bias = sb("bias", [DK, GLA_HEADS])
        keep = sb("keep", [DK, SEQ])
        z = room[0][0:DK, :]
        soft = sb("soft", [DK, SEQ])
        cum = room[1][0:DK, :]
        from_mid, to_last = soft, z
        q_mid, k_mid = sb("q_mid", [DK, SEQ]), sb("k_mid", [DK, SEQ])
        q_in, k_out = sb("q_in", [DK, SEQ]), sb("k_out", [DK, SEQ])
        chunk_decay = sb("chunk_decay", [DK, CH])
        decay = sb("decay", [DK, PAIRS])
        att = sb("att", [P, PAIRS, P])
        k_rows = sb("k_rows", [P, PAIRS, DK])
        state = sb("state", [DK, PAIRS, DV])
        squares = sb("squares", [P, 2, DV])
        sums, rstd = sb("sums", [P, PAIRS]), sb("rstd", [P, PAIRS])

        small_loaded = sem("small_loaded")
        w_loaded, w_high, w_split = sem("w_loaded"), sem("w_high"), sem("w_split")
        kv_loaded, kept = sem("kv_loaded"), sem("kept")
        projected = sem("projected")
        rank_ready = sem("rank_ready")
        copied = sem("copied")
        z_ready = sem("z_ready")
        softened = sem("softened")
        act_link, link = sem("act_link"), sem("dve_link")
        shifted = sem("shifted")
        expd = sem("expd")
        timed = sem("timed")
        factored = sem("factored")
        mixed = sem("mixed")
        masked = sem("masked")
        state_ready = sem("state_ready")
        squared, mean, rstd_ready = sem("squared"), sem("mean"), sem("rstd_ready")
        by_act, by_dve = sem("ring_freed_by_act"), sem("ring_freed_by_dve")

        PER_HEAD = [("att", "act")] * 2 + [("cross", "dve")] + [("keys", "act")] * 2 + [("delta", "state")] * 4 + [("out", "dve")] * 4
        ring = [("z", "act")] * 2
        q_sb, k_sb = (Y[0:DK, :, D_MIX + i * P:D_MIX + (i + 1) * P] for i in range(2))
        first_of, z_of = [], [0]
        for h in range(GLA_HEADS):
            if h + 1 < GLA_HEADS:
                z_of.append(len(ring))
                ring += [("z", "act")] * 2
            first_of.append(len(ring))
            ring += PER_HEAD

        def freed(i):
            kind, who = ring[i]
            if kind == "delta":
                h = max(h for h in range(GLA_HEADS) if first_of[h] <= i)
                return state_ready, (PAIRS - 1) * h + min(2 * (i - first_of[h] - 5) + 2, PAIRS - 1)
            return (by_act if who == "act" else by_dve), sum(w == who for _, w in ring[:i + 1])

        def bank(i):
            return psum[:, 4 + i % 4, :]

        def raw_of(s):
            return Y[:, :, D_MIX:D_MIX + P] if s == 0 else w_raw[:, :, :]

        def mixes_before(i):
            return sum(kind != "z" for kind, _ in ring[:i])

        block = ctx.enter_context(nc.Block())
        w_view = w_in.rearrange("(d p) n -> p d n", p=P)

        @block.sync
        def _(sp):
            sp.dma_start(gate2[:, :], w_gate2).then_inc(small_loaded, 16)
            sp.dma_start(bias[:, :], b_gate.rearrange("(h k) -> k h", k=DK), allow_slow_non_contiguous=True).then_inc(small_loaded, 16)
            for h in range(GLA_HEADS):
                if h:
                    sp.wait_ge(w_split, h + 1)
                for part in range(2):
                    sp.dma_start(w_raw[:, :, part * DK:(part + 1) * DK],
                                 w_view[:, :, (part * GLA_HEADS + h) * DK:(part * GLA_HEADS + h + 1) * DK]).then_inc(w_loaded, 16)
            sp.wait_ge(w_split, GLA_HEADS + 1)
            for dst, src in kv_loads:
                sp.dma_start(dst, src).then_inc(kv_loaded, 16)
            sp.wait_ge(kv_loaded, 16 * len(kv_loads))

        @block.gpsimd
        def _(pool):
            nc.gpsimd.memset(keep[:, :], 1.0).then_inc(kept, 1)
            pool.wait_ge(kept, 1)
            nc.gpsimd.memset(keep[:, :].rearrange("p (c i) -> p c i", i=CHUNK)[:, :, 0:1], 0.0).then_inc(kept, 1)
            for h in range(GLA_HEADS):
                pool.wait_ge(*freed(first_of[h] + 1))
                pool.wait_ge(*freed(first_of[h] + 2))
                nc.gpsimd.affine_select(out=att[:, :, :], in_=att[:, :, :], compare_op=ALU.is_ge, fill=0.0, base=0,
                                        pattern=[[0, PAIRS], [1, P]], channel_multiplier=-1).then_inc(masked, 1)
                for half in range(2):
                    ps = slice(half * PAIRS // 2, (half + 1) * PAIRS // 2)
                    pool.wait_ge(squared, PAIRS * h + ps.stop)
                    nc.gpsimd.tensor_scalar(sums[:, ps], sums[:, ps], 1.0 / DV, EPS, ALU.mult, ALU.add).then_inc(mean, 1)
                    pool.wait_ge(mean, 2 * h + half + 1)
                    nc.gpsimd.tensor_tensor(rstd[:, ps], sums[:, ps], neg_half[:, ps], ALU.pow).then_inc(rstd_ready, 1)

        @block.scalar
        def _(act):
            links = [0]

            def high(s):
                if s:
                    act.wait_ge(w_loaded, 32 * s)
                    act.wait_ge(projected, 2 * s - 1)
                n = P if s == 0 else QK
                nc.scalar.activation(w_hi[:, :, 0:n], raw_of(s), ACT.Copy).then_inc(w_high, 1)

            def copy(h, i):
                act.wait_ge(projected, 2 * h + 2 + i)
                if h:
                    act.wait_ge(timed, 4 * h - i)
                nc.scalar.activation((q_sb, k_sb)[i], psum[0:DK, 2 * i:2 * i + 2, :].rearrange("p b (c n) -> p (b c) n", n=P),
                                     ACT.Copy).then_inc(copied, 1)

            def gate(h):
                if h:
                    act.wait_ge(expd, 4 * h)
                for half in range(2):
                    cols, src = slice(half * HALF, (half + 1) * HALF), bank(z_of[h] + half)[0:DK, :]
                    act.wait_ge(z_ready, 2 * h + half + 1)
                    nc.scalar.activation(z[:, cols], src, ACT.Identity, bias=bias[:, h:h + 1])
                    nc.scalar.activation(soft[:, cols], src, ACT.Abs, bias=bias[:, h:h + 1]).then_inc(by_act, 1)
                act.wait_ge(by_act, freed(z_of[h] + 1)[1])
                nc.scalar.activation(soft[:, :], soft[:, :], ACT.Exp, scale=-1.0).then_inc(act_link, 1)
                links[0] += 1
                act.wait_ge(act_link, links[0])
                nc.scalar.activation(soft[:, :], soft[:, :], ACT.Ln, bias=1.0).then_inc(softened, 1)

            def factor(h, i):
                out, src, s, entries = ((q_mid, from_mid, 1, 2), (k_mid, from_mid, -1, 2), (k_out, to_last, 1, 5), (q_in, cum, 1, 13))[i]
                act.wait_ge(shifted, h + 1)
                if h:
                    act.wait_ge(mixed, mixes_before(first_of[h - 1] + entries))
                nc.scalar.activation(out[:, :], src[:, :], ACT.Exp, scale=s / 16.0).then_inc(expd, 1)

            high(0)
            act.wait_ge(projected, 1)
            act.wait_ge(small_loaded, 32)
            for half in range(2):
                nc.scalar.activation(rank[:, half * HALF:(half + 1) * HALF], psum[0:GLA_RANK, half, :], ACT.Copy).then_inc(rank_ready, 1)
            high(1)
            gate(0)
            for i in range(4):
                factor(0, i)
            copy(0, 0)
            copy(0, 1)
            high(2)
            for h in range(GLA_HEADS):
                f, more = first_of[h], h + 1 < GLA_HEADS
                if more:
                    gate(h + 1)
                if h:
                    act.wait_ge(mixed, mixes_before(f))
                for i in range(2):
                    act.wait_ge(mixed, mixes_before(f + i) + 1)
                    nc.scalar.activation(att[:, 4 * i:4 * i + 4, :], bank(f + i).rearrange("p (c n) -> p c n", n=P), ACT.Copy).then_inc(by_act, 1)
                if more:
                    factor(h + 1, 0)
                    factor(h + 1, 1)
                    copy(h + 1, 0)
                for i in range(2):
                    act.wait_ge(mixed, mixes_before(f + 3 + i) + 1)
                    nc.scalar.activation(k_rows[:, 4 * i:4 * i + 4, :], bank(f + 3 + i)[:, 0:4 * DK].rearrange("p (c k) -> p c k", k=DK),
                                         ACT.Copy).then_inc(by_act, 1)
                if more:
                    factor(h + 1, 2)
                    copy(h + 1, 1)
                if h + 2 < GLA_HEADS:
                    high(h + 3)
                if h:
                    act.wait_ge(rstd_ready, 2 * h)
                for p in range(PAIRS):
                    act.wait_ge(mixed, mixes_before(f + 9 + p // 2) + 1)
                    if h or p >= 2:
                        act.wait_ge(squared, PAIRS * h + p - 1)
                    nc.scalar.activation(squares[:, p % 2, :], bank(f + 9 + p // 2)[:, (p % 2) * DV:(p % 2 + 1) * DV], ACT.Square,
                                         accum_out=sums[:, p:p + 1]).then_inc(squared, 1)
                if more:
                    factor(h + 1, 3)

        @block.vector
        def _(dve):
            links = [0]

            def chain(ins):
                ins.then_inc(link, 1)
                links[0] += 1
                dve.wait_ge(link, links[0])

            def low(s):
                dve.wait_ge(w_high, s + 1)
                n = P if s == 0 else QK
                nc.vector.tensor_tensor(w_lo[:, :, 0:n], raw_of(s), w_hi[:, :, 0:n].bitcast(F32), ALU.subtract).then_inc(w_split, 1)

            def sums_of(h):
                dve.wait_ge(softened, h + 1)
                chain(nc.vector.scalar_tensor_tensor(soft[:, :], z[:, :], 0.0, soft[:, :], ALU.min, ALU.subtract))
                chain(nc.vector.tensor_tensor_scan(cum[:, :], keep[:, :], soft[:, :], 0.0, ALU.mult, ALU.add))
                c = cum[:, :].rearrange("p (c i) -> p c i", i=CHUNK)
                mid, last = (c[:, :, i:i + 1].broadcast_to([DK, CH, CHUNK]) for i in (CHUNK // 2 - 1, CHUNK - 1))
                nc.vector.tensor_tensor(from_mid[:, :].rearrange("p (c i) -> p c i", i=CHUNK), c, mid, ALU.subtract)
                nc.vector.tensor_tensor(to_last[:, :].rearrange("p (c i) -> p c i", i=CHUNK), last, c, ALU.subtract).then_inc(shifted, 1)

            def product(h, i):
                x, src = ((q_mid, q_sb), (k_mid, k_sb), (k_out, k_sb), (q_in, q_sb))[i]
                x = x[:, :].rearrange("p (c n) -> p c n", n=P)
                dve.wait_ge(expd, 4 * h + i + 1)
                if i == 3:
                    chain(nc.vector.tensor_copy(chunk_decay[:, :], q_in[:, :].rearrange("p (c i) -> p c i", i=CHUNK)[:, :, CHUNK - 1]))
                    cd = chunk_decay[:, :].rearrange("p (c two) -> p c two", two=2)
                    nc.vector.tensor_tensor(decay[:, :], cd[:, :, 0], cd[:, :, 1], ALU.mult)
                if src is q_sb:
                    dve.wait_ge(copied, 2 * h + 1)
                    nc.vector.scalar_tensor_tensor(x, src, float(DK) ** -0.5, x, ALU.mult, ALU.mult).then_inc(timed, 1)
                else:
                    dve.wait_ge(copied, 2 * h + 2)
                    nc.vector.tensor_tensor(x, src, x, ALU.mult).then_inc(timed, 1)

            def cross_pair(h):
                qi = q_in[:, :].rearrange("p (c two i) -> p c two i", two=2, i=CHUNK)
                ko = k_out[:, :].rearrange("p (c two i) -> p c two i", two=2, i=CHUNK)
                cd = chunk_decay[:, :].rearrange("p (c two) -> p c two", two=2)
                f = first_of[h]
                dve.wait_ge(mixed, mixes_before(f + 2) + 1)
                dve.wait_ge(timed, 4 * h + 4)
                nc.vector.tensor_tensor(qi[:, :, 1, :], qi[:, :, 1, :], cd[:, :, 0:1].broadcast_to([DK, PAIRS, CHUNK]), ALU.mult)
                nc.vector.tensor_tensor(ko[:, :, 0, :], ko[:, :, 0, :], cd[:, :, 1:2].broadcast_to([DK, PAIRS, CHUNK]), ALU.mult).then_inc(factored, 1)
                dve.wait_ge(*freed(f + 1))
                nc.vector.tensor_copy(att[0:CHUNK, :, CHUNK:P], bank(f + 2)[0:CHUNK, :].rearrange("p (c i) -> p c i", i=CHUNK)).then_inc(by_dve, 1)

            def states(h):
                f = first_of[h]
                for p in range(PAIRS - 1):
                    delta = bank(f + 5 + p // 2)[0:DK, (p % 2) * DV:(p % 2 + 1) * DV]
                    dve.wait_ge(mixed, mixes_before(f + 5 + p // 2) + 1)
                    if p == 0:
                        ins = nc.vector.tensor_copy(state[:, 1, :], delta)
                    else:
                        ins = nc.vector.scalar_tensor_tensor(state[:, p + 1, :], state[:, p, :], decay[:, p:p + 1], delta, ALU.mult, ALU.add)
                    ins.then_inc(state_ready, 1)
                    dve.wait_ge(state_ready, (PAIRS - 1) * h + p + 1)

            def outputs(h):
                f = first_of[h]
                for p in range(PAIRS):
                    if p % (PAIRS // 2) == 0:
                        dve.wait_ge(rstd_ready, 2 * h + 1 + p // (PAIRS // 2))
                    y = Y[:, p, h * DV:(h + 1) * DV]
                    ins = nc.vector.scalar_tensor_tensor(y, bank(f + 9 + p // 2)[:, (p % 2) * DV:(p % 2 + 1) * DV], rstd[:, p:p + 1], y,
                                                         ALU.mult, ALU.mult)
                    if p % 2:
                        ins.then_inc(by_dve, 1)

            dve.wait_ge(kept, 2)
            low(0)
            low(1)
            sums_of(0)
            for i in range(4):
                product(0, i)
            low(2)
            for h in range(GLA_HEADS):
                more = h + 1 < GLA_HEADS
                if more:
                    sums_of(h + 1)
                cross_pair(h)
                if more:
                    product(h + 1, 0)
                states(h)
                if more:
                    product(h + 1, 1)
                    product(h + 1, 2)
                if h + 2 < GLA_HEADS:
                    low(h + 3)
                outputs(h)
                if more:
                    product(h + 1, 3)

        @block.tensor
        def _(pe):
            def ring_wait(i):
                if i >= 4:
                    pe.wait_ge(*freed(i - 4))

            def project(s, part, ds=range(DC)):
                pe.wait_ge(w_split, s + 1)
                if s == 1 and part == 0:
                    pe.wait_ge(rank_ready, 2)
                if s >= 2:
                    pe.wait_ge(copied, 2 * (s - 2) + part + 1)
                m = P if s == 0 else DK
                for d in ds:
                    for w, h, first, final in ((w_hi, hT_hi, d == 0, False), (w_hi, hT_lo, False, False), (w_lo, hT_hi, False, d == DC - 1)):
                        for half in range(2):
                            mm = nc.tensor.matmul(psum[0:m, 2 * part + half, :], w[:, d, part * DK:part * DK + m],
                                                  h[:, d, half * HALF:(half + 1) * HALF], start=first, stop=final)
                if ds[-1] == DC - 1:
                    mm.then_inc(projected, 1)

            def gate(h):
                for half in range(2):
                    i = z_of[h] + half
                    ring_wait(i)
                    nc.tensor.matmul(bank(i)[0:DK, :], gate2[:, h * DK:(h + 1) * DK], rank[:, half * HALF:(half + 1) * HALF],
                                     start=True, stop=True).then_inc(z_ready, 1)

            def token_products(h):
                f = first_of[h]
                pe.wait_ge(timed, 4 * h + 2)
                for i in range(2):
                    ring_wait(f + i)
                    for c in range(4):
                        tok = slice((4 * i + c) * P, (4 * i + c + 1) * P)
                        mm = nc.tensor.matmul(bank(f + i)[:, c * P:(c + 1) * P], k_mid[:, tok], q_mid[:, tok], start=True, stop=True)
                    mm.then_inc(mixed, 1)
                ring_wait(f + 2)
                pe.wait_ge(timed, 4 * h + 4)
                for p in range(PAIRS):
                    mm = nc.tensor.matmul(bank(f + 2)[0:CHUNK, p * CHUNK:(p + 1) * CHUNK], k_out[:, p * P:p * P + CHUNK],
                                          q_in[:, p * P + CHUNK:(p + 1) * P], start=True, stop=True)
                mm.then_inc(mixed, 1)

            def state_changes(h):
                f = first_of[h]
                pe.wait_ge(factored, h + 1)
                for i in range(2):
                    ring_wait(f + 3 + i)
                    for c in range(4):
                        p = 4 * i + c
                        mm = nc.tensor.transpose(bank(f + 3 + i)[:, c * DK:(c + 1) * DK], k_out[:, p * P:(p + 1) * P], ident[0:DK, 0:DK])
                    mm.then_inc(mixed, 1)
                for p in range(PAIRS - 1):
                    i = f + 5 + p // 2
                    if p % 2 == 0:
                        ring_wait(i)
                    pe.wait_ge(by_act, freed(f + 3 + p // 4)[1])
                    mm = nc.tensor.matmul(bank(i)[0:DK, (p % 2) * DV:(p % 2 + 1) * DV], k_rows[:, p, :],
                                          V[:, p, h * DV:(h + 1) * DV], start=True, stop=True)
                    if p % 2 or p == PAIRS - 2:
                        mm.then_inc(mixed, 1)

            def outputs(h):
                f = first_of[h]
                pe.wait_ge(masked, h + 1)
                for p in range(PAIRS):
                    i = f + 9 + p // 2
                    if p % 2 == 0:
                        ring_wait(i)
                    out = bank(i)[:, (p % 2) * DV:(p % 2 + 1) * DV]
                    mm = nc.tensor.matmul(out, att[:, p, :], V[:, p, h * DV:(h + 1) * DV], start=True, stop=p == 0)
                    if p:
                        pe.wait_ge(state_ready, (PAIRS - 1) * h + p)
                        mm = nc.tensor.matmul(out, q_in[:, p * P:(p + 1) * P], state[:, p, :], start=False, stop=True)
                    if p % 2:
                        mm.then_inc(mixed, 1)

            FIRST = 2
            project(0, 0)
            pe.wait_ge(rank_ready, 2)
            gate(0)
            project(1, 0)
            project(1, 1)
            for h in range(GLA_HEADS):
                more = h + 1 < GLA_HEADS
                if more:
                    gate(h + 1)
                token_products(h)
                if more:
                    project(h + 2, 0, range(FIRST, DC) if h else range(DC))
                state_changes(h)
                if more:
                    project(h + 2, 1)
                outputs(h)
                if h + 2 < GLA_HEADS:
                    project(h + 3, 0, range(FIRST))


class Merge:

    def __init__(self, nc, ctx, ph, stage, Y):
        def sb(name, shape):
            return ctx.enter_context(nc.sbuf_tensor(f"{ph}_{name}", shape, F32))

        def sem(name):
            return phase_semaphore(nc, ctx, f"{ph}_{name}")

        self.nc, self.stage, self.Y, self.G = nc, stage, Y, len(stage.outs)
        self.logs = sb("logs", [P, self.G, TT, DIL_HEADS])
        self.top, self.inv = sb("top", [P, TT, DIL_HEADS]), sb("inv", [P, TT, DIL_HEADS])
        self.outs = [sb(f"outs{i}", [P, self.G, D_DIL]) for i in range(2)]
        self.logs_loaded, self.link, self.expd = sem("logs_loaded"), sem("link"), sem("expd")
        self.loaded = [sem(f"group_outs_loaded{i}") for i in range(2)]
        self.added = sem("added")
        self.links = 0

    def load_logs(self, sp):
        for g in range(self.G):
            sp.dma_start(self.logs[:, g, :, :], self.stage.lses[g].rearrange("(t p) h -> p t h", p=P)).then_inc(self.logs_loaded, 16)

    def load(self, sp, t):
        if t >= 2:
            sp.wait_ge(self.added, t - 1)
        for g in range(self.G):
            sp.dma_start(self.outs[t % 2][:, g, :], self.stage.outs[g][t * P:(t + 1) * P, :]).then_inc(self.loaded[t % 2], 16)

    def act_exp(self, act):
        act.wait_ge(self.link, 3)
        self.nc.scalar.activation(self.logs[:, :, :, :], self.logs[:, :, :, :], ACT.Exp).then_inc(self.expd, 1)

    def chain(self, dve, ins):
        ins.then_inc(self.link, 1)
        self.links += 1
        dve.wait_ge(self.link, self.links)

    def dve_weights(self, dve):
        nc, logs, top, inv = self.nc, self.logs, self.top[:, :, :], self.inv[:, :, :]
        dve.wait_ge(self.logs_loaded, 16 * self.G)
        self.chain(dve, nc.vector.tensor_tensor(top, logs[:, 0, :, :], logs[:, 1, :, :], ALU.max))
        self.chain(dve, nc.vector.tensor_tensor(top, top, logs[:, 2, :, :], ALU.max))
        for g in range(self.G):
            ins = nc.vector.tensor_tensor(logs[:, g, :, :], logs[:, g, :, :], top, ALU.subtract)
        self.chain(dve, ins)
        dve.wait_ge(self.expd, 1)
        self.chain(dve, nc.vector.tensor_tensor(inv, logs[:, 0, :, :], logs[:, 1, :, :], ALU.add))
        self.chain(dve, nc.vector.tensor_tensor(inv, inv, logs[:, 2, :, :], ALU.add))
        self.chain(dve, nc.vector.reciprocal(inv, inv))
        for g in range(self.G):
            ins = nc.vector.tensor_tensor(logs[:, g, :, :], logs[:, g, :, :], inv, ALU.mult)
        self.chain(dve, ins)

    def dve_add(self, dve, t):
        nc, Y = self.nc, self.Y
        dve.wait_ge(self.loaded[t % 2], 16 * self.G * (t // 2 + 1))
        for g in range(self.G):
            for h in range(DIL_HEADS):
                cols = slice(h * DIL_DIM, (h + 1) * DIL_DIM)
                w, o = self.logs[:, g, t, h:h + 1], self.outs[t % 2][:, g, cols]
                if g == 0:
                    ins = nc.vector.tensor_scalar(Y[:, t, cols], o, w, None, ALU.mult)
                else:
                    ins = nc.vector.scalar_tensor_tensor(Y[:, t, cols], o, w, Y[:, t, cols], ALU.mult, ALU.add)
            if g + 1 < self.G:
                self.chain(dve, ins)
        ins.then_inc(self.added, 1)


class Rope:

    def __init__(self, nc, ctx, positions, inv_freq, room, cos_d, sin_d, last_load):
        HD = DIL_DIM // 2

        def sb(name, shape, dt=F32):
            return ctx.enter_context(nc.sbuf_tensor(f"rope_{name}", shape, dt))

        def sem(name):
            return phase_semaphore(nc, ctx, f"rope_{name}")

        self.nc, self.positions, self.inv_freq, self.drams, self.last_load = nc, positions, inv_freq, (sin_d, cos_d), last_load
        self.pos_i, self.pos = sb("pos_i", [P, TT], mybir.dt.int32), sb("pos", [P, TT])
        self.freq = sb("freq", [P, HD])
        self.turns, self.angle, *self.tables = [room[:, :, i * HD:(i + 1) * HD] for i in range(4)]
        self.loaded, self.link, self.reduced = sem("loaded"), sem("link"), sem("reduced")
        self.sined, self.stored = sem("sined"), sem("stored")

    def load(self, sp, s):
        if s == 2:
            sp.dma_start(self.pos_i[:, :], self.positions[0, :].rearrange("(t p) -> p t", p=P),
                         allow_slow_non_contiguous=True).then_inc(self.loaded, 16)
            sp.dma_start(self.freq[:, :], self.inv_freq.partition_broadcast(P)).then_inc(self.loaded, 16)

    def store(self, sp):
        for i, dram in enumerate(self.drams):
            sp.wait_ge(self.sined, i + 1)
            sp.dma_start(dram.rearrange("p (t k) -> p t k", t=TT), self.tables[i]).then_inc(self.stored, 16)
        sp.wait_ge(self.stored, 16 * 2)
        sp.dma_start(*self.last_load).then_inc(self.stored, 16)
        sp.wait_ge(self.stored, 16 * 3)

    def act(self, act, k):
        if k != 1:
            return
        for i, out in enumerate(self.tables):
            act.wait_ge(self.reduced, i + 1)
            self.nc.scalar.activation(out[:, :, :], out[:, :, :], ACT.Sin).then_inc(self.sined, 1)

    def dve(self, dve, k):
        if k != 0:
            return
        nc, angle, turns, pos = self.nc, self.angle, self.turns, self.pos
        links = [0]

        def chain(ins):
            ins.then_inc(self.link, 1)
            links[0] += 1
            dve.wait_ge(self.link, links[0])

        two_pi = 2 * math.pi
        parts, left = [], two_pi
        for bits in (5, 13, 21):
            parts.append(math.floor(left * 2 ** bits) / 2 ** bits)
            left -= parts[-1]
        parts.append(left)
        ROUND = 1.5 * 2 ** 23
        dve.wait_ge(self.loaded, 32)
        chain(nc.vector.tensor_copy(pos[:, :], self.pos_i[:, :]))
        for shift, out in zip((0.0, math.pi / 2), self.tables):
            for t in range(TT):
                ins = nc.vector.tensor_scalar(angle[:, t, :], self.freq[:, :], pos[:, t:t + 1], None, ALU.mult)
            chain(ins)
            chain(nc.vector.tensor_scalar(turns[:, :, :], angle[:, :, :], 1 / two_pi, shift / two_pi, ALU.mult, ALU.add))
            chain(nc.vector.tensor_scalar(turns[:, :, :], turns[:, :, :], ROUND, ROUND, ALU.add, ALU.subtract))
            for part in parts:
                chain(nc.vector.scalar_tensor_tensor(angle[:, :, :], turns[:, :, :], -part, angle[:, :, :], ALU.mult, ALU.add))
            chain(nc.vector.tensor_scalar(angle[:, :, :], angle[:, :, :], shift, 3.1415925, ALU.add, ALU.min))
            ins = nc.vector.tensor_scalar(out[:, :, :], angle[:, :, :], -3.1415925, None, ALU.max)
            ins.then_inc(self.reduced, 1)
            dve.wait_ge(self.reduced, 1 if out is self.tables[0] else 2)


class Constants:

    def __init__(self, nc, ctx, ident, neg_half, band, split, zeros, keys0):
        self.nc, self.ident, self.neg_half, self.band, self.mask, self.zeros, self.keys0 = nc, ident, neg_half, band, split, zeros, keys0
        self.done = phase_semaphore(nc, ctx, "constant_done")
        self.parity = phase_semaphore(nc, ctx, "constant_parity")
        self.apart = ctx.enter_context(nc.sbuf_tensor("apart", [P, P], mybir.dt.int32))
        self.steps = 0

    def step(self, pool, ins):
        ins.then_inc(self.done, 1)
        self.steps += 1
        pool.wait_ge(self.done, self.steps)

    def select(self, pool, x, op, fill, base, pattern, channel):
        self.step(pool, self.nc.gpsimd.affine_select(out=x, in_=x, compare_op=op, fill=fill, base=base, pattern=pattern,
                                                     channel_multiplier=channel))

    def first(self, pool):
        memset = self.nc.gpsimd.memset
        self.step(pool, memset(self.ident[:, :], 0.0))
        self.select(pool, self.ident[:, :], ALU.not_equal, 1.0, 0, [[-1, P]], 1)
        self.step(pool, memset(self.neg_half[:, :], -0.5))
        for k in self.keys0:
            self.step(pool, memset(k, 0.0))

    def masks(self, pool):
        memset, band, apart = self.nc.gpsimd.memset, self.band[:, :], self.apart[:, :]
        self.step(pool, memset(self.zeros[:, :], 0.0))
        self.step(pool, memset(band, 0.0))
        self.select(pool, band, ALU.is_ge, NEG, 0, [[1, 2 * P]], -1)
        self.select(pool, band, ALU.is_ge, NEG, P, [[-1, 2 * P]], 1)
        self.step(pool, self.nc.gpsimd.iota(apart, pattern=[[-1, P]], base=2 * P, channel_multiplier=1))
        self.apart_step = self.steps

    def last(self, pool):
        mask = self.mask[:, :]
        pool.wait_ge(self.parity, 2)
        self.select(pool, mask, ALU.is_ge, NEG, 0, [[-1, P]], 1)

    def dve(self, dve):
        dve.wait_ge(self.done, self.apart_step)
        self.nc.vector.tensor_scalar(self.apart[:, :], self.apart[:, :], 1, None, ALU.bitwise_and).then_inc(self.parity, 1)
        dve.wait_ge(self.parity, 1)
        self.nc.vector.tensor_scalar(self.mask[:, :], self.apart[:, :], NEG, None, ALU.mult).then_inc(self.parity, 1)


def start_phase(nc, psum, ident, neg_half, band, split, zeros, keys0, broadcasts, mem, x, X, scratch, mem_norm, mix_norm,
                mem_hi, mem_lo, hT_hi, hT_lo, slots, next_w):
    with ExitStack() as ctx:
        ctx.callback(nc.all_engine_barrier)
        gains = [ctx.enter_context(nc.sbuf_tensor(f"{n}_gain", [P, DC], F32)) for n in ("mem", "x")]
        tiles = N_MEM // P + TT
        loaded = [phase_semaphore(nc, ctx, f"rows_loaded{i}") for i in range(tiles)]
        gains_loaded = phase_semaphore(nc, ctx, "start_gains_loaded")
        broadcast = phase_semaphore(nc, ctx, "start_broadcast")
        flat = scratch.rearrange("p t n -> p (t n)")
        room = [flat[:, i * D:(i + 1) * D] for i in range(6)]
        rows = room[0:2] + [X[:, t, :] for t in range(TT)]
        constants = Constants(nc, ctx, ident, neg_half, band, split, zeros, keys0)
        norm = Norm(nc, ctx, "start", psum, (0, 2), ident, neg_half,
                    norm_plan(mem_hi, mem_lo, gains[0], N_MEM // P) + norm_plan(hT_hi, hT_lo, gains[1]),
                    room[2:4], [r.rearrange("p (d n) -> p d n", d=DC) for r in room[4:6]])
        SPLIT_AT = 5
        block = ctx.enter_context(nc.Block())

        @block.sync
        def _(sp):
            for n in range(tiles):
                src, t = (mem, n) if n < 2 else (x, n - 2)
                sp.dma_start(rows[n], src[t * P:(t + 1) * P, :]).then_inc(loaded[n], 16)
                if n == SPLIT_AT - 1:
                    for s in range(2):
                        slots.load(sp, s, next_w)
            for out, row in broadcasts:
                sp.dma_start(out, row.partition_broadcast(P)).then_inc(broadcast, 16)
            sp.wait_ge(broadcast, 16 * len(broadcasts))

        @block.scalar
        def _(act):
            for out, row in zip(gains, (mem_norm, mix_norm)):
                act.dma_start(out[:, :], row.rearrange("(d p) -> p d", p=P), allow_slow_non_contiguous=True).then_inc(gains_loaded, 16)
            for t in range(tiles):
                act.wait_ge(loaded[t], 16)
                norm.act_square(act, t, rows[t])
                if t >= 2:
                    norm.act_high(act, t - 2)
                norm.act_scale(act, t, rows[t])
                if t == SPLIT_AT:
                    for s in range(2):
                        slots.high_part(act, s, next_w)
            norm.act_high(act, tiles - 2)
            norm.act_high(act, tiles - 1)

        @block.gpsimd
        def _(pool):
            constants.first(pool)
            for t in range(tiles):
                norm.pool(pool, t)
                if t == 3:
                    constants.masks(pool)
            constants.last(pool)

        @block.tensor
        def _(pe):
            pe.wait_ge(constants.done, 2)
            for t in range(tiles):
                norm.pe(pe, t)

        @block.vector
        def _(dve):
            dve.wait_ge(gains_loaded, 32)
            for t in range(tiles):
                if t >= 2:
                    norm.dve_low(dve, t - 2)
                norm.dve_gain(dve, t)
                if t == 6:
                    constants.dve(dve)
                if t == SPLIT_AT:
                    for s in range(2):
                        slots.low_part(dve, s, next_w)
            norm.dve_low(dve, tiles - 2)
            norm.dve_low(dve, tiles - 1)

        slots.ahead = 2


class Stage:

    def __init__(self, nc, ctx, outs, lses):
        self.outs, self.lses = outs, lses
        self.tile = [ctx.enter_context(nc.sbuf_tensor(f"stage{i}", [P, D_DIL], F32)) for i in range(2)]
        self.lse_tiles = [ctx.enter_context(nc.sbuf_tensor(f"stage_lse{g}", [P, TT * DIL_HEADS], F32)) for g in range(len(outs))]
        self.stored = [phase_semaphore(nc, ctx, f"stage_stored{i}") for i in range(2)]
        self.lse_stored = phase_semaphore(nc, ctx, "stage_lse_stored")
        self.groups = 0

    @property
    def lse(self):
        return self.lse_tiles[self.groups]

    def before(self, t):
        return 16 * (self.groups * TT // 2 + t // 2)

    def rows(self, dram, t):
        r = min(DILATIONS[self.groups], SEQ // P)
        per = SEQ // r // P
        return dram.rearrange("(a r) c -> r a c", r=r)[t // per, (t % per) * P:(t % per + 1) * P, :]

    def store(self, sp, t):
        sp.dma_start(self.rows(self.outs[self.groups], t), self.tile[t % 2][:, :]).then_inc(self.stored[t % 2], 16)

    def store_lse(self, sp):
        r = min(DILATIONS[self.groups], SEQ // P)
        q = TT // r
        lse = self.lse[:, :].rearrange("p (r q h) -> p r q h", r=r, q=q)
        rows = self.lses[self.groups].rearrange("(q p r) h -> p r q h", p=P, r=r)
        for i in range(q):
            sp.dma_start(rows[:, :, i, :], lse[:, :, i, :]).then_inc(self.lse_stored, 16)

    def wait_logs(self, eng):
        eng.wait_ge(self.lse_stored, 16 * sum(TT // min(r, SEQ // P) for r in DILATIONS))

    def wait_outputs(self, eng):
        for sem in self.stored:
            eng.wait_ge(sem, self.before(0))


def build(nc, a, out):
    with ExitStack() as ctx:
        def sb(name, shape, dt=F32, c=ctx, side="left"):
            return c.enter_context(nc.sbuf_tensor(name, shape, dt, side=side))

        psum = ctx.enter_context(nc.psum_tensor("psum", [P, BANKS, HALF], F32))
        ident, neg_half = sb("ident", [P, P]), sb("neg_half", [P, TT])
        band, split, zeros = sb("band", [P, 2 * P]), sb("split", [P, P]), sb("zeros", [P, 2 * P])
        xa_gain = [[sb(f"xa_{n}_gain{i}", [P, XA_DIM]) for n in "qk"] for i in range(2)]
        o_gain = sb("o_gain", [P, GLA_DV])
        dil_gain = [sb("dil_q_gain", [P, DIL_DIM]), sb("dil_k_gain", [P, DIL_DIM])]
        hT_hi, hT_lo = sb("hT_hi", [P, DC, SEQ], F32R), sb("hT_lo", [P, DC, SEQ], F32R)
        XY = sb("XY", [P, TT, D])
        raws = RawPair(nc, ctx)

        def dram(name, shape):
            return nc.dram_tensor(name, shape, F32, kind="Internal").ap()

        x2 = dram("x_layer1", [SEQ, D])
        keys_d = [dram(f"mem_keys{i}", [P, XA_HEADS * N_MEM]) for i in range(2)]
        vals_d = [dram(f"mem_values{i}", [P, 2 * D_XA]) for i in range(2)]
        rope_d = [dram(f"rope_table_{n}", [P, TT * DIL_DIM // 2]) for n in ("cos", "sin")]
        outs_d = [dram(f"group_out{g}", [SEQ, D_DIL]) for g in range(3)]
        lses_d = [dram(f"group_lse{g}", [SEQ, DIL_HEADS]) for g in range(3)]

        def plain(x, d, t):
            return x[:, d, t * P:(t + 1) * P]

        def xa_dest(xqT):
            def dest(t, src):
                return [(xqT[:, :, t * P:(t + 1) * P], src.rearrange("p (a n) -> p a n", n=P))]
            return dest

        def xa_units(q_of, keys, vals, base):
            return [(q_of(h, t), keys[:, h, :], N_MEM, zeros[:, :],
                     [vals[:, c, h * XA_DIM:(h + 1) * XA_DIM] for c in range(2)],
                     XY[:, t, base + h * XA_DIM:base + (h + 1) * XA_DIM], float(XA_DIM) ** -0.5) for t in range(TT) for h in range(XA_HEADS)]

        def xa_keys(i, c):
            return sb(f"xa_keys{i}", [P, XA_HEADS, N_MEM], F32, c), sb(f"xa_values{i}", [P, 2, D_XA], F32, c)

        def xa_loads(i, keys, vals):
            return [(keys[:, :, :].rearrange("p h n -> p (h n)"), keys_d[i]), (vals[:, :, :].rearrange("p h n -> p (h n)"), vals_d[i])]

        def tokens(x, t, r):
            r = min(r, SEQ // P)
            v = x.rearrange("p (a r) -> p r a", r=r)
            per = SEQ // r // P
            return v[:, t // per, (t % per) * P:(t % per + 1) * P]

        def keys_of(x, t, r):
            per = max(1, SEQ // r // P)
            if r == 16 or t % per == 0:
                return tokens(x, t, r), P, t
            v = x.rearrange("p (a r) -> p r a", r=r)
            b = t % per
            return v[:, t // per, (b - 1) * P:(b + 1) * P], 2 * P, t - 1

        c0 = ctx.enter_context(ExitStack())
        with ExitStack() as c:
            xqT = sb("xqT0", [P, 2, SEQ], F32, c)
            kv_size = XA_HEADS * N_MEM
            with ExitStack() as c2:
                V = sb("gla_v", [P, TT, D_MIX], F32, c2, "right")
                w = a["a_w_in"]
                v0 = 2 * GLA_HEADS * GLA_DK
                g0 = v0 + D_MIX + GLA_RANK
                B = 2 * GLA_DV
                whole = dict(tiles=TT, stat=(hT_hi, hT_lo))
                blocks = [dict(whole, kind="copy", w=w[:, v0 + i * B:v0 + (i + 1) * B], pick=plain,
                               dest=lambda t, i=i: V[:, t, i * B:(i + 1) * B]) for i in range(2)]
                blocks += [dict(whole, kind="gate", w=w[:, g0 + i * B:g0 + (i + 1) * B], pick=plain, gain=o_gain[:, :],
                                dest=lambda t, i=i: XY[:, t, i * B:(i + 1) * B]) for i in range(2)]
                blocks += [dict(whole, kind="heads", dim=XA_DIM, gain=xa_gain[0][0][:, :], w=w[:, g0 + D_MIX:g0 + D_MIX + D_XA],
                                pick=plain, dest=xa_dest(xqT))]
                with ExitStack() as c3:
                    slots = WeightSlots(nc, c3, "w0", B)
                    keys = [raws.tiles[1][:, :].rearrange("p (h n) -> p h n", h=XA_HEADS), sb("keys1", [P, XA_HEADS, N_MEM], F32, c3)]
                    vals = [raws.tiles[0][:, i * D // 2:(i + 1) * D // 2].rearrange("p (c n) -> p c n", c=2) for i in range(2)]
                    mem_parts = sb("mem_hi", [P, DC, N_MEM], F32R, c3), sb("mem_lo", [P, DC, N_MEM], F32R, c3)
                    start_phase(nc, psum, ident, neg_half, band, split, zeros, [k[:, :, :] for k in keys],
                                [(xa_gain[i][j][:, :], a[f"xa_{n}_norm"][i, :]) for i in range(2) for j, n in enumerate("qk")]
                                + [(o_gain[:, :], a["a_o_norm"]), (dil_gain[0][:, :], a["b_q_norm"]), (dil_gain[1][:, :], a["b_k_norm"])],
                                a["mem"][0, :, :], a["x"][0, :, :], XY, V[:, :, :], a["mem_norm"], a["mix_norm"][0, :],
                                *mem_parts, hT_hi, hT_lo, slots, blocks[0]["w"])

                    def key_dest(i):
                        def dest(t, src):
                            s = src.rearrange("p (a n) -> p a n", n=P)
                            tok = slice(t * P, (t + 1) * P)
                            return [(keys[i][0:64, 0:XA_HEADS:2, tok], s[0:64, :, :]), (keys[i][64:P, 1:XA_HEADS:2, tok], s[64:P, :, :])]
                        return dest

                    kv_blocks = []
                    for i in range(2):
                        wkv = a["xa_w_kv"][i, :, :]
                        kv = dict(tiles=N_MEM // P, stat=mem_parts, pick=plain)
                        kv_blocks += [dict(kind="heads", dim=XA_DIM, gain=xa_gain[i][1][:, :], w=wkv[:, 0:D_XA], dest=key_dest(i), **kv),
                                      dict(kind="copy", w=wkv[:, D_XA:2 * D_XA], dest=lambda t, i=i: vals[i][:, t, :], **kv)]
                    blocks[2:2] = kv_blocks
                    with ExitStack() as c4:
                        c4.callback(nc.all_engine_barrier)
                        saves = [(keys_d[i], keys[i][:, :, :].rearrange("p h n -> p (h n)")) for i in range(2)]
                        saves += [(vals_d[i], vals[i][:, :, :].rearrange("p h n -> p (h n)")) for i in range(2)]
                        rank_w = w[:, v0 + D_MIX:v0 + D_MIX + P].rearrange("(d p) n -> p d n", p=P)
                        rope = Rope(nc, c4, a["positions"], a["inv_freq"], XY[:, :, D_MIX:], *rope_d,
                                    last_load=(XY[:, :, D_MIX:D_MIX + P], rank_w))
                        project_phase(nc, "p0", psum, ident, neg_half, blocks, slots, guest=rope, saves=(5, saves))
                kv_room = sb("kv_room", [P, kv_size + 2 * D_XA], F32, c)
                keys = kv_room[:, 0:kv_size].rearrange("p (h n) -> p h n", h=XA_HEADS)
                vals = kv_room[:, kv_size:].rearrange("p (c n) -> p c n", c=2)
                gla_phase(nc, "gla", psum, ident, neg_half, hT_hi, hT_lo, w, a["a_w_gate2"], a["a_b_gate"], V, XY, raws.tiles,
                          kv_room, [(kv_room[:, 0:kv_size], keys_d[0]), (kv_room[:, kv_size:], vals_d[0])])
            weights = OutWeights(nc, c0, "o0", DC, a["a_w_out"], raws, 5)
            attention_phase(nc, "xa0", psum, ident, xa_units(lambda h, t: xqT[:, h // 2, t * P:(t + 1) * P], keys, vals, D_MIX),
                            ahead=weights)
        out_phase(nc, "o0", psum, ident, neg_half, XY, weights, a["x"][0, :, :], a["ffn_norm"][0, :], hT_hi, hT_lo, a["ffn_w_up"][0, :, :])
        c0.close()
        w, cols = a["b_w_in"], 3 * D_DIL
        xq_w = w[:, 3 * cols:3 * cols + D_XA]
        ffn_phase(nc, "f0", psum, ident, neg_half, XY, hT_hi, hT_lo, a["ffn_w_up"][0, :, :], a["ffn_conv_w"][0, :, :], a["ffn_conv_b"][0, :],
                  a["ffn_w_down"][0, :, :], x2, raws, a["mix_norm"][1, :], [half_rows(xq_w, kh) for kh in range(2)])

        stage = Stage(nc, ctx, outs_d, lses_d)
        c1 = ctx.enter_context(ExitStack())
        with ExitStack() as c:
            cos, sin = sb("cos", [P, TT, DIL_DIM // 2], F32, c), sb("sin", [P, TT, DIL_DIM // 2], F32, c)
            rope_loads = [(x[:, :, :].rearrange("p t k -> p (t k)"), d) for x, d in zip((cos, sin), rope_d)]
            qT, kT = (sb(f"dil_{n}T", [P, DIL_HEADS, SEQ], F32, c) for n in "qk")
            V = XY[:, :, 0:D_DIL]
            XQ = XY[:, :, D_DIL + D_XA:]
            slots_ctx = c.enter_context(ExitStack())
            slots_ctx.callback(nc.all_engine_barrier)
            slots = WeightSlots(nc, slots_ctx, "w", HALF, raws)

            def head_dest(x):
                return lambda t, src: [(x[:, :, t * P:(t + 1) * P], src.rearrange("p (h n) -> p h n", n=P))]

            def group_blocks(g):
                off, r = g * D_DIL, DILATIONS[g]
                blocks = [dict(whole, kind="heads", dim=DIL_DIM, gain=dil_gain[i][:, :], rope=(cos, sin), w=w[:, i * cols + off:i * cols + off + D_DIL],
                               pick=plain, dest=head_dest(x)) for i, x in enumerate((qT, kT))]
                return blocks + [dict(whole, kind="copy", w=w[:, 2 * cols + off:2 * cols + off + D_DIL],
                                      pick=lambda x, d, t: tokens(x[:, d, :], t, r), dest=lambda t: V[:, t, :])]

            for g, r in enumerate(DILATIONS):
                blocks = group_blocks(g)
                if g == 0:
                    blocks.insert(0, dict(whole, kind="heads", dim=XA_DIM, gain=xa_gain[1][0][:, :], w=xq_w,
                                          pick=plain, dest=lambda t, src: [(XQ[:, t, :], src)]))
                project_phase(nc, f"p1_{g}", psum, ident, neg_half, blocks, slots, rope_loads if g == 0 else (),
                              room=raws.tiles)
                with ExitStack() as c2:
                    if g + 1 < len(DILATIONS):
                        ahead = SlotsAhead(slots, group_blocks(g + 1)[0]["w"])
                    else:
                        slots_ctx.close()
                        ahead = weights = OutWeights(nc, c1, "o1", (D_DIL + D_XA) // P, a["b_w_out"], raws, 3)
                    units = []
                    for t in range(TT):
                        for h in range(DIL_HEADS):
                            k, n, first = keys_of(kT[:, h, :], t, r)
                            mask = split[:, :] if r == 16 else band[:, 2 * P - n:2 * P]
                            units.append((tokens(qT[:, h, :], t, r), k, n, mask,
                                          [V[:, first + i, h * P:(h + 1) * P] for i in range(n // P)],
                                          stage.tile[t % 2][:, h * P:(h + 1) * P], float(DIL_DIM) ** -0.5))
                    loads = ()
                    if g == 0:
                        keys, vals = xa_keys(1, c2)
                        loads = xa_loads(1, keys, vals)
                        units += xa_units(lambda h, t: XQ[:, t, h // 2 * P:(h // 2 + 1) * P], keys, vals, D_DIL)
                    attention_phase(nc, f"da{g}", psum, ident, units, stage, loads, TT * DIL_HEADS,
                                    ahead=ahead, room=raws.tiles if g + 1 < len(DILATIONS) else ())
        out_phase(nc, "o1", psum, ident, neg_half, XY, weights, x2, a["ffn_norm"][1, :], hT_hi, hT_lo, a["ffn_w_up"][1, :, :], stage)
        c1.close()
        ffn_phase(nc, "f1", psum, ident, neg_half, XY, hT_hi, hT_lo, a["ffn_w_up"][1, :, :], a["ffn_conv_w"][1, :, :], a["ffn_conv_b"][1, :],
                  a["ffn_w_down"][1, :, :], out, raws)


_INS = ["x", "mem", "positions", "mem_norm", "mix_norm", "xa_w_kv", "xa_q_norm", "xa_k_norm", "ffn_norm", "ffn_w_up",
        "ffn_conv_w", "ffn_conv_b", "ffn_w_down", "a_w_in", "a_w_gate2", "a_b_gate", "a_o_norm", "a_w_out",
        "b_w_in", "b_q_norm", "b_k_norm", "b_w_out"]


def kernel(**inputs):
    import numpy as _np
    import concourse.bacc as _bacc
    from concourse import mybir as _mybir
    from concourse.bass_utils import run_bass_kernel_spmd as _run

    nc = _bacc.Bacc("TRN2", target_bir_lowering=False, num_devices=1)
    half = DIL_DIM // 2
    arrays, aps = {}, {}
    given = {name: _np.ascontiguousarray(inputs[name]) for name in _INS}
    given["inv_freq"] = _np.float32(10000.0) ** (-_np.arange(half, dtype=_np.float32) / _np.float32(half))
    for name, x in given.items():
        arrays[f"in_{name}_dram"] = x
        aps[name] = nc.dram_tensor(f"in_{name}_dram", x.shape, _mybir.dt.from_np(x.dtype), kind="ExternalInput").ap()
    out = nc.dram_tensor("out_0_dram", (1, SEQ, D), F32, kind="ExternalOutput").ap()
    build(nc, aps, out[0, :, :])
    r = _run(nc, [arrays], core_ids=[0])
    return r.results[0]["out_0_dram"]
```
